# Optimizing a Trainium2 kernel written in Bass

```python
import jax, jax.numpy as jnp
from jax import lax
import numpy as np

D_MODEL = 1024
BATCH = 1
SEQ = 512
DEPTH = 1

CHUNK = 64
MIX_W = D_MODEL
GLA_HEADS = 4
GLA_DV = MIX_W // 2 // GLA_HEADS
GLA_DK = GLA_DV // 2
GLA_QK_W = GLA_HEADS * GLA_DK
GLA_V_W = GLA_HEADS * GLA_DV
GLA_RANK = 16
GLA_GATE_NORM = 16.0
ATT_HEADS = 8
ATT_DH = (MIX_W - GLA_V_W) // ATT_HEADS
ATT_W = ATT_HEADS * ATT_DH
BAND_CHUNKS = 8
BAND = (BAND_CHUNKS + 1) * CHUNK
REL_CLIP = 128
PEER_HEADS = 8
N_KEYS = 128
N_EXPERTS = N_KEYS * N_KEYS
PEER_DK = 256
PEER_TOPK = 16
PEER_BLOCK = 128
PLE_DIM = 256
RMS_EPS = 1e-6
SPLIT_SIZES = (GLA_QK_W, GLA_QK_W, GLA_V_W, GLA_RANK, GLA_V_W, ATT_W, ATT_W, ATT_W)
SPLIT_POINTS = tuple(int(v) for v in np.cumsum(SPLIT_SIZES)[:-1])
IN_W = sum(SPLIT_SIZES)

kernel_name = 'hybrid_gla_bandattn_peer_ple'

def rms_norm(x, g):
    xf = x.astype(jnp.float32)
    y = xf * lax.rsqrt(jnp.mean(xf * xf, axis=-1, keepdims=True) + RMS_EPS)
    return (y * g.astype(jnp.float32)).astype(x.dtype)

def gla_group(q, k, v, g_lr, g_w2, g_b, head_norm, out_gate):
    b, s, _ = q.shape
    nc = s // CHUNK
    f32 = jnp.float32

    def heads(t, d):
        return t.astype(f32).reshape(b, nc, CHUNK, GLA_HEADS, d).transpose(0, 3, 1, 2, 4)

    q = heads(q, GLA_DK) * (GLA_DK ** -0.5)
    k = heads(k, GLA_DK)
    v = heads(v, GLA_DV)
    g = jax.nn.log_sigmoid((g_lr @ g_w2 + g_b).astype(f32)) / GLA_GATE_NORM
    g = heads(g, GLA_DK)
    cum = jnp.cumsum(g, axis=3)
    last = cum[:, :, :, -1:, :]
    mid = cum[:, :, :, CHUNK // 2:CHUNK // 2 + 1, :]
    a = jnp.einsum('bhnid,bhnjd->bhnij', q * jnp.exp(cum - mid), k * jnp.exp(mid - cum))
    causal = jnp.tril(jnp.ones((CHUNK, CHUNK), dtype=bool))
    o_intra = jnp.einsum('bhnij,bhnje->bhnie', jnp.where(causal, a, 0.0), v)
    k_state = k * jnp.exp(last - cum)
    decay = jnp.exp(last[:, :, :, 0, :])

    def step(state, inp):
        kc, vc, dc = inp
        new = dc[..., None] * state + jnp.einsum('bhcd,bhce->bhde', kc, vc)
        return new, state

    xs = (k_state.transpose(2, 0, 1, 3, 4), v.transpose(2, 0, 1, 3, 4), decay.transpose(2, 0, 1, 3))
    init = jnp.zeros((b, GLA_HEADS, GLA_DK, GLA_DV), f32)
    _, prev = lax.scan(step, init, xs)
    o_inter = jnp.einsum('bhnid,nbhde->bhnie', q * jnp.exp(cum), prev)
    o = o_intra + o_inter
    o = o * lax.rsqrt(jnp.mean(o * o, axis=-1, keepdims=True) + RMS_EPS) * head_norm.astype(f32)
    o = o.transpose(0, 2, 3, 1, 4).reshape(b, s, GLA_V_W)
    return (o * jax.nn.silu(out_gate.astype(f32))).astype(out_gate.dtype)

def band_attention(q, k, v, rel_table):
    b, s, _ = q.shape
    nc = s // CHUNK
    pad = BAND_CHUNKS * CHUNK
    f32 = jnp.float32

    def heads(t):
        return t.reshape(b, s, ATT_HEADS, ATT_DH).transpose(0, 2, 1, 3)

    q, k, v = heads(q), heads(k), heads(v)
    kp = jnp.pad(k, ((0, 0), (0, 0), (pad, 0), (0, 0)))
    vp = jnp.pad(v, ((0, 0), (0, 0), (pad, 0), (0, 0)))
    rel = jnp.arange(CHUNK)[:, None] + pad - jnp.arange(BAND)[None, :]
    bias = rel_table.astype(f32)[:, jnp.clip(rel, -REL_CLIP, REL_CLIP) + REL_CLIP]
    scale = ATT_DH ** -0.5
    key_off = jnp.arange(BAND)

    def one_chunk(c):
        start = c * CHUNK
        qc = lax.dynamic_slice_in_dim(q, start, CHUNK, axis=2)
        kc = lax.dynamic_slice_in_dim(kp, start, BAND, axis=2)
        vc = lax.dynamic_slice_in_dim(vp, start, BAND, axis=2)
        sc = jnp.einsum('bhqd,bhkd->bhqk', qc, kc).astype(f32) * scale + bias
        valid = (start - pad + key_off) >= 0
        sc = jnp.where(valid, sc, -1e30)
        pr = jax.nn.softmax(sc, axis=-1).astype(vc.dtype)
        return jnp.einsum('bhqk,bhkd->bhqd', pr, vc)

    out = lax.map(one_chunk, jnp.arange(nc))
    return out.transpose(1, 0, 3, 2, 4).reshape(b, s, ATT_W)

def peer_ffn(xn, w_q, subkeys, u_tab, v_tab):
    b, s, d = xn.shape
    xt = xn.reshape(b * s // PEER_BLOCK, PEER_BLOCK, d)

    def block(xb):
        qh = (xb @ w_q).reshape(PEER_BLOCK, PEER_HEADS, 2, PEER_DK // 2)
        sc = jnp.einsum('thpd,hpnd->thpn', qh, subkeys).astype(jnp.float32)
        s1, i1 = lax.top_k(sc[:, :, 0], PEER_TOPK)
        s2, i2 = lax.top_k(sc[:, :, 1], PEER_TOPK)
        comb = (s1[..., :, None] + s2[..., None, :]).reshape(PEER_BLOCK, PEER_HEADS, PEER_TOPK * PEER_TOPK)
        top, pos = lax.top_k(comb, PEER_TOPK)
        e = (jnp.take_along_axis(i1, pos // PEER_TOPK, axis=-1) * N_KEYS
             + jnp.take_along_axis(i2, pos % PEER_TOPK, axis=-1))
        gate = jax.nn.softmax(top, axis=-1)
        act = jnp.einsum('thkd,td->thk', u_tab[e], xb).astype(jnp.float32)
        hid = (gate * jax.nn.gelu(act, approximate=False)).astype(xb.dtype)
        return jnp.einsum('thk,thkd->td', hid, v_tab[e])

    return lax.map(block, xt).reshape(b, s, d)

def setup_inputs(seed: int = 0) -> dict:
    key = jax.random.key(seed)
    ks = jax.random.split(key, 20)
    nrm = jax.random.normal
    D = D_MODEL
    return {
        'x': nrm(ks[0], (BATCH, SEQ, D), jnp.float32),
        'p': nrm(ks[1], (DEPTH, BATCH, SEQ, PLE_DIM), jnp.float32),
        'norm_mix': 1.0 + 0.02 * nrm(ks[2], (DEPTH, D), jnp.float32),
        'w_in': nrm(ks[3], (DEPTH, D, IN_W), jnp.float32) * D ** -0.5,
        'gla_gate_w2': nrm(ks[4], (DEPTH, GLA_RANK, GLA_QK_W), jnp.float32) * GLA_RANK ** -0.5,
        'gla_gate_b': 0.1 * nrm(ks[5], (DEPTH, GLA_QK_W), jnp.float32),
        'gla_head_norm': 1.0 + 0.02 * nrm(ks[6], (DEPTH, GLA_DV), jnp.float32),
        'rel_bias': 0.1 * nrm(ks[7], (DEPTH, ATT_HEADS, 2 * REL_CLIP + 1), jnp.float32),
        'w_out': nrm(ks[8], (DEPTH, MIX_W, D), jnp.float32) * MIX_W ** -0.5,
        'norm_ffn': 1.0 + 0.02 * nrm(ks[9], (DEPTH, D), jnp.float32),
        'peer_wq': nrm(ks[10], (DEPTH, D, PEER_HEADS * PEER_DK), jnp.float32) * D ** -0.5,
        'peer_subkeys': nrm(ks[11], (DEPTH, PEER_HEADS, 2, N_KEYS, PEER_DK // 2), jnp.float32) * (PEER_DK // 2) ** -0.5,
        'peer_u': nrm(ks[12], (DEPTH, N_EXPERTS, D), jnp.float32) * D ** -0.5,
        'peer_v': nrm(ks[13], (DEPTH, N_EXPERTS, D), jnp.float32) * PEER_HEADS ** -0.5,
        'norm_ple': 1.0 + 0.02 * nrm(ks[14], (DEPTH, D), jnp.float32),
        'w_ple_gate': nrm(ks[15], (DEPTH, D, D), jnp.float32) * D ** -0.5,
        'w_ple': nrm(ks[16], (DEPTH, PLE_DIM, D), jnp.float32) * PLE_DIM ** -0.5,
        'final_norm': 1.0 + 0.02 * nrm(ks[17], (D,), jnp.float32),
    }

def reference(x, p, norm_mix, w_in, gla_gate_w2, gla_gate_b, gla_head_norm, rel_bias, w_out,
              norm_ffn, peer_wq, peer_subkeys, peer_u, peer_v, norm_ple, w_ple_gate, w_ple, final_norm):
    h = x
    for i in range(DEPTH):
        hn = rms_norm(h, norm_mix[i])
        proj = hn @ w_in[i]
        gq, gk, gv, glr, gog, aq, ak, av = jnp.split(proj, SPLIT_POINTS, axis=-1)
        o_gla = gla_group(gq, gk, gv, glr, gla_gate_w2[i], gla_gate_b[i], gla_head_norm[i], gog)
        o_att = band_attention(aq, ak, av, rel_bias[i])
        h = h + jnp.concatenate([o_gla, o_att], axis=-1) @ w_out[i]
        h = h + peer_ffn(rms_norm(h, norm_ffn[i]), peer_wq[i], peer_subkeys[i], peer_u[i], peer_v[i])
        gate = jax.nn.sigmoid(rms_norm(h, norm_ple[i]) @ w_ple_gate[i])
        h = h + (p[i] @ w_ple[i]) * gate
    return rms_norm(h, final_norm)


_drawn_inputs = setup_inputs


def setup_inputs(seed=0):
    import zlib

    import numpy as np

    out = dict(_drawn_inputs(seed))
    spreads = {}
    factors = {'gla_head_norm': 3.385,
     'rel_bias': 4.03,
     'norm_ple': 193.778,
     'final_norm': 23.755,
     'norm_ffn': 3.591}
    for name, (base, spread) in spreads.items():
        noise = np.random.default_rng([zlib.crc32(name.encode()), seed]).standard_normal(out[name].shape)
        drawn = base * np.exp(spread * noise) if base else spread * noise
        out[name] = __import__('jax').numpy.asarray(drawn.astype(out[name].dtype))
    for name, factor in factors.items():
        out[name] = (out[name] * factor).astype(out[name].dtype)
    return out
```

```python
import concourse.bass as bass
from concourse import mybir
from contextlib import ExitStack

F32 = mybir.dt.float32
F32R = mybir.dt.float32r
I32 = mybir.dt.int32
U32 = mybir.dt.uint32
ALU = mybir.AluOpType
ACT = mybir.ActivationFunctionType
AX = mybir.AxisListType

P = 128
SEQ, D = 512, 1024
NT, ND = SEQ // P, D // P
CHUNK = 64
NCH = SEQ // CHUNK
GLA_HEADS, GLA_DK, GLA_DV, RANK = 4, 64, 128, 16
ATT_HEADS, ATT_DH = 8, 64
REL_CLIP = 128
NEG = -1e30
EPS = 1e-6
GATE_NORM = 16.0
PH, NKEYS, TOPK = 8, 128, 16
PLE = 256
LOWEST = -3.0e38

UQ, UK, UV, UG, UAQ, UAK, UAV = 0, 2, 4, 8, 12, 16, 20
NU_IN = 24
GLR_COL = 1024
CAND = [(a, TOPK // (a + 1)) for a in range(TOPK)]
NCAND = sum(n for _, n in CAND)


class Chip:

    def __init__(self, nc, ctx):
        self.nc, self.ctx = nc, ctx

    def sem(self, name):
        return self.ctx.enter_context(self.nc.semaphore(name))

    def keep(self, name, shape, dt):
        return self.ctx.enter_context(self.nc.sbuf_tensor(name, shape, dt))


class Chain:

    def __init__(self, eng, sem):
        self.eng, self.sem, self.n = eng, sem, 0

    def step(self, ins):
        self.n += 1
        ins.then_inc(self.sem, 1)
        return self.n

    def wait(self, n=None):
        self.eng.wait_ge(self.sem, self.n if n is None else n)


def constants_and_load(c, x, small):
    nc = c.nc
    s_x, s_small, s_id = c.sem("x_loaded"), c.sem("small_loaded"), c.sem("ident_steps")
    with nc.Block() as block:

        @block.sync
        def _(sp):
            sp.dma_start(c.H[:], x[0].rearrange("(t p) d -> p t d", p=P)).then_inc(s_x, 16)
            for dst, src in small:
                sp.dma_start(dst, src).then_inc(s_small, 16)
            sp.wait_ge(s_x, 16)
            sp.wait_ge(s_small, 16 * len(small))

        @block.gpsimd
        def _(pool):
            nc.gpsimd.memset(c.ident[:], 0.0).then_inc(s_id, 1)
            pool.wait_ge(s_id, 1)
            nc.gpsimd.affine_select(out=c.ident[:], in_=c.ident[:], compare_op=ALU.not_equal, fill=1.0, base=0,
                                    pattern=[[-1, P]], channel_multiplier=1).then_inc(s_id, 1)


def normalize(c, tag):
    nc = c.nc
    with ExitStack() as mem:
        rms = mem.enter_context(nc.sbuf_tensor(f"rms_{tag}", [P, NT], F32))
        ssq = mem.enter_context(nc.sbuf_tensor(f"ssq_{tag}", [P, NT], F32))
        rstd = mem.enter_context(nc.sbuf_tensor(f"rstd_{tag}", [P, NT], F32))
        s_ssq, s_rms, s_rstd = c.sem(f"ssq_{tag}"), c.sem(f"rms_{tag}"), c.sem(f"rstd_{tag}")
        with nc.Block() as block:

            @block.scalar
            def _(act):
                for t in range(NT):
                    nc.scalar.activation(c.XN[:, t, :], c.H[:, t, :], ACT.Square,
                                         accum_out=ssq[:, t:t + 1]).then_inc(s_ssq, 1)
                act.wait_ge(s_ssq, NT)
                nc.scalar.activation(rms[:], ssq[:], ACT.Sqrt, scale=1.0 / D, bias=c.eps[:]).then_inc(s_rms, 1)
                act.wait_ge(s_rstd, 1)
                for t in range(NT):
                    nc.scalar.activation(c.XN[:, t, :], c.H[:, t, :], ACT.Copy, scale=rstd[:, t:t + 1])

            @block.vector
            def _(dve):
                dve.wait_ge(s_rms, 1)
                nc.vector.reciprocal(rstd[:], rms[:]).then_inc(s_rstd, 1)


def feature_major(c, tag, src, nd=ND, gain=None):
    nc = c.nc
    with ExitStack() as mem:
        ps = [mem.enter_context(nc.psum_tensor(f"nt_{tag}{i}", [P, NT, P], F32)) for i in range(4)]
        s_tr, s_hi, s_lo = c.sem(f"tr_{tag}"), c.sem(f"hi_{tag}"), c.sem(f"lo_{tag}")
        with nc.Block() as block:

            @block.tensor
            def _(pe):
                for d in range(nd):
                    if d >= 4:
                        pe.wait_ge(s_lo, d - 3)
                    for t in range(NT):
                        last = nc.tensor.transpose(ps[d % 4][:, t, :], src[:, t, d * P:(d + 1) * P], c.ident[:])
                    last.then_inc(s_tr, 1)

            @block.scalar
            def _(act):
                for d in range(nd):
                    act.wait_ge(s_tr, d + 1)
                    nc.scalar.activation(c.XH[:, d, :], ps[d % 4][:], ACT.Copy,
                                         scale=1.0 if gain is None else gain[:, d:d + 1]).then_inc(s_hi, 1)

            @block.vector
            def _(dve):
                for d in range(nd):
                    dve.wait_ge(s_hi, d + 1)
                    high = c.XH[:, d, :].bitcast(F32)
                    if gain is None:
                        nc.vector.tensor_tensor(c.XL[:, d, :], ps[d % 4][:], high, ALU.subtract).then_inc(s_lo, 1)
                    else:
                        nc.vector.scalar_tensor_tensor(out=c.XL[:, d, :], in0=ps[d % 4][:], scalar=gain[:, d:d + 1],
                                                       in1=high, op0=ALU.mult, op1=ALU.subtract).then_inc(s_lo, 1)


def add_rows(c, tag, src):
    nc = c.nc
    with ExitStack() as mem:
        ps = [mem.enter_context(nc.psum_tensor(f"ar_{tag}{i}", [P, NT, P], F32)) for i in range(4)]
        s_tr, s_add = c.sem(f"ar_tr_{tag}"), c.sem(f"ar_add_{tag}")
        with nc.Block() as block:

            @block.tensor
            def _(pe):
                for d in range(ND):
                    if d >= 4:
                        pe.wait_ge(s_add, d - 3)
                    for t in range(NT):
                        last = nc.tensor.transpose(ps[d % 4][:, t, :], src[:, d * SEQ + t * P:d * SEQ + (t + 1) * P],
                                                   c.ident[:])
                    last.then_inc(s_tr, 1)

            @block.vector
            def _(dve):
                for d in range(ND):
                    dve.wait_ge(s_tr, d + 1)
                    h = c.H[:, :, d * P:(d + 1) * P]
                    nc.vector.tensor_tensor(h, h, ps[d % 4][:], ALU.add).then_inc(s_add, 1)


def three_pass(nc, out, ah, al, bh, bl, first, final, skip=False):
    nc.tensor.matmul(out, ah, bh, start=first, stop=False, skip_group_check=skip)
    nc.tensor.matmul(out, ah, bl, start=False, stop=False, skip_group_check=skip)
    return nc.tensor.matmul(out, al, bh, start=False, stop=final, skip_group_check=skip)


def project(c, tag, jobs):
    nc = c.nc
    with ExitStack() as mem:
        stage = [mem.enter_context(nc.sbuf_tensor(f"wst_{tag}{i}", [P, ND, P], F32)) for i in range(2)]
        wh = [mem.enter_context(nc.sbuf_tensor(f"wh_{tag}{i}", [P, ND, P], F32R)) for i in range(2)]
        wl = [mem.enter_context(nc.sbuf_tensor(f"wl_{tag}{i}", [P, ND, P], F32R)) for i in range(2)]
        ps = [mem.enter_context(nc.psum_tensor(f"pp_{tag}{i}", [P, SEQ], F32)) for i in range(2)]
        s_w = [c.sem(f"w_{tag}{i}") for i in range(2)]
        s_hi, s_lo, s_pe, s_out = c.sem(f"whi_{tag}"), c.sem(f"wlo_{tag}"), c.sem(f"prod_{tag}"), c.sem(f"stored_{tag}")

        def turns(eng, body):
            base = 0
            for job in jobs:
                count = job[0]
                assert count <= 2 or count % 2 == 0
                if count <= 2:
                    for u in range(count):
                        body(u, (base + u) % 2, base + u, job)
                else:
                    if base == 0:
                        for u in range(2):
                            body(u, u % 2, u, job)
                        start = 1
                    else:
                        for u in range(2):
                            body(u, (base + u) % 2, base + u, job)
                        start = 1
                    with eng.Fori(start, count // 2) as i:
                        for j in range(2):
                            body(i * 2 + j, (base + j) % 2, i * 2 + (base + j), job)
                base += count

        with nc.Block() as block:

            @block.sync
            def _(sp):
                def load(u, b, n, job):
                    if not isinstance(n, int) or n >= 2:
                        sp.wait_ge(s_lo, n - 1)
                    sp.dma_start(stage[b][:, 0:job[2], 0:job[3]], job[1](u)).then_inc(s_w[b], 16)
                turns(sp, load)

            @block.scalar
            def _(act):
                def high(u, b, n, job):
                    if isinstance(n, int):
                        act.wait_ge(s_w[b], 16 * (n // 2 + 1))
                        if n >= 2:
                            act.wait_ge(s_pe, n - 1)
                    else:
                        act.wait_ge(s_w[b], n * 8 + (16 - 8 * b))
                        act.wait_ge(s_pe, n - 1)
                    nc.scalar.activation(wh[b][:, 0:job[2], 0:job[3]], stage[b][:, 0:job[2], 0:job[3]],
                                         ACT.Copy).then_inc(s_hi, 1)
                turns(act, high)

            @block.vector
            def _(dve):
                def low(u, b, n, job):
                    dve.wait_ge(s_hi, n + 1)
                    nc.vector.tensor_tensor(wl[b][:, 0:job[2], 0:job[3]], stage[b][:, 0:job[2], 0:job[3]],
                                            wh[b][:, 0:job[2], 0:job[3]].bitcast(F32),
                                            ALU.subtract).then_inc(s_lo, 1)

                def both(u, b, n, job):
                    low(u, b, n, job)
                    dve.wait_ge(s_pe, n + 1)
                    job[4](dve, ps[b], u, n, s_out)
                turns(dve, both)

            @block.tensor
            def _(pe):
                def product(u, b, n, job):
                    pe.wait_ge(s_lo, n + 1)
                    if not isinstance(n, int) or n >= 2:
                        pe.wait_ge(s_out, n - 1)
                    k, cols = job[2], job[3]
                    for d in range(k):
                        last = three_pass(nc, ps[b][0:cols, :], wh[b][:, d, 0:cols], wl[b][:, d, 0:cols],
                                          c.XH[:, d, :], c.XL[:, d, :], d == 0, d == k - 1)
                    last.then_inc(s_pe, 1)
                turns(pe, product)


def relative_bias(c, rel_bias):
    nc = c.nc
    W = 3 * P
    rows = nc.dram_tensor("rev_tables", (P, ATT_HEADS, W), F32, kind="Internal").ap()
    with ExitStack() as mem:
        table = mem.enter_context(nc.sbuf_tensor("rel_table", [P, ATT_HEADS, 2 * REL_CLIP + 1], F32))
        rev = mem.enter_context(nc.sbuf_tensor("rev", [P, ATT_HEADS, W], F32))
        s_t, s_rev, s_out, s_in = c.sem("table_loaded"), c.sem("table_reversed"), c.sem("table_stored"), c.sem("bias_loaded")
        with nc.Block() as block:

            @block.sync
            def _(sp):
                sp.dma_start(table[:], rel_bias.broadcast_to([P, ATT_HEADS, 2 * REL_CLIP + 1])).then_inc(s_t, 16)
                sp.wait_ge(s_rev, 3)
                sp.dma_start(rows, rev[:]).then_inc(s_out, 16)
                sp.wait_ge(s_out, 16)
                src = bass.AP(tensor=rows.tensor, offset=P - 1, ap=[[ATT_HEADS * W - 1, P], [W, ATT_HEADS], [1, 2 * P]])
                sp.dma_start(c.BIAS[:], src).then_inc(s_in, 16)
                sp.wait_ge(s_in, 16)

            @block.vector
            def _(dve):
                dve.wait_ge(s_t, 16)
                nc.vector.tensor_copy(rev[:, :, P - 1:W - 1], table[:, :, 2 * REL_CLIP:0:-1]).then_inc(s_rev, 1)
                nc.vector.tensor_copy(rev[:, :, 0:P - 1], table[:, :, 2 * REL_CLIP:2 * REL_CLIP + 1]
                                      .broadcast_to([P, ATT_HEADS, P - 1])).then_inc(s_rev, 1)
                nc.vector.tensor_copy(rev[:, :, W - 1:W], table[:, :, 0:1]).then_inc(s_rev, 1)

            @block.gpsimd
            def _(pool):
                pool.wait_ge(s_in, 16)
                nc.gpsimd.memset(c.BIAS[0:CHUNK, :, P + CHUNK:2 * P], NEG)


def tokens_as_rows(c):
    nc = c.nc
    units = [UV + i for i in range(4)] + [UG + i for i in range(4)] + [UAV + i for i in range(4)]
    with ExitStack() as mem:
        ps = [mem.enter_context(nc.psum_tensor(f"tok{i}", [P, NT, P], F32)) for i in range(4)]
        s_tr, s_act, s_dve = c.sem("tok_transposed"), c.sem("tok_stored_act"), c.sem("tok_stored_dve")
        with nc.Block() as block:

            @block.tensor
            def _(pe):
                for j, u in enumerate(units):
                    if j >= 4:
                        pe.wait_ge(s_dve if j % 2 else s_act, (j - 4) // 2 + 1)
                    for t in range(NT):
                        last = nc.tensor.transpose(ps[j % 4][:, t, :], c.PROJ[:, u * SEQ + t * P:u * SEQ + (t + 1) * P],
                                                   c.ident[:])
                    last.then_inc(s_tr, 1)

            @block.scalar
            def _(act):
                for j in range(0, 12, 2):
                    act.wait_ge(s_tr, j + 1)
                    nc.scalar.activation(c.TOK[:, :, j * P:(j + 1) * P], ps[j % 4][:], ACT.Copy).then_inc(s_act, 1)

            @block.vector
            def _(dve):
                for j in range(1, 12, 2):
                    dve.wait_ge(s_tr, j + 1)
                    nc.vector.tensor_copy(c.TOK[:, :, j * P:(j + 1) * P], ps[j % 4][:]).then_inc(s_dve, 1)


def gla(c, ins):
    nc = c.nc
    NP = GLA_HEADS // 2
    with ExitStack() as mem:
        def sb(name, shape, dt=F32):
            return mem.enter_context(nc.sbuf_tensor(name, shape, dt))

        w2 = sb("gate_w2", [RANK, GLA_HEADS * GLA_DK])
        b = sb("gate_b", [P, NP])
        hn = sb("head_norm", [P, GLA_DV])
        starts = sb("chunk_starts", [P, SEQ])
        one = sb("one", [P, 1])
        q1 = sb("q1", [P, NP, SEQ])
        k1 = sb("k1", [P, NP, SEQ])
        q2 = sb("q2", [P, NP, SEQ])
        k4 = sb("k4", [P, NP, SEQ])
        cum = sb("cum", [P, NP, SEQ])
        dm = sb("dm", [P, NP, SEQ])
        decay = sb("decay", [P, NP, NCH])
        KS = sb("KS", [P, NP, NT, P])
        AT = sb("AT", [P, GLA_HEADS, NT, P])
        SS = sb("states", [P, NP, NCH, 2 * GLA_DV])
        maskf = sb("maskf", [P, P])
        mask = sb("mask", [P, P], I32)
        ssq = sb("gla_ssq", [P, NT * GLA_HEADS])
        rms = sb("gla_rms", [P, NT * GLA_HEADS])
        rstd = sb("gla_rstd", [P, NT * GLA_HEADS])
        bank = [mem.enter_context(nc.psum_tensor(f"gb{i}", [P, SEQ], F32)) for i in range(8)]
        s_in, s_set = c.sem("gla_loaded"), c.sem("gla_consts")
        s_z, s_zmin, s_ln, s_d = c.sem("gla_z"), c.sem("gla_zmin"), c.sem("gla_ln"), c.sem("gla_diffs")
        s_e, s_a, s_v = c.sem("gla_exps"), c.sem("gla_act"), c.sem("gla_dve")
        s_qk, s_k4 = c.sem("gla_qk"), c.sem("gla_k4")
        s_ks, s_kss, s_at, s_ats = c.sem("gla_kst"), c.sem("gla_ks"), c.sem("gla_scores"), c.sem("gla_masked")
        s_kv, s_s, s_o, s_sq, s_sr, s_silu = c.sem("gla_kv"), c.sem("gla_state"), c.sem("gla_o"), c.sem("gla_sq"), \
            c.sem("gla_rms"), c.sem("gla_silu")
        s_ss, s_m = c.sem("gla_ssq"), c.sem("gla_out")

        def chunks(x):
            return x.rearrange("p (n c) -> p n c", c=CHUNK)

        with nc.Block() as block:

            @block.sync
            def _(sp):
                sp.dma_start(w2[:], ins["gla_gate_w2"][0]).then_inc(s_in, 16)
                with nc.allow_non_contiguous_dma(reason="1 KiB of gate bias, once"):
                    sp.dma_start(b[:], ins["gla_gate_b"][0].rearrange("(m p) -> p m", p=P)).then_inc(s_in, 16)
                sp.dma_start(hn[:], ins["gla_head_norm"].broadcast_to([P, GLA_DV])).then_inc(s_in, 16)

            @block.gpsimd
            def _(pool):
                nc.gpsimd.memset(starts[:], 1.0).then_inc(s_set, 1)
                nc.gpsimd.memset(one[:], 1.0).then_inc(s_set, 1)
                nc.gpsimd.memset(maskf[:], 1.0).then_inc(s_set, 1)
                nc.gpsimd.memset(AT[:], 0.0).then_inc(s_set, 1)
                for m in range(NP):
                    nc.gpsimd.memset(SS[:, m, 0, :], 0.0).then_inc(s_set, 1)
                pool.wait_ge(s_set, 4 + NP)
                nc.gpsimd.memset(chunks(starts[:])[:, :, 0:1], 0.0).then_inc(s_set, 1)
                nc.gpsimd.affine_select(out=maskf[:], in_=maskf[:], compare_op=ALU.is_ge, fill=0.0, base=0,
                                        pattern=[[1, P]], channel_multiplier=-1).then_inc(s_set, 1)
                pool.wait_ge(s_set, 6 + NP)
                nc.gpsimd.memset(maskf[0:CHUNK, CHUNK:P], 0.0).then_inc(s_set, 1)

            ALL_SET = 7 + NP

            @block.tensor
            def _(pe):
                pe.wait_ge(s_in, 48)
                for m in range(NP):
                    nc.tensor.matmul(bank[4 + m][:], w2[:, m * P:(m + 1) * P], c.GLR[:], start=True,
                                     stop=True).then_inc(s_z, 1)
                pe.wait_ge(s_qk, 2 * NP)
                for h in range(GLA_HEADS):
                    m, r = h // 2, GLA_DK * (h % 2)
                    for t in range(NT):
                        last = nc.tensor.matmul(bank[h][:, t * P:(t + 1) * P], k1[r:r + GLA_DK, m, t * P:(t + 1) * P],
                                                q1[r:r + GLA_DK, m, t * P:(t + 1) * P], start=True, stop=True)
                    last.then_inc(s_at, 1)
                for m in range(NP):
                    pe.wait_ge(s_k4, m + 1)
                    for t in range(NT):
                        last = nc.tensor.transpose(bank[6 + m][:, t * P:(t + 1) * P], k4[:, m, t * P:(t + 1) * P],
                                                   c.ident[:])
                    last.then_inc(s_ks, 1)
                pe.wait_ge(s_kss, NP)
                for n in range(NCH - 1):
                    for m in range(NP):
                        i = n * NP + m
                        if i >= 4:
                            pe.wait_ge(s_s, i - 3)
                        rows = slice(CHUNK * (n % 2), CHUNK * (n % 2) + CHUNK)
                        nc.tensor.matmul(bank[4 + i % 4][:, 0:2 * GLA_DV], KS[rows, m, n // 2, :],
                                         c.TOK[rows, n // 2, m * 2 * GLA_DV:(m + 1) * 2 * GLA_DV],
                                         start=True, stop=True).then_inc(s_kv, 1)
                pe.wait_ge(s_ats, GLA_HEADS)
                pe.wait_ge(s_s, NP * (NCH - 1))
                for t in range(NT):
                    for h in range(GLA_HEADS):
                        m, r = h // 2, GLA_DK * (h % 2)
                        o = bank[t + NT * (h % 2)]
                        cols = slice(m * GLA_DV, (m + 1) * GLA_DV)
                        nc.tensor.matmul(o[:, cols], AT[:, h, t, :], c.TOK[:, t, h * GLA_DV:(h + 1) * GLA_DV],
                                         start=True, stop=False, skip_group_check=True)
                        for half in range(2):
                            n = 2 * t + half
                            rows = slice(CHUNK * half, CHUNK * half + CHUNK)
                            last = nc.tensor.matmul(
                                o[rows, cols], q2[r:r + GLA_DK, m, n * CHUNK:(n + 1) * CHUNK],
                                SS[r:r + GLA_DK, m, n, (h % 2) * GLA_DV:(h % 2 + 1) * GLA_DV],
                                start=False, stop=True, skip_group_check=True)
                    last.then_inc(s_o, 1)

            @block.scalar
            def _(act):
                act.wait_ge(s_in, 48)
                ch = Chain(act, s_a)
                for m in range(NP):
                    act.wait_ge(s_z, m + 1)
                    ch.step(nc.scalar.activation(k1[:, m, :], bank[4 + m][:], ACT.Abs, bias=b[:, m:m + 1]))
                ch.wait()
                ch.step(nc.scalar.activation(k1[:], k1[:], ACT.Exp, scale=-1.0))
                ch.wait()
                act.wait_ge(s_set, ALL_SET)
                nc.scalar.activation(k1[:], k1[:], ACT.Ln, bias=one[:]).then_inc(s_ln, 1)
                act.wait_ge(s_d, 2)
                g = 1.0 / GATE_NORM
                nc.scalar.activation(q1[:], dm[:], ACT.Exp, scale=g).then_inc(s_e, 1)
                nc.scalar.activation(k1[:], dm[:], ACT.Exp, scale=-g).then_inc(s_e, 1)
                nc.scalar.activation(q2[:], cum[:], ACT.Exp, scale=g).then_inc(s_e, 1)
                act.wait_ge(s_d, 4)
                nc.scalar.activation(k4[:], k4[:], ACT.Exp, scale=g).then_inc(s_e, 1)
                for m in range(NP):
                    ch.step(nc.scalar.activation(decay[:, m, :], chunks(cum[:, m, :])[:, :, CHUNK - 1], ACT.Exp, scale=g))
                gates = c.TOK[:, :, GLA_HEADS * GLA_DV:2 * GLA_HEADS * GLA_DV]
                nc.scalar.activation(gates, gates, ACT.Silu).then_inc(s_silu, 1)
                for t in range(NT):
                    act.wait_ge(s_o, t + 1)
                    if t == 0:
                        act.wait_ge(s_o, NT)
                    for s in range(2):
                        nc.scalar.activation(AT[:, t, s::2, :], bank[t + NT * s][:, 0:NP * GLA_DV].rearrange(
                            "p (h e) -> p h e", e=P), ACT.Square).then_inc(s_sq, 1)
                act.wait_ge(s_ss, NT)
                nc.scalar.activation(rms[:], ssq[:], ACT.Sqrt, scale=1.0 / GLA_DV, bias=c.eps[:]).then_inc(s_sr, 1)

            @block.vector
            def _(dve):
                ch = Chain(dve, s_v)
                dve.wait_ge(s_in, 48)
                for m in range(NP):
                    dve.wait_ge(s_a, m + 1)
                    ch.step(nc.vector.tensor_scalar(q1[:, m, :], bank[4 + m][:], b[:, m:m + 1], 0.0, ALU.add, ALU.min))
                dve.wait_ge(s_set, ALL_SET)
                ch.step(nc.vector.tensor_copy(mask[:], maskf[:]))
                dve.wait_ge(s_ln, 1)
                ch.wait()
                for m in range(NP):
                    ch.step(nc.vector.tensor_tensor(q1[:, m, :], q1[:, m, :], k1[:, m, :], ALU.subtract))
                ch.wait()
                for m in range(NP):
                    ch.step(nc.vector.tensor_tensor_scan(cum[:, m, :], starts[:], q1[:, m, :], 0.0, ALU.mult, ALU.add))
                ch.wait()
                for m in range(NP):
                    x = chunks(cum[:, m, :])
                    nc.vector.tensor_tensor(chunks(dm[:, m, :]), x, x[:, :, CHUNK // 2:CHUNK // 2 + 1]
                                            .broadcast_to([P, NCH, CHUNK]), ALU.subtract).then_inc(s_d, 1)
                for m in range(NP):
                    x = chunks(cum[:, m, :])
                    nc.vector.tensor_tensor(chunks(k4[:, m, :]), x[:, :, CHUNK - 1:CHUNK].broadcast_to([P, NCH, CHUNK]),
                                            x, ALU.subtract).then_inc(s_d, 1)
                Q, K = [c.PROJ[:, u * SEQ:(u + NP) * SEQ].rearrange("p (m t) -> p m t", m=NP) for u in (UQ, UK)]
                scale = GLA_DK ** -0.5
                dve.wait_ge(s_e, 2)
                for m in range(NP):
                    nc.vector.scalar_tensor_tensor(out=q1[:, m, :], in0=Q[:, m, :], scalar=scale, in1=q1[:, m, :],
                                                   op0=ALU.mult, op1=ALU.mult).then_inc(s_qk, 1)
                    nc.vector.tensor_tensor(k1[:, m, :], K[:, m, :], k1[:, m, :], ALU.mult).then_inc(s_qk, 1)
                dve.wait_ge(s_e, 4)
                for m in range(NP):
                    nc.vector.tensor_tensor(k4[:, m, :], K[:, m, :], k4[:, m, :], ALU.mult).then_inc(s_k4, 1)
                for m in range(NP):
                    ch.step(nc.vector.scalar_tensor_tensor(out=q2[:, m, :], in0=Q[:, m, :], scalar=scale,
                                                           in1=q2[:, m, :], op0=ALU.mult, op1=ALU.mult))
                for h in range(GLA_HEADS):
                    dve.wait_ge(s_at, h + 1)
                    if h == 0:
                        ch.wait()
                    nc.vector.copy_predicated(AT[:, h, :, :], mask[:].unsqueeze(1).broadcast_to([P, NT, P]),
                                              bank[h][:].rearrange("p (t i) -> p t i", t=NT)).then_inc(s_ats, 1)
                for m in range(NP):
                    dve.wait_ge(s_ks, m + 1)
                    nc.vector.tensor_copy(KS[:, m, :, :], bank[6 + m][:].rearrange("p (t i) -> p t i", t=NT)).then_inc(s_kss, 1)
                dve.wait_ge(s_a, NP + 1 + NP)
                for n in range(NCH - 1):
                    for m in range(NP):
                        i = n * NP + m
                        dve.wait_ge(s_kv, i + 1)
                        if n:
                            dve.wait_ge(s_s, i - 1)
                        nc.vector.scalar_tensor_tensor(
                            out=SS[:, m, n + 1, :], in0=SS[:, m, n, :], scalar=decay[:, m, n:n + 1],
                            in1=bank[4 + i % 4][:, 0:2 * GLA_DV], op0=ALU.mult, op1=ALU.add).then_inc(s_s, 1)
                for t in range(NT):
                    dve.wait_ge(s_sq, 2 * (t + 1))
                    nc.vector.tensor_reduce(ssq[:, t * GLA_HEADS:(t + 1) * GLA_HEADS], AT[:, t, :, :], AX.X,
                                            ALU.add).then_inc(s_ss, 1)
                dve.wait_ge(s_sr, 1)
                ch.step(nc.vector.reciprocal(rstd[:], rms[:]))
                ch.wait()
                dve.wait_ge(s_silu, 1)
                W = GLA_HEADS * GLA_DV
                for t in range(NT):
                    o = c.MIX[:, t, 0:W].rearrange("p (h e) -> p h e", e=GLA_DV)
                    for s in range(2):
                        ch.step(nc.vector.tensor_tensor(
                            o[:, s::2, :], bank[t + NT * s][:, 0:NP * GLA_DV].rearrange("p (h e) -> p h e", e=GLA_DV),
                            rstd[:, t * GLA_HEADS + s:(t + 1) * GLA_HEADS:2].unsqueeze(2)
                            .broadcast_to([P, NP, GLA_DV]), ALU.mult))
                ch.wait()
                for t in range(NT):
                    o = c.MIX[:, t, 0:W].rearrange("p (h e) -> p h e", e=GLA_DV)
                    ch.step(nc.vector.tensor_tensor(o, o, hn[:].unsqueeze(1).broadcast_to([P, GLA_HEADS, GLA_DV]),
                                                    ALU.mult))
                ch.wait()
                for t in range(NT):
                    nc.vector.tensor_tensor(c.MIX[:, t, 0:W], c.MIX[:, t, 0:W], c.TOK[:, t, W:2 * W],
                                            ALU.mult).then_inc(s_m, 1)


def band_attention(c):
    nc = c.nc
    steps = [(t, h) for t in range(NT) for h in range(ATT_HEADS)]
    N = len(steps)
    scale = ATT_DH ** -0.5
    V0 = 2 * GLA_HEADS * GLA_DV
    with ExitStack() as mem:
        def sb(name, shape, dt=F32):
            return mem.enter_context(nc.sbuf_tensor(name, shape, dt))

        sc = [sb(f"att_sc{i}", [P, SEQ]) for i in range(2)]
        pr = [sb(f"att_p{i}", [P, SEQ]) for i in range(2)]
        pt = [sb(f"att_pt{i}", [P, SEQ]) for i in range(2)]
        nmax = sb("att_nmax", [P, N])
        rsum = sb("att_rsum", [P, N])
        rinv = sb("att_rinv", [P, N])
        ps_s = [mem.enter_context(nc.psum_tensor(f"as{i}", [P, SEQ], F32)) for i in range(2)]
        ps_t = [mem.enter_context(nc.psum_tensor(f"at{i}", [P, SEQ], F32)) for i in range(2)]
        ps_o = [mem.enter_context(nc.psum_tensor(f"ao{i}", [P, SEQ], F32)) for i in range(2)]
        s_qk, s_sc, s_mx, s_p, s_pt, s_pts = (c.sem("att_" + n) for n in ("qk", "biased", "max", "exp", "ptr", "pts"))
        s_pv, s_o, s_ri = (c.sem("att_" + n) for n in ("pv", "out", "rinv"))

        with nc.Block() as block:

            @block.tensor
            def _(pe):
                def scores(i):
                    t, h = steps[i]
                    r = ATT_DH * (h % 2)
                    q0 = (UAQ + h // 2) * SEQ + t * P
                    k0 = (UAK + h // 2) * SEQ
                    if i >= 2:
                        pe.wait_ge(s_sc, 2 * (i - 1))
                    nc.tensor.matmul(ps_s[i % 2][:, 0:(t + 1) * P], c.PROJ[r:r + ATT_DH, q0:q0 + P],
                                     c.PROJ[r:r + ATT_DH, k0:k0 + (t + 1) * P], start=True, stop=True).then_inc(s_qk, 1)

                def flip(i):
                    t, h = steps[i]
                    pe.wait_ge(s_p, i + 1)
                    if i >= 2:
                        pe.wait_ge(s_pts, i - 1)
                    for k in range(t + 1):
                        last = nc.tensor.transpose(ps_t[i % 2][:, k * P:(k + 1) * P], pr[i % 2][:, k * P:(k + 1) * P],
                                                   c.ident[:])
                    last.then_inc(s_pt, 1)

                def values(i):
                    t, h = steps[i]
                    pe.wait_ge(s_pts, i + 1)
                    if h == 0 and t >= 2:
                        pe.wait_ge(s_o, t - 1)
                    for k in range(t + 1):
                        last = nc.tensor.matmul(ps_o[t % 2][:, h * ATT_DH:(h + 1) * ATT_DH], pt[i % 2][:, k * P:(k + 1) * P],
                                                c.TOK[:, k, V0 + h * ATT_DH:V0 + (h + 1) * ATT_DH],
                                                start=(k == 0), stop=(k == t))
                    last.then_inc(s_pv, 1)

                for i in range(N + 2):
                    if i < N:
                        scores(i)
                    if 0 <= i - 1 < N:
                        flip(i - 1)
                    if i - 2 >= 0:
                        values(i - 2)

            @block.vector
            def _(dve):
                def biased(i):
                    t, h = steps[i]
                    dve.wait_ge(s_qk, i + 1)
                    if i >= 2:
                        dve.wait_ge(s_p, i - 1)
                    far = max(0, (t - 1) * P)
                    n = (t + 1) * P - far
                    if far:
                        nc.vector.tensor_scalar(sc[i % 2][:, 0:far], ps_s[i % 2][:, 0:far], scale, c.BIAS[:, h, 0:1],
                                                ALU.mult, ALU.add).then_inc(s_sc, 1)
                    nc.vector.scalar_tensor_tensor(
                        out=sc[i % 2][:, far:far + n], in0=ps_s[i % 2][:, far:far + n], scalar=scale,
                        in1=c.BIAS[:, h, 2 * P - n:2 * P], op0=ALU.mult, op1=ALU.add).then_inc(s_sc, 1 if far else 2)
                    dve.wait_ge(s_sc, 2 * (i + 1))
                    nc.vector.tensor_reduce(nmax[:, i:i + 1], sc[i % 2][:, 0:far + n], AX.X, ALU.max,
                                            negate=True).then_inc(s_mx, 1)

                def keep(i):
                    t, h = steps[i]
                    dve.wait_ge(s_pt, i + 1)
                    if i >= 2:
                        dve.wait_ge(s_pv, i - 1)
                    nc.vector.tensor_copy(pt[i % 2][:, 0:(t + 1) * P], ps_t[i % 2][:, 0:(t + 1) * P]).then_inc(s_pts, 1)

                def output(t):
                    a = t * ATT_HEADS
                    dve.wait_ge(s_p, a + ATT_HEADS)
                    nc.vector.reciprocal(rinv[:, a:a + ATT_HEADS], rsum[:, a:a + ATT_HEADS]).then_inc(s_ri, 1)
                    dve.wait_ge(s_ri, t + 1)
                    dve.wait_ge(s_pv, a + ATT_HEADS)
                    nc.vector.tensor_tensor(
                        c.MIX[:, t, SEQ:2 * SEQ].rearrange("p (h e) -> p h e", e=ATT_DH),
                        ps_o[t % 2][:].rearrange("p (h e) -> p h e", e=ATT_DH),
                        rinv[:, a:a + ATT_HEADS].unsqueeze(2).broadcast_to([P, ATT_HEADS, ATT_DH]),
                        ALU.mult).then_inc(s_o, 1)

                for i in range(N + 3):
                    if i < N:
                        biased(i)
                    if 0 <= i - 1 < N:
                        keep(i - 1)
                    if i - 2 >= 0 and (i - 2) % ATT_HEADS == ATT_HEADS - 1 and i - 2 < N:
                        output((i - 2) // ATT_HEADS)

            @block.scalar
            def _(act):
                for i, (t, h) in enumerate(steps):
                    act.wait_ge(s_mx, i + 1)
                    if i >= 2:
                        act.wait_ge(s_pt, i - 1)
                    nc.scalar.activation(pr[i % 2][:, 0:(t + 1) * P], sc[i % 2][:, 0:(t + 1) * P], ACT.Exp,
                                         bias=nmax[:, i:i + 1], accum_out=rsum[:, i:i + 1]).then_inc(s_p, 1)


def key_scores(c, subkeys):
    nc = c.nc
    U = 2 * PH
    with ExitStack() as mem:
        keys = mem.enter_context(nc.sbuf_tensor("keys", [P, U, P], F32))
        kh = mem.enter_context(nc.sbuf_tensor("keys_hi", [P, U * P], F32R))
        kl = mem.enter_context(nc.sbuf_tensor("keys_lo", [P, U * P], F32R))
        ps = [mem.enter_context(nc.psum_tensor(f"kt{i}", [P, SEQ], F32)) for i in range(4)]
        s_k, s_tr, s_hi, s_lo = c.sem("keys_loaded"), c.sem("keys_tr"), c.sem("keys_high"), c.sem("keys_low")
        s_sc, s_st = c.sem("scores"), [c.sem("scores_even"), c.sem("scores_odd")]
        with nc.Block() as block:

            @block.sync
            def _(sp):
                sp.dma_start(keys[:], subkeys.rearrange("h s n d -> n (h s) d")).then_inc(s_k, 16)

            @block.tensor
            def _(pe):
                pe.wait_ge(s_k, 16)
                for g in range(U // 4):
                    for j in range(4):
                        last = nc.tensor.transpose(ps[g][:, j * P:(j + 1) * P], keys[:, 4 * g + j, :], c.ident[:])
                    last.then_inc(s_tr, 1)
                pe.wait_ge(s_lo, U // 4)
                for u in range(U):
                    if u >= 4:
                        pe.wait_ge(s_st[u % 2], (u - 4) // 2 + 1)
                    for t in range(NT):
                        a = slice(u * SEQ + t * P, u * SEQ + (t + 1) * P)
                        k = slice(u * P, (u + 1) * P)
                        last = three_pass(nc, ps[u % 4][:, t * P:(t + 1) * P], c.QH[:, a], c.QL[:, a], kh[:, k],
                                          kl[:, k], True, True)
                    last.then_inc(s_sc, 1)

            @block.scalar
            def _(act):
                for g in range(U // 4):
                    act.wait_ge(s_tr, g + 1)
                    nc.scalar.activation(kh[:, g * SEQ:(g + 1) * SEQ], ps[g][:], ACT.Copy).then_inc(s_hi, 1)
                for u in range(0, U, 2):
                    act.wait_ge(s_sc, u + 1)
                    nc.scalar.activation(c.SC[:, :, u, :], ps[u % 4][:].rearrange("p (t n) -> p t n", t=NT),
                                         ACT.Copy).then_inc(s_st[0], 1)

            @block.vector
            def _(dve):
                for g in range(U // 4):
                    dve.wait_ge(s_hi, g + 1)
                    nc.vector.tensor_tensor(kl[:, g * SEQ:(g + 1) * SEQ], ps[g][:],
                                            kh[:, g * SEQ:(g + 1) * SEQ].bitcast(F32), ALU.subtract).then_inc(s_lo, 1)
                for u in range(1, U, 2):
                    dve.wait_ge(s_sc, u + 1)
                    nc.vector.tensor_copy(c.SC[:, :, u, :],
                                          ps[u % 4][:].rearrange("p (t n) -> p t n", t=NT)).then_inc(s_st[1], 1)


def select_experts(c):
    nc = c.nc
    U, NPAIR = 2 * PH, PH * TOPK
    runs, off = [], 0
    for a, n in CAND:
        if runs and runs[-1][2] == n:
            runs[-1][1] += 1
        else:
            runs.append([a, 1, n, off])
        off += n
    with ExitStack() as mem:
        def sb(name, shape, dt=F32):
            return mem.enter_context(nc.sbuf_tensor(name, shape, dt))

        rest = sb("rest", [P, U, NKEYS])
        top = sb("top", [P, U, TOPK])
        idx = sb("idx", [P, U, TOPK], U32)
        idxf = sb("idxf", [P, U, TOPK])
        cv = sb("cand_values", [P, PH, NCAND])
        cr = sb("cand_rest", [P, PH, NCAND])
        ce = sb("cand_experts", [P, PH, NCAND])
        best = sb("best", [P, PH, TOPK])
        pos = sb("pos", [P, PH, TOPK], U32)
        posf = sb("posf", [P, PH, TOPK])
        iota = sb("iota_cand", [P, NCAND])
        hit = sb("hit", [P, PH, TOPK, NCAND])
        ex = sb("exp_gate", [P, PH, TOPK])
        esum = sb("exp_sum", [P, PH])
        gate = sb("gate", [P, NT, NPAIR])
        expert = sb("expert", [P, NT, NPAIR])
        e_int = sb("expert_int", [P, NT, NPAIR], I32)
        part = [sb(f"expert_part{i}", [P, NT, NPAIR], I32) for i in range(2)]
        partf = [sb(f"expert_partf{i}", [P, NT, NPAIR]) for i in range(2)]
        ps = [mem.enter_context(nc.psum_tensor(f"se{i}", [P, SEQ], F32)) for i in range(3)]
        s_iota, s_v, s_d, s_ex = c.sem("iota_cand_set"), c.sem("select_dve"), c.sem("gate_diffs"), c.sem("gate_exps")
        s_oh, s_hit, s_tr, s_red = c.sem("hits_found"), c.sem("hits_weighted"), c.sem("pairs_tr"), c.sem("experts_found")
        with nc.Block() as block:

            @block.gpsimd
            def _(pool):
                nc.gpsimd.iota(iota[:], [[1, NCAND]], base=0, channel_multiplier=0,
                               allow_small_or_imprecise_dtypes=True).then_inc(s_iota, 1)
                for t in range(NT):
                    pool.wait_ge(s_oh, t + 1)
                    for h in range(PH):
                        last = nc.gpsimd.tensor_tensor(hit[:, h, :, :], hit[:, h, :, :],
                                                       ce[:, h, :].unsqueeze(1).broadcast_to([P, TOPK, NCAND]), ALU.mult)
                    last.then_inc(s_hit, 1)

            @block.scalar
            def _(act):
                for t in range(NT):
                    act.wait_ge(s_d, t + 1)
                    nc.scalar.activation(ex[:], ex[:], ACT.Exp).then_inc(s_ex, 1)

            @block.vector
            def _(dve):
                ch = Chain(dve, s_v)
                for t in range(NT):
                    for u in range(U):
                        ch.step(nc.vector.max(top[:, u, 0:8], c.SC[:, t, u, :]))
                    ch.wait()
                    for u in range(U):
                        ch.step(nc.vector.match_replace(rest[:, u, :], top[:, u, 0:8], c.SC[:, t, u, :], LOWEST))
                    for u in range(U):
                        ch.step(nc.vector.max_index(idx[:, u, 0:8], top[:, u, 0:8], c.SC[:, t, u, :]))
                    ch.wait(ch.n - U)
                    for u in range(U):
                        ch.step(nc.vector.max(top[:, u, 8:16], rest[:, u, :]))
                    ch.wait()
                    for u in range(U):
                        ch.step(nc.vector.max_index(idx[:, u, 8:16], top[:, u, 8:16], rest[:, u, :]))
                    v = top[:].rearrange("p (h s) k -> p h s k", s=2)
                    for a0, na, n, o in runs:
                        ch.step(nc.vector.tensor_tensor(
                            cv[:, :, o:o + na * n].rearrange("p h (a b) -> p h a b", b=n),
                            v[:, :, 0, a0:a0 + na].unsqueeze(3).broadcast_to([P, PH, na, n]),
                            v[:, :, 1, 0:n].unsqueeze(2).broadcast_to([P, PH, na, n]), ALU.add))
                    ch.wait()
                    ch.step(nc.vector.tensor_copy(idxf[:], idx[:]))
                    for h in range(PH):
                        ch.step(nc.vector.max(best[:, h, 0:8], cv[:, h, :]))
                    ch.wait(ch.n - PH)
                    i1 = idxf[:].rearrange("p (h s) k -> p h s k", s=2)[:, :, 0, :]
                    i2 = idxf[:].rearrange("p (h s) k -> p h s k", s=2)[:, :, 1, :]
                    if t:
                        dve.wait_ge(s_hit, t)
                    ch.step(nc.vector.tensor_scalar(i1, i1, float(NKEYS), None, ALU.mult))
                    ch.wait()
                    for h in range(PH):
                        ch.step(nc.vector.match_replace(cr[:, h, :], best[:, h, 0:8], cv[:, h, :], LOWEST))
                    for a0, na, n, o in runs:
                        ch.step(nc.vector.tensor_tensor(
                            ce[:, :, o:o + na * n].rearrange("p h (a b) -> p h a b", b=n),
                            i1[:, :, a0:a0 + na].unsqueeze(3).broadcast_to([P, PH, na, n]),
                            i2[:, :, 0:n].unsqueeze(2).broadcast_to([P, PH, na, n]), ALU.add))
                    ch.wait()
                    for h in range(PH):
                        ch.step(nc.vector.max(best[:, h, 8:16], cr[:, h, :]))
                    for h in range(PH):
                        ch.step(nc.vector.max_index(pos[:, h, 0:8], best[:, h, 0:8], cv[:, h, :]))
                    ch.wait(ch.n - PH)
                    for h in range(PH):
                        ch.step(nc.vector.max_index(pos[:, h, 8:16], best[:, h, 8:16], cr[:, h, :]))
                    nc.vector.tensor_tensor(ex[:], best[:], best[:, :, 0:1].broadcast_to([P, PH, TOPK]),
                                            ALU.subtract).then_inc(s_d, 1)
                    ch.wait()
                    ch.step(nc.vector.tensor_copy(posf[:], pos[:]))
                    dve.wait_ge(s_ex, t + 1)
                    ch.step(nc.vector.tensor_reduce(esum[:], ex[:], AX.X, ALU.add))
                    ch.wait()
                    if t == 0:
                        dve.wait_ge(s_iota, 1)
                    if t:
                        dve.wait_ge(s_red, t)
                    for h in range(PH):
                        last = nc.vector.tensor_tensor(
                            hit[:, h, :, :], iota[:].unsqueeze(1).broadcast_to([P, TOPK, NCAND]),
                            posf[:, h, :].unsqueeze(2).broadcast_to([P, TOPK, NCAND]), ALU.is_equal)
                    last.then_inc(s_oh, 1)
                    ch.step(nc.vector.reciprocal(esum[:], esum[:]))
                    ch.wait()
                    ch.step(nc.vector.tensor_tensor(gate[:, t, :].rearrange("p (h k) -> p h k", h=PH), ex[:],
                                                    esum[:].unsqueeze(2).broadcast_to([P, PH, TOPK]), ALU.mult))
                    dve.wait_ge(s_hit, t + 1)
                    nc.vector.tensor_reduce(expert[:, t, :].rearrange("p (h k) -> p h k", h=PH), hit[:], AX.X,
                                            ALU.add).then_inc(s_red, 1)
                dve.wait_ge(s_red, NT)
                ch.step(nc.vector.tensor_copy(e_int[:], expert[:]))
                ch.wait()
                ch.step(nc.vector.tensor_scalar(part[0][:], e_int[:], 7, None, ALU.arith_shift_right))
                ch.step(nc.vector.tensor_scalar(part[1][:], e_int[:], NKEYS - 1, None, ALU.bitwise_and))
                ch.wait()
                for i in range(2):
                    ch.step(nc.vector.tensor_copy(partf[i][:], part[i][:]))
                for i, dst in enumerate((c.I1T, c.I2T, c.GT)):
                    dve.wait_ge(s_tr, i + 1)
                    nc.vector.tensor_copy(dst[:], ps[i][:])
                c.select_steps = ch.n

            @block.tensor
            def _(pe):
                pe.wait_ge(s_v, c.select_steps)
                for i, src in enumerate((partf[0], partf[1], gate)):
                    for t in range(NT):
                        last = nc.tensor.transpose(ps[i][:, t * P:(t + 1) * P], src[:, t, :], c.ident[:])
                    last.then_inc(s_tr, 1)


GT_BLK = 64
NB = SEQ // GT_BLK


def dense_gates(c):
    nc = c.nc
    RING, Q = 16, 4
    with ExitStack() as mem:
        iota = mem.enter_context(nc.sbuf_tensor("iota_keys", [P, NKEYS], F32))
        oh2 = mem.enter_context(nc.sbuf_tensor("one_hot2", [P, RING, NKEYS], F32))
        oh1 = mem.enter_context(nc.sbuf_tensor("gated_hot1", [P, RING, NKEYS], F32))
        blk = [mem.enter_context(nc.sbuf_tensor(f"gate_block{i}", [P, NKEYS, GT_BLK], F32)) for i in range(2)]
        ps = [mem.enter_context(nc.psum_tensor(f"dg{i}", [P, SEQ], F32)) for i in range(4)]
        s_iota, s_hot, s_pe, s_st = c.sem("iota_keys_set"), c.sem("one_hots"), c.sem("gates_made"), c.sem("gates_stored")
        s_dma = [c.sem("gate_block_out0"), c.sem("gate_block_out1")]
        with nc.Block() as block:

            @block.gpsimd
            def _(pool):
                nc.gpsimd.iota(iota[:], [[1, NKEYS]], base=0, channel_multiplier=0,
                               allow_small_or_imprecise_dtypes=True).then_inc(s_iota, 1)

            @block.vector
            def _(dve):
                dve.wait_ge(s_iota, 1)

                def hots(i, first):
                    for r in range(RING):
                        if r % Q == 0 and not first:
                            dve.wait_ge(s_pe, i * 4 + (r // Q - 3))
                        tok = bass.ds(i * RING + r, 1)
                        nc.vector.tensor_scalar(oh2[:, r, :], iota[:], c.I2T[:, tok], None, ALU.is_equal)
                        last = nc.vector.tensor_scalar(oh1[:, r, :], iota[:], c.I1T[:, tok], c.GT[:, tok],
                                                       ALU.is_equal, ALU.mult)
                        if r % Q == Q - 1:
                            last.then_inc(s_hot, 1)
                hots(0, True)
                with dve.Fori(1, SEQ // RING) as i:
                    hots(i, False)

            @block.tensor
            def _(pe):
                def products(i, first):
                    for q in range(RING // Q):
                        pe.wait_ge(s_hot, i * 4 + (q + 1))
                        if not first:
                            pe.wait_ge(s_st, i * 4 + (q - 3))
                        for r in range(q * Q, q * Q + Q):
                            last = nc.tensor.matmul(ps[q][:, (r % Q) * P:(r % Q + 1) * P], oh2[:, r, :], oh1[:, r, :],
                                                    start=True, stop=True)
                        last.then_inc(s_pe, 1)
                products(0, True)
                with pe.Fori(1, SEQ // RING) as i:
                    products(i, False)

            @block.scalar
            def _(act):
                per = GT_BLK // Q

                def stores(i, first):
                    for b in range(2):
                        if not first:
                            act.wait_ge(s_dma[b], i * 16)
                        for q in range(per):
                            act.wait_ge(s_pe, i * (2 * per) + (b * per + q + 1))
                            nc.scalar.activation(blk[b][:, :, q * Q:(q + 1) * Q],
                                                 ps[q % 4][:].rearrange("p (t n) -> p n t", t=Q),
                                                 ACT.Copy).then_inc(s_st, 1)
                stores(0, True)
                with act.Fori(1, NB // 2) as i:
                    stores(i, False)

            @block.sync
            def _(sp):
                per = GT_BLK // Q
                for i in range(NB // 2):
                    for b in range(2):
                        sp.wait_ge(s_st, (2 * i + b + 1) * per)
                        sp.dma_start(c.gates[2 * i + b], blk[b][:]).then_inc(s_dma[b], 16)
                for b in range(2):
                    sp.wait_ge(s_dma[b], 16 * NB // 2)


def experts(c, u_tab, v_tab):
    nc = c.nc
    NE, G, B = NKEYS, 2, 4
    HALF = D // 2
    with ExitStack() as mem:
        def sb(name, shape, dt=F32):
            return mem.enter_context(nc.sbuf_tensor(name, shape, dt))

        ust = [sb(f"u{j}", [P, D]) for j in range(B)]
        vst = [sb(f"v{j}", [P, D]) for j in range(B)]
        uh = [sb(f"u_hi{j}", [P, ND, P], F32R) for j in range(2)]
        ul = [sb(f"u_lo{j}", [P, ND, P], F32R) for j in range(2)]
        vh = [sb(f"v_hi{j}", [P, D], F32R) for j in range(B)]
        vl = [sb(f"v_lo{j}", [P, D], F32R) for j in range(B)]
        gst = [sb(f"g{j}", [P, NB, G * GT_BLK]) for j in range(2)]
        gel = [sb(f"gelu{j}", [P, SEQ]) for j in range(2)]
        hid = [sb(f"hid{j}", [P, SEQ]) for j in range(2)]
        hh = [sb(f"hid_hi{j}", [P, SEQ], F32R) for j in range(B)]
        hl = [sb(f"hid_lo{j}", [P, SEQ], F32R) for j in range(B)]
        tr = [[mem.enter_context(nc.psum_tensor(f"ut{j}{k}", [P, 4, P], F32)) for k in range(2)] for j in range(2)]
        pa = [mem.enter_context(nc.psum_tensor(f"acts{j}", [P, SEQ], F32)) for j in range(2)]
        po = [mem.enter_context(nc.psum_tensor(f"outs{j}", [P, HALF], F32)) for j in range(2)]
        s_u = [c.sem(f"u_loaded{j}") for j in range(B)]
        s_vl = [c.sem(f"v_loaded{j}") for j in range(B)]
        s_g = [c.sem(f"g_loaded{j}") for j in range(2)]
        s_tr, s_uhi, s_ulo, s_act = c.sem("u_transposed"), c.sem("u_high"), c.sem("u_low"), c.sem("acts_made")
        s_gelu, s_hid, s_hh, s_hl = c.sem("gelu_done"), c.sem("hid_made"), c.sem("hid_high"), c.sem("hid_low")
        s_vh, s_vlo, s_out, s_acc = c.sem("v_high"), c.sem("v_low"), c.sem("outs_made"), c.sem("outs_added")
        outs = [(t, h) for t in range(NT) for h in range(2)]
        NO = len(outs)
        T = NE // B

        def turns(eng, body):
            body(0, True, False)
            with eng.Fori(1, T - 1) as i:
                body(i, False, False)
            body(T - 1, False, True)

        with nc.Block() as block:

            @block.sync
            def _(sp):
                def loads(i, first, last):
                    for j in range(B):
                        n = i * B + j
                        if not first:
                            sp.wait_ge(s_tr, i * B + (j - 3))
                        sp.dma_start(ust[j][:], u_tab[bass.ds(n * P, P), :]).then_inc(s_u[j], 16)
                        if j % G == 0:
                            if not first:
                                sp.wait_ge(s_hid, i * B + (j - 2))
                            sp.dma_start(gst[j // G][:], c.gates[:, :, bass.ds(n, G), :].rearrange(
                                "b p i t -> p b (i t)")).then_inc(s_g[j // G], 16)
                        if not first:
                            sp.wait_ge(s_vlo, i * B + (j - 3))
                        sp.dma_start(vst[j][:], v_tab[bass.ds(n * P, P), :]).then_inc(s_vl[j], 16)
                turns(sp, loads)

            @block.tensor
            def _(pe):
                def flip(n, i, j, first):
                    pe.wait_ge(s_u[j % B], 16 * i + (16 if j < B else 32))
                    if not (first and j < 2):
                        pe.wait_ge(s_ulo, i * B + (j - 1))
                    for k in range(2):
                        for d in range(4):
                            last = nc.tensor.transpose(tr[j % 2][k][:, d, :], ust[j % B][:, (4 * k + d) * P:(4 * k + d + 1) * P],
                                                       c.ident[:])
                    last.then_inc(s_tr, 1)

                def acts(i, j, first):
                    pe.wait_ge(s_ulo, i * B + (j + 1))
                    if not (first and j < 2):
                        pe.wait_ge(s_gelu, i * B + (j - 1))
                    for d in range(ND):
                        last = three_pass(nc, pa[j % 2][:], uh[j % 2][:, d, :], ul[j % 2][:, d, :], c.XH[:, d, :],
                                          c.XL[:, d, :], d == 0, d == ND - 1)
                    last.then_inc(s_act, 1)

                def values(i, g, first):
                    pe.wait_ge(s_vlo, i * B + (G * g + G))
                    pe.wait_ge(s_hl, i * B + (G * g + G))
                    for o, (t, h) in enumerate(outs):
                        if not (first and g == 0 and o < 2):
                            pe.wait_ge(s_acc, i * (2 * NO) + (g * NO + o - 1))
                        for k in range(G):
                            j = (G * g + k) % B
                            a, v = slice(t * P, (t + 1) * P), slice(h * HALF, (h + 1) * HALF)
                            last = three_pass(nc, po[o % 2][:], hh[j][:, a], hl[j][:, a], vh[j][:, v], vl[j][:, v],
                                              k == 0, k == G - 1)
                        last.then_inc(s_out, 1)

                def turn(i, first, last):
                    if first:
                        flip(0, 0, 0, True)
                    for j in range(B):
                        if not (last and j == B - 1):
                            flip(None, i, j + 1, first)
                        acts(i, j, first)
                        if j % G == G - 1 and not (first and j < G):
                            values(i, j // G - 1, first)
                    if last:
                        values(i, 1, first)
                turns(pe, turn)

            @block.scalar
            def _(act):
                def u_high(i, j, first):
                    act.wait_ge(s_tr, i * B + (j + 1))
                    if not (first and j < 2):
                        act.wait_ge(s_act, i * B + (j - 1))
                    for k in range(2):
                        nc.scalar.activation(uh[j % 2][:, 4 * k:4 * k + 4, :], tr[j % 2][k][:], ACT.Copy).then_inc(s_uhi, 1)

                def turn(i, first, last):
                    if first:
                        u_high(0, 0, True)
                    for j in range(B):
                        if not (last and j == B - 1):
                            u_high(i, j + 1, first)
                        act.wait_ge(s_vl[j], 16 * i + 16)
                        if not first:
                            act.wait_ge(s_out, i * (2 * NO) + (j // G - 1) * NO)
                        nc.scalar.activation(vh[j][:], vst[j][:], ACT.Copy).then_inc(s_vh, 1)
                        act.wait_ge(s_act, i * B + (j + 1))
                        if not (first and j < 2):
                            act.wait_ge(s_hid, i * B + (j - 1))
                        nc.scalar.activation(gel[j % 2][:], pa[j % 2][:], ACT.Gelu).then_inc(s_gelu, 1)
                        act.wait_ge(s_hid, i * B + (j + 1))
                        nc.scalar.activation(hh[j][:], hid[j % 2][:], ACT.Copy).then_inc(s_hh, 1)
                turns(act, turn)

            @block.vector
            def _(dve):
                def u_low(i, j, first):
                    for k in range(2):
                        dve.wait_ge(s_uhi, i * (2 * B) + (2 * j + k + 1))
                        d = slice(4 * k, 4 * k + 4)
                        last = nc.vector.tensor_tensor(ul[j % 2][:, d, :], tr[j % 2][k][:], uh[j % 2][:, d, :].bitcast(F32),
                                                       ALU.subtract)
                    last.then_inc(s_ulo, 1)

                def add(i, g):
                    for o, (t, h) in enumerate(outs):
                        dve.wait_ge(s_out, i * (2 * NO) + (g * NO + o + 1))
                        H = c.H[:, t, h * HALF:(h + 1) * HALF]
                        nc.vector.tensor_tensor(H, H, po[o % 2][:], ALU.add).then_inc(s_acc, 1)

                def turn(i, first, last):
                    if first:
                        u_low(0, 0, True)
                    for j in range(B):
                        if not (last and j == B - 1):
                            u_low(i, j + 1, first)
                        dve.wait_ge(s_vh, i * B + (j + 1))
                        nc.vector.tensor_tensor(vl[j][:], vst[j][:], vh[j][:].bitcast(F32), ALU.subtract).then_inc(s_vlo, 1)
                        if j % G == 0:
                            dve.wait_ge(s_g[j // G], 16 * i + 16)
                        dve.wait_ge(s_gelu, i * B + (j + 1))
                        if not (first and j < 2):
                            dve.wait_ge(s_hl, i * B + (j - 1))
                        nc.vector.tensor_tensor(
                            hid[j % 2][:].rearrange("p (b t) -> p b t", b=NB), gel[j % 2][:].rearrange("p (b t) -> p b t", b=NB),
                            gst[j // G][:, :, (j % G) * GT_BLK:(j % G + 1) * GT_BLK], ALU.mult).then_inc(s_hid, 1)
                        dve.wait_ge(s_hh, i * B + (j + 1))
                        nc.vector.tensor_tensor(hl[j][:], hid[j % 2][:], hh[j][:].bitcast(F32), ALU.subtract).then_inc(s_hl, 1)
                        if j % G == G - 1 and not (first and j < G):
                            add(i, j // G - 1)
                    if last:
                        add(i, 1)
                turns(dve, turn)


def load_tokens(c, tag, dst, src):
    nc = c.nc
    s = c.sem(f"loaded_{tag}")
    with nc.Block() as block:

        @block.sync
        def _(sp):
            sp.dma_start(dst, src).then_inc(s, 16)
            sp.wait_ge(s, 16)


def gated(c, z, r):
    nc = c.nc
    s_s = c.sem("sigmoids")
    with nc.Block() as block:

        @block.scalar
        def _(act):
            for d in range(ND):
                nc.scalar.activation(z[:, d * SEQ:(d + 1) * SEQ], z[:, d * SEQ:(d + 1) * SEQ], ACT.Sigmoid).then_inc(s_s, 1)

        @block.vector
        def _(dve):
            for d in range(ND):
                dve.wait_ge(s_s, d + 1)
                a = slice(d * SEQ, (d + 1) * SEQ)
                nc.vector.tensor_tensor(z[:, a], z[:, a], r[:, a], ALU.mult)


def finish(c, gain, out):
    nc = c.nc
    s_m, s_o = c.sem("final_scaled"), c.sem("final_out")
    with nc.Block() as block:

        @block.vector
        def _(dve):
            for t in range(NT):
                nc.vector.tensor_tensor(c.XN[:, t, :], c.XN[:, t, :], gain[:], ALU.mult).then_inc(s_m, 1)

        @block.sync
        def _(sp):
            for t in range(NT):
                sp.wait_ge(s_m, t + 1)
                sp.dma_start(out[0, t * P:(t + 1) * P, :], c.XN[:, t, :]).then_inc(s_o, 16)
            sp.wait_ge(s_o, 16 * NT)


def build(nc, ins, out):
    with ExitStack() as ctx:
        c = Chip(nc, ctx)
        c.H = c.keep("H", [P, NT, D], F32)
        c.XH = c.keep("XH", [P, ND, SEQ], F32R)
        c.XL = c.keep("XL", [P, ND, SEQ], F32R)
        c.ident = c.keep("ident", [P, P], F32)
        c.eps = c.keep("eps", [P, 1], F32)
        g_mix = c.keep("g_mix", [P, ND], F32)
        g_ffn = c.keep("g_ffn", [P, ND], F32)
        g_ple = c.keep("g_ple", [P, ND], F32)

        small = [(g_mix[:], ins["norm_mix"][0].rearrange("(k p) -> p k", p=P)),
                 (g_ffn[:], ins["norm_ffn"][0].rearrange("(k p) -> p k", p=P)),
                 (g_ple[:], ins["norm_ple"][0].rearrange("(k p) -> p k", p=P))]
        with nc.allow_non_contiguous_dma(reason="three gains of 4 KiB, once"):
            constants_and_load(c, ins["x"], small)
        s_eps = c.sem("eps_set")
        with nc.Block() as block:
            @block.vector
            def _(dve):
                nc.vector.memset(c.eps[:], EPS).then_inc(s_eps, 1)

        w_in = ins["w_in"][0].rearrange("(k p) n -> p k n", p=P)
        with ExitStack() as mem:
            c.PROJ = mem.enter_context(nc.sbuf_tensor("PROJ", [P, NU_IN * SEQ], F32))
            c.GLR = mem.enter_context(nc.sbuf_tensor("GLR", [RANK, SEQ], F32))
            with ExitStack() as m2:
                c.XN = m2.enter_context(nc.sbuf_tensor("XN", [P, NT, D], F32))
                normalize(c, "mix")
                feature_major(c, "mix", c.XN, gain=g_mix)

            def keep_tile(base):
                def store(dve, ps, u, n, sem):
                    nc.vector.tensor_scalar(c.PROJ[:, bass.ds(u * SEQ + base * SEQ, SEQ)], ps[:], 1.0, None,
                                            ALU.mult).then_inc(sem, 1)
                return store

            def keep_rank(dve, ps, u, n, sem):
                nc.vector.tensor_copy(c.GLR[:], ps[0:RANK, :]).then_inc(sem, 1)
            project(c, "in", [
                (1, lambda u: w_in[:, :, GLR_COL:GLR_COL + RANK], ND, RANK, keep_rank),
                (8, lambda u: w_in[:, :, bass.ds(u * P, P)], ND, P, keep_tile(0)),
                (16, lambda u: w_in[:, :, bass.ds(u * P + (GLR_COL + RANK), P)], ND, P, keep_tile(8)),
            ])
            c.TOK = mem.enter_context(nc.sbuf_tensor("TOK", [P, NT, 1536], F32))
            c.MIX = mem.enter_context(nc.sbuf_tensor("MIX", [P, NT, D], F32))
            c.BIAS = mem.enter_context(nc.sbuf_tensor("BIAS", [P, ATT_HEADS, 2 * P], F32))
            relative_bias(c, ins["rel_bias"])
            tokens_as_rows(c)
            gla(c, ins)
            band_attention(c)
            feature_major(c, "att", c.MIX)

        def keep_in(dst):
            def store(dve, ps, u, n, sem):
                nc.vector.tensor_scalar(dst[:, bass.ds(u * SEQ, SEQ)], ps[:], 1.0, None, ALU.mult).then_inc(sem, 1)
            return store

        def columns(w, k):
            w = w.rearrange("(k p) n -> p k n", p=P)
            return lambda u: w[:, :, bass.ds(u * P, P)]

        with ExitStack() as mem:
            rows = mem.enter_context(nc.sbuf_tensor("out_proj", [P, ND * SEQ], F32))
            project(c, "out", [(ND, columns(ins["w_out"][0], ND), ND, P, keep_in(rows))])
            add_rows(c, "out", rows)
        with ExitStack() as mem:
            c.XN = mem.enter_context(nc.sbuf_tensor("XN2", [P, NT, D], F32))
            normalize(c, "ffn")
            feature_major(c, "ffn", c.XN, gain=g_ffn)
        with ExitStack() as mem:
            c.SC = mem.enter_context(nc.sbuf_tensor("scores", [P, NT, 2 * PH, NKEYS], F32))
            with ExitStack() as m2:
                c.QH = m2.enter_context(nc.sbuf_tensor("queries_hi", [P, 2 * PH * SEQ], F32R))
                c.QL = m2.enter_context(nc.sbuf_tensor("queries_lo", [P, 2 * PH * SEQ], F32R))
                s_qh = c.sem("query_high")

                def split_query(dve, ps, u, n, sem):
                    a = bass.ds(u * SEQ, SEQ)
                    nc.vector.tensor_scalar(c.QH[:, a], ps[:], 1.0, None, ALU.mult).then_inc(s_qh, 1)
                    dve.wait_ge(s_qh, n + 1)
                    nc.vector.tensor_tensor(c.QL[:, a], ps[:], c.QH[:, a].bitcast(F32), ALU.subtract).then_inc(sem, 1)
                project(c, "query", [(2 * PH, columns(ins["peer_wq"][0], ND), ND, P, split_query)])
                key_scores(c, ins["peer_subkeys"][0])
            c.I1T = mem.enter_context(nc.sbuf_tensor("I1T", [P, SEQ], F32))
            c.I2T = mem.enter_context(nc.sbuf_tensor("I2T", [P, SEQ], F32))
            c.GT = mem.enter_context(nc.sbuf_tensor("GT", [P, SEQ], F32))
            select_experts(c)
            c.gates = nc.dram_tensor("gates", (NB, NKEYS, NKEYS, GT_BLK), F32, kind="Internal").ap()
            dense_gates(c)
        experts(c, ins["peer_u"][0], ins["peer_v"][0])
        with ExitStack() as mem:
            c.XN = mem.enter_context(nc.sbuf_tensor("XN3", [P, NT, D], F32))
            z = mem.enter_context(nc.sbuf_tensor("ple_gate", [P, ND * SEQ], F32))
            r = mem.enter_context(nc.sbuf_tensor("ple_value", [P, ND * SEQ], F32))
            gain = mem.enter_context(nc.sbuf_tensor("final_gain", [P, D], F32))
            normalize(c, "ple")
            feature_major(c, "ple", c.XN, gain=g_ple)
            project(c, "gate", [(ND, columns(ins["w_ple_gate"][0], ND), ND, P, keep_in(z))])
            load_tokens(c, "p", c.XN[:, :, 0:PLE], ins["p"][0, 0].rearrange("(t p) d -> p t d", p=P))
            feature_major(c, "emb", c.XN, nd=PLE // P)
            project(c, "emb", [(ND, columns(ins["w_ple"][0], 2), PLE // P, P, keep_in(r))])
            gated(c, z, r)
            add_rows(c, "ple", z)
            load_tokens(c, "gain", gain[:], ins["final_norm"].unsqueeze(0).broadcast_to([P, D]))
            normalize(c, "final")
            finish(c, gain, out)


_INS = ["x", "p", "norm_mix", "w_in", "gla_gate_w2", "gla_gate_b", "gla_head_norm", "rel_bias", "w_out", "norm_ffn",
        "peer_wq", "peer_subkeys", "peer_u", "peer_v", "norm_ple", "w_ple_gate", "w_ple", "final_norm"]

def kernel(**inputs):
    import numpy as _np
    import concourse.bacc as _bacc
    from concourse import mybir as _mybir
    from concourse.bass_utils import run_bass_kernel_spmd as _run

    nc = _bacc.Bacc("TRN2", target_bir_lowering=False, num_devices=1)
    arrays, args = {}, {}
    for name in _INS:
        a = _np.ascontiguousarray(inputs[name])
        arrays[f"in_{name}_dram"] = a
        args[name] = nc.dram_tensor(f"in_{name}_dram", a.shape, _mybir.dt.from_np(a.dtype), kind="ExternalInput").ap()
    out = nc.dram_tensor("out_0_dram", (1, SEQ, D), _mybir.dt.float32, kind="ExternalOutput").ap()
    build(nc, args, out)
    r = _run(nc, [arrays], core_ids=[0])
    return r.results[0]["out_0_dram"]
```

```python
import concourse.bass as bass
from concourse import mybir
from contextlib import ExitStack, contextmanager

F32 = mybir.dt.float32
F32R = mybir.dt.float32r
I32 = mybir.dt.int32
U32 = mybir.dt.uint32
ALU = mybir.AluOpType
ACT = mybir.ActivationFunctionType
AX = mybir.AxisListType

P = 128
SEQ, D = 512, 1024
NT, ND = SEQ // P, D // P
CHUNK = 64
NCH = SEQ // CHUNK
GLA_HEADS, GLA_DK, GLA_DV, RANK = 4, 64, 128, 16
ATT_HEADS, ATT_DH = 8, 64
REL_CLIP = 128
NEG = -1e30
EPS = 1e-6
GATE_NORM = 16.0
PH, NKEYS, TOPK = 8, 128, 16
PLE = 256
LOWEST = -3.0e38

UQ, UK, UV, UG, UAQ, UAK, UAV = 0, 2, 4, 8, 12, 16, 20
NU_IN = 24
GLR_COL = 1024
CAND = [(a, TOPK // (a + 1)) for a in range(TOPK)]
NCAND = sum(n for _, n in CAND)


class Chip:

    def __init__(self, nc, ctx):
        self.nc, self.ctx, self.used, self.names = nc, ctx, [], []

    def sem(self, name):
        self.names.append(name)
        again = self.names.count(name)
        self.used.append(self.nc.alloc_semaphore(name if again == 1 else f"{name}_{again}"))
        return self.used[-1]

    @contextmanager
    def stage(self):
        before, self.used = self.used, []
        with ExitStack() as mem:
            yield mem
        self.nc.clear_and_free_semaphores(self.used)
        self.nc.all_engine_barrier()
        self.used = before

    def keep(self, name, shape, dt):
        return self.ctx.enter_context(self.nc.sbuf_tensor(name, shape, dt))


class Chain:

    def __init__(self, eng, sem):
        self.eng, self.sem, self.n = eng, sem, 0

    def step(self, ins):
        self.n += 1
        ins.then_inc(self.sem, 1)
        return self.n

    def wait(self, n=None):
        self.eng.wait_ge(self.sem, self.n if n is None else n)


def constants_and_load(c, x, small):
    nc = c.nc
    s_x, s_small, s_id = c.sem("x_loaded"), c.sem("small_loaded"), c.sem("ident_steps")
    with nc.Block() as block:

        @block.sync
        def _(sp):
            sp.dma_start(c.H[:], x[0].rearrange("(t p) d -> p t d", p=P)).then_inc(s_x, 16)
            for dst, src in small:
                sp.dma_start(dst, src).then_inc(s_small, 16)
            sp.wait_ge(s_x, 16)
            sp.wait_ge(s_small, 16 * len(small))

        @block.gpsimd
        def _(pool):
            nc.gpsimd.memset(c.ident[:], 0.0).then_inc(s_id, 1)
            pool.wait_ge(s_id, 1)
            nc.gpsimd.affine_select(out=c.ident[:], in_=c.ident[:], compare_op=ALU.not_equal, fill=1.0, base=0,
                                    pattern=[[-1, P]], channel_multiplier=1).then_inc(s_id, 1)


def normalize(c, tag):
    nc = c.nc
    with c.stage() as mem:
        rms = mem.enter_context(nc.sbuf_tensor(f"rms_{tag}", [P, NT], F32))
        ssq = mem.enter_context(nc.sbuf_tensor(f"ssq_{tag}", [P, NT], F32))
        rstd = mem.enter_context(nc.sbuf_tensor(f"rstd_{tag}", [P, NT], F32))
        s_ssq, s_rms, s_rstd = c.sem(f"ssq_{tag}"), c.sem(f"rms_{tag}"), c.sem(f"rstd_{tag}")
        with nc.Block() as block:

            @block.scalar
            def _(act):
                for t in range(NT):
                    nc.scalar.activation(c.XN[:, t, :], c.H[:, t, :], ACT.Square,
                                         accum_out=ssq[:, t:t + 1]).then_inc(s_ssq, 1)
                act.wait_ge(s_ssq, NT)
                nc.scalar.activation(rms[:], ssq[:], ACT.Sqrt, scale=1.0 / D, bias=c.eps[:]).then_inc(s_rms, 1)
                act.wait_ge(s_rstd, 1)
                for t in range(NT):
                    nc.scalar.activation(c.XN[:, t, :], c.H[:, t, :], ACT.Copy, scale=rstd[:, t:t + 1])

            @block.vector
            def _(dve):
                dve.wait_ge(s_rms, 1)
                nc.vector.reciprocal(rstd[:], rms[:]).then_inc(s_rstd, 1)


def feature_major(c, tag, src, nd=ND, gain=None):
    nc = c.nc
    with c.stage() as mem:
        ps = [mem.enter_context(nc.psum_tensor(f"nt_{tag}{i}", [P, NT, P], F32)) for i in range(4)]
        s_tr, s_hi, s_lo = c.sem(f"tr_{tag}"), c.sem(f"hi_{tag}"), c.sem(f"lo_{tag}")
        with nc.Block() as block:

            @block.tensor
            def _(pe):
                for d in range(nd):
                    if d >= 4:
                        pe.wait_ge(s_lo, d - 3)
                    for t in range(NT):
                        last = nc.tensor.transpose(ps[d % 4][:, t, :], src[:, t, d * P:(d + 1) * P], c.ident[:])
                    last.then_inc(s_tr, 1)

            @block.scalar
            def _(act):
                for d in range(nd):
                    act.wait_ge(s_tr, d + 1)
                    nc.scalar.activation(c.XH[:, d, :], ps[d % 4][:], ACT.Copy,
                                         scale=1.0 if gain is None else gain[:, d:d + 1]).then_inc(s_hi, 1)

            @block.vector
            def _(dve):
                for d in range(nd):
                    dve.wait_ge(s_hi, d + 1)
                    high = c.XH[:, d, :].bitcast(F32)
                    if gain is None:
                        nc.vector.tensor_tensor(c.XL[:, d, :], ps[d % 4][:], high, ALU.subtract).then_inc(s_lo, 1)
                    else:
                        nc.vector.scalar_tensor_tensor(out=c.XL[:, d, :], in0=ps[d % 4][:], scalar=gain[:, d:d + 1],
                                                       in1=high, op0=ALU.mult, op1=ALU.subtract).then_inc(s_lo, 1)


def add_rows(c, tag, src):
    nc = c.nc
    with c.stage() as mem:
        ps = [mem.enter_context(nc.psum_tensor(f"ar_{tag}{i}", [P, NT, P], F32)) for i in range(4)]
        s_tr, s_add = c.sem(f"ar_tr_{tag}"), c.sem(f"ar_add_{tag}")
        with nc.Block() as block:

            @block.tensor
            def _(pe):
                for d in range(ND):
                    if d >= 4:
                        pe.wait_ge(s_add, d - 3)
                    for t in range(NT):
                        last = nc.tensor.transpose(ps[d % 4][:, t, :], src[:, d * SEQ + t * P:d * SEQ + (t + 1) * P],
                                                   c.ident[:])
                    last.then_inc(s_tr, 1)

            @block.vector
            def _(dve):
                for d in range(ND):
                    dve.wait_ge(s_tr, d + 1)
                    h = c.H[:, :, d * P:(d + 1) * P]
                    nc.vector.tensor_tensor(h, h, ps[d % 4][:], ALU.add).then_inc(s_add, 1)


def three_pass(nc, out, ah, al, bh, bl, first, final, skip=False):
    nc.tensor.matmul(out, ah, bh, start=first, stop=False, skip_group_check=skip)
    nc.tensor.matmul(out, ah, bl, start=False, stop=False, skip_group_check=skip)
    return nc.tensor.matmul(out, al, bh, start=False, stop=final, skip_group_check=skip)


def project(c, tag, jobs):
    nc = c.nc
    S = 4
    with c.stage() as mem:
        stage = [mem.enter_context(nc.sbuf_tensor(f"wst_{tag}{i}", [P, ND, P], F32)) for i in range(S)]
        wh = [mem.enter_context(nc.sbuf_tensor(f"wh_{tag}{i}", [P, ND, P], F32R)) for i in range(2)]
        wl = [mem.enter_context(nc.sbuf_tensor(f"wl_{tag}{i}", [P, ND, P], F32R)) for i in range(2)]
        ps = [mem.enter_context(nc.psum_tensor(f"pp_{tag}{i}", [P, SEQ], F32)) for i in range(2)]
        s_w = [c.sem(f"w_{tag}{i}") for i in range(S)]
        s_hi, s_lo, s_pe, s_out = c.sem(f"whi_{tag}"), c.sem(f"wlo_{tag}"), c.sem(f"prod_{tag}"), c.sem(f"stored_{tag}")

        def turns(eng, body):
            base = 0
            for job in jobs:
                count, u = job[0], 0
                while u < count and (count < 2 * S or base + u < S or u < S):
                    body(u, base + u, (base + u) % S, (base + u) // S + 1, job)
                    u += 1
                if u < count:
                    assert (count - u) % S == 0
                    with eng.Fori(0, (count - u) // S) as i:
                        for j in range(S):
                            n = base + u + j
                            body(i * S + (u + j), i * S + n, n % S, i + (n // S + 1), job)
                base += count

        def early(n, k):
            return isinstance(n, int) and n < k

        with nc.Block() as block:

            @block.sync
            def _(sp):
                def load(u, n, r, fills, job):
                    if not early(n, S):
                        sp.wait_ge(s_lo, n - (S - 1))
                    sp.dma_start(stage[r][:, 0:job[2], 0:job[3]], job[1](u)).then_inc(s_w[r], 16)
                turns(sp, load)

            @block.scalar
            def _(act):
                def high(u, n, r, fills, job):
                    act.wait_ge(s_w[r], fills * 16)
                    if not early(n, 2):
                        act.wait_ge(s_pe, n - 1)
                    nc.scalar.activation(wh[r % 2][:, 0:job[2], 0:job[3]], stage[r][:, 0:job[2], 0:job[3]],
                                         ACT.Copy).then_inc(s_hi, 1)
                turns(act, high)

            @block.gpsimd
            def _(pool):
                def low(u, n, r, fills, job):
                    pool.wait_ge(s_hi, n + 1)
                    nc.gpsimd.tensor_tensor(wl[r % 2][:, 0:job[2], 0:job[3]], stage[r][:, 0:job[2], 0:job[3]],
                                            wh[r % 2][:, 0:job[2], 0:job[3]].bitcast(F32),
                                            ALU.subtract).then_inc(s_lo, 1)
                turns(pool, low)

            @block.vector
            def _(dve):
                def keep(u, n, r, fills, job):
                    dve.wait_ge(s_pe, n + 1)
                    job[4](dve, ps[r % 2], u, n, s_out)
                turns(dve, keep)

            @block.tensor
            def _(pe):
                def product(u, n, r, fills, job):
                    pe.wait_ge(s_lo, n + 1)
                    if not early(n, 2):
                        pe.wait_ge(s_out, n - 1)
                    k, cols = job[2], job[3]
                    for d in range(k):
                        last = three_pass(nc, ps[r % 2][0:cols, :], wh[r % 2][:, d, 0:cols], wl[r % 2][:, d, 0:cols],
                                          c.XH[:, d, :], c.XL[:, d, :], d == 0, d == k - 1)
                    last.then_inc(s_pe, 1)
                turns(pe, product)


def relative_bias(c, rel_bias):
    nc = c.nc
    W = 3 * P
    rows = nc.dram_tensor("rev_tables", (P, ATT_HEADS, W), F32, kind="Internal").ap()
    with c.stage() as mem:
        table = mem.enter_context(nc.sbuf_tensor("rel_table", [P, ATT_HEADS, 2 * REL_CLIP + 1], F32))
        rev = mem.enter_context(nc.sbuf_tensor("rev", [P, ATT_HEADS, W], F32))
        s_t, s_rev, s_out, s_in = c.sem("table_loaded"), c.sem("table_reversed"), c.sem("table_stored"), c.sem("bias_loaded")
        with nc.Block() as block:

            @block.sync
            def _(sp):
                sp.dma_start(table[:], rel_bias.broadcast_to([P, ATT_HEADS, 2 * REL_CLIP + 1])).then_inc(s_t, 16)
                sp.wait_ge(s_rev, 3)
                sp.dma_start(rows, rev[:]).then_inc(s_out, 16)
                sp.wait_ge(s_out, 16)
                src = bass.AP(tensor=rows.tensor, offset=P - 1, ap=[[ATT_HEADS * W - 1, P], [W, ATT_HEADS], [1, 2 * P]])
                sp.dma_start(c.BIAS[:], src).then_inc(s_in, 16)
                sp.wait_ge(s_in, 16)

            @block.vector
            def _(dve):
                dve.wait_ge(s_t, 16)
                nc.vector.tensor_copy(rev[:, :, P - 1:W - 1], table[:, :, 2 * REL_CLIP:0:-1]).then_inc(s_rev, 1)
                nc.vector.tensor_copy(rev[:, :, 0:P - 1], table[:, :, 2 * REL_CLIP:2 * REL_CLIP + 1]
                                      .broadcast_to([P, ATT_HEADS, P - 1])).then_inc(s_rev, 1)
                nc.vector.tensor_copy(rev[:, :, W - 1:W], table[:, :, 0:1]).then_inc(s_rev, 1)

            @block.gpsimd
            def _(pool):
                pool.wait_ge(s_in, 16)
                nc.gpsimd.memset(c.BIAS[0:CHUNK, :, P + CHUNK:2 * P], NEG)


def tokens_as_rows(c):
    nc = c.nc
    units = [UV + i for i in range(4)] + [UG + i for i in range(4)] + [UAV + i for i in range(4)]
    with c.stage() as mem:
        ps = [mem.enter_context(nc.psum_tensor(f"tok{i}", [P, NT, P], F32)) for i in range(4)]
        s_tr, s_act, s_dve = c.sem("tok_transposed"), c.sem("tok_stored_act"), c.sem("tok_stored_dve")
        with nc.Block() as block:

            @block.tensor
            def _(pe):
                for j, u in enumerate(units):
                    if j >= 4:
                        pe.wait_ge(s_dve if j % 2 else s_act, (j - 4) // 2 + 1)
                    for t in range(NT):
                        last = nc.tensor.transpose(ps[j % 4][:, t, :], c.PROJ[:, u * SEQ + t * P:u * SEQ + (t + 1) * P],
                                                   c.ident[:])
                    last.then_inc(s_tr, 1)

            @block.scalar
            def _(act):
                for j in range(0, 12, 2):
                    act.wait_ge(s_tr, j + 1)
                    nc.scalar.activation(c.TOK[:, :, j * P:(j + 1) * P], ps[j % 4][:], ACT.Copy).then_inc(s_act, 1)

            @block.vector
            def _(dve):
                for j in range(1, 12, 2):
                    dve.wait_ge(s_tr, j + 1)
                    nc.vector.tensor_copy(c.TOK[:, :, j * P:(j + 1) * P], ps[j % 4][:]).then_inc(s_dve, 1)


def gla(c, ins):
    nc = c.nc
    NP = GLA_HEADS // 2
    with c.stage() as mem:
        def sb(name, shape, dt=F32):
            return mem.enter_context(nc.sbuf_tensor(name, shape, dt))

        w2 = sb("gate_w2", [RANK, GLA_HEADS * GLA_DK])
        b = sb("gate_b", [P, NP])
        hn = sb("head_norm", [P, GLA_DV])
        starts = sb("chunk_starts", [P, SEQ])
        one = sb("one", [P, 1])
        q1 = sb("q1", [P, NP, SEQ])
        k1 = sb("k1", [P, NP, SEQ])
        q2 = sb("q2", [P, NP, SEQ])
        k4 = sb("k4", [P, NP, SEQ])
        cum = sb("cum", [P, NP, SEQ])
        dm = sb("dm", [P, NP, SEQ])
        decay = sb("decay", [P, NP, NCH])
        KS = sb("KS", [P, NP, NT, P])
        AT = sb("AT", [P, GLA_HEADS, NT, P])
        SS = sb("states", [P, NP, NCH, 2 * GLA_DV])
        maskf = sb("maskf", [P, P])
        mask = sb("mask", [P, P], I32)
        ssq = sb("gla_ssq", [P, NT * GLA_HEADS])
        rms = sb("gla_rms", [P, NT * GLA_HEADS])
        rstd = sb("gla_rstd", [P, NT * GLA_HEADS])
        bank = [mem.enter_context(nc.psum_tensor(f"gb{i}", [P, SEQ], F32)) for i in range(8)]
        s_in, s_set = c.sem("gla_loaded"), c.sem("gla_consts")
        s_z, s_zmin, s_ln, s_d = c.sem("gla_z"), c.sem("gla_zmin"), c.sem("gla_ln"), c.sem("gla_diffs")
        s_e, s_a, s_v = c.sem("gla_exps"), c.sem("gla_act"), c.sem("gla_dve")
        s_qk, s_k4 = c.sem("gla_qk"), c.sem("gla_k4")
        s_ks, s_kss, s_at, s_ats = c.sem("gla_kst"), c.sem("gla_ks"), c.sem("gla_scores"), c.sem("gla_masked")
        s_kv, s_s, s_o, s_sq, s_sr, s_silu = c.sem("gla_kv"), c.sem("gla_state"), c.sem("gla_o"), c.sem("gla_sq"), \
            c.sem("gla_rms"), c.sem("gla_silu")
        s_ss, s_m = c.sem("gla_ssq"), c.sem("gla_out")

        def chunks(x):
            return x.rearrange("p (n c) -> p n c", c=CHUNK)

        with nc.Block() as block:

            @block.sync
            def _(sp):
                sp.dma_start(w2[:], ins["gla_gate_w2"][0]).then_inc(s_in, 16)
                with nc.allow_non_contiguous_dma(reason="1 KiB of gate bias, once"):
                    sp.dma_start(b[:], ins["gla_gate_b"][0].rearrange("(m p) -> p m", p=P)).then_inc(s_in, 16)
                sp.dma_start(hn[:], ins["gla_head_norm"].broadcast_to([P, GLA_DV])).then_inc(s_in, 16)

            @block.gpsimd
            def _(pool):
                nc.gpsimd.memset(starts[:], 1.0).then_inc(s_set, 1)
                nc.gpsimd.memset(one[:], 1.0).then_inc(s_set, 1)
                nc.gpsimd.memset(maskf[:], 1.0).then_inc(s_set, 1)
                nc.gpsimd.memset(AT[:], 0.0).then_inc(s_set, 1)
                for m in range(NP):
                    nc.gpsimd.memset(SS[:, m, 0, :], 0.0).then_inc(s_set, 1)
                pool.wait_ge(s_set, 4 + NP)
                nc.gpsimd.memset(chunks(starts[:])[:, :, 0:1], 0.0).then_inc(s_set, 1)
                nc.gpsimd.affine_select(out=maskf[:], in_=maskf[:], compare_op=ALU.is_ge, fill=0.0, base=0,
                                        pattern=[[1, P]], channel_multiplier=-1).then_inc(s_set, 1)
                pool.wait_ge(s_set, 6 + NP)
                nc.gpsimd.memset(maskf[0:CHUNK, CHUNK:P], 0.0).then_inc(s_set, 1)

            ALL_SET = 7 + NP

            @block.tensor
            def _(pe):
                pe.wait_ge(s_in, 48)
                for m in range(NP):
                    nc.tensor.matmul(bank[4 + m][:], w2[:, m * P:(m + 1) * P], c.GLR[:], start=True,
                                     stop=True).then_inc(s_z, 1)
                pe.wait_ge(s_qk, 2 * NP)
                for h in range(GLA_HEADS):
                    m, r = h // 2, GLA_DK * (h % 2)
                    for t in range(NT):
                        last = nc.tensor.matmul(bank[h][:, t * P:(t + 1) * P], k1[r:r + GLA_DK, m, t * P:(t + 1) * P],
                                                q1[r:r + GLA_DK, m, t * P:(t + 1) * P], start=True, stop=True)
                    last.then_inc(s_at, 1)
                for m in range(NP):
                    pe.wait_ge(s_k4, m + 1)
                    for t in range(NT):
                        last = nc.tensor.transpose(bank[6 + m][:, t * P:(t + 1) * P], k4[:, m, t * P:(t + 1) * P],
                                                   c.ident[:])
                    last.then_inc(s_ks, 1)
                pe.wait_ge(s_kss, NP)
                for n in range(NCH - 1):
                    for m in range(NP):
                        i = n * NP + m
                        if i >= 4:
                            pe.wait_ge(s_s, i - 3)
                        rows = slice(CHUNK * (n % 2), CHUNK * (n % 2) + CHUNK)
                        nc.tensor.matmul(bank[4 + i % 4][:, 0:2 * GLA_DV], KS[rows, m, n // 2, :],
                                         c.TOK[rows, n // 2, m * 2 * GLA_DV:(m + 1) * 2 * GLA_DV],
                                         start=True, stop=True).then_inc(s_kv, 1)
                pe.wait_ge(s_ats, GLA_HEADS)
                pe.wait_ge(s_s, NP * (NCH - 1))
                for t in range(NT):
                    for h in range(GLA_HEADS):
                        m, r = h // 2, GLA_DK * (h % 2)
                        o = bank[t + NT * (h % 2)]
                        cols = slice(m * GLA_DV, (m + 1) * GLA_DV)
                        nc.tensor.matmul(o[:, cols], AT[:, h, t, :], c.TOK[:, t, h * GLA_DV:(h + 1) * GLA_DV],
                                         start=True, stop=False, skip_group_check=True)
                        for half in range(2):
                            n = 2 * t + half
                            rows = slice(CHUNK * half, CHUNK * half + CHUNK)
                            last = nc.tensor.matmul(
                                o[rows, cols], q2[r:r + GLA_DK, m, n * CHUNK:(n + 1) * CHUNK],
                                SS[r:r + GLA_DK, m, n, (h % 2) * GLA_DV:(h % 2 + 1) * GLA_DV],
                                start=False, stop=True, skip_group_check=True)
                    last.then_inc(s_o, 1)

            @block.scalar
            def _(act):
                act.wait_ge(s_in, 48)
                ch = Chain(act, s_a)
                for m in range(NP):
                    act.wait_ge(s_z, m + 1)
                    ch.step(nc.scalar.activation(k1[:, m, :], bank[4 + m][:], ACT.Abs, bias=b[:, m:m + 1]))
                ch.wait()
                ch.step(nc.scalar.activation(k1[:], k1[:], ACT.Exp, scale=-1.0))
                ch.wait()
                act.wait_ge(s_set, ALL_SET)
                nc.scalar.activation(k1[:], k1[:], ACT.Ln, bias=one[:]).then_inc(s_ln, 1)
                act.wait_ge(s_d, 2)
                g = 1.0 / GATE_NORM
                nc.scalar.activation(q1[:], dm[:], ACT.Exp, scale=g).then_inc(s_e, 1)
                nc.scalar.activation(k1[:], dm[:], ACT.Exp, scale=-g).then_inc(s_e, 1)
                nc.scalar.activation(q2[:], cum[:], ACT.Exp, scale=g).then_inc(s_e, 1)
                act.wait_ge(s_d, 4)
                nc.scalar.activation(k4[:], k4[:], ACT.Exp, scale=g).then_inc(s_e, 1)
                for m in range(NP):
                    ch.step(nc.scalar.activation(decay[:, m, :], chunks(cum[:, m, :])[:, :, CHUNK - 1], ACT.Exp, scale=g))
                gates = c.TOK[:, :, GLA_HEADS * GLA_DV:2 * GLA_HEADS * GLA_DV]
                nc.scalar.activation(gates, gates, ACT.Silu).then_inc(s_silu, 1)
                for t in range(NT):
                    act.wait_ge(s_o, t + 1)
                    if t == 0:
                        act.wait_ge(s_o, NT)
                    for s in range(2):
                        nc.scalar.activation(AT[:, t, s::2, :], bank[t + NT * s][:, 0:NP * GLA_DV].rearrange(
                            "p (h e) -> p h e", e=P), ACT.Square).then_inc(s_sq, 1)
                act.wait_ge(s_ss, NT)
                nc.scalar.activation(rms[:], ssq[:], ACT.Sqrt, scale=1.0 / GLA_DV, bias=c.eps[:]).then_inc(s_sr, 1)

            @block.vector
            def _(dve):
                ch = Chain(dve, s_v)
                dve.wait_ge(s_in, 48)
                for m in range(NP):
                    dve.wait_ge(s_a, m + 1)
                    ch.step(nc.vector.tensor_scalar(q1[:, m, :], bank[4 + m][:], b[:, m:m + 1], 0.0, ALU.add, ALU.min))
                dve.wait_ge(s_set, ALL_SET)
                ch.step(nc.vector.tensor_copy(mask[:], maskf[:]))
                dve.wait_ge(s_ln, 1)
                ch.wait()
                for m in range(NP):
                    ch.step(nc.vector.tensor_tensor(q1[:, m, :], q1[:, m, :], k1[:, m, :], ALU.subtract))
                ch.wait()
                for m in range(NP):
                    ch.step(nc.vector.tensor_tensor_scan(cum[:, m, :], starts[:], q1[:, m, :], 0.0, ALU.mult, ALU.add))
                ch.wait()
                for m in range(NP):
                    x = chunks(cum[:, m, :])
                    nc.vector.tensor_tensor(chunks(dm[:, m, :]), x, x[:, :, CHUNK // 2:CHUNK // 2 + 1]
                                            .broadcast_to([P, NCH, CHUNK]), ALU.subtract).then_inc(s_d, 1)
                for m in range(NP):
                    x = chunks(cum[:, m, :])
                    nc.vector.tensor_tensor(chunks(k4[:, m, :]), x[:, :, CHUNK - 1:CHUNK].broadcast_to([P, NCH, CHUNK]),
                                            x, ALU.subtract).then_inc(s_d, 1)
                Q, K = [c.PROJ[:, u * SEQ:(u + NP) * SEQ].rearrange("p (m t) -> p m t", m=NP) for u in (UQ, UK)]
                scale = GLA_DK ** -0.5
                dve.wait_ge(s_e, 2)
                for m in range(NP):
                    nc.vector.scalar_tensor_tensor(out=q1[:, m, :], in0=Q[:, m, :], scalar=scale, in1=q1[:, m, :],
                                                   op0=ALU.mult, op1=ALU.mult).then_inc(s_qk, 1)
                    nc.vector.tensor_tensor(k1[:, m, :], K[:, m, :], k1[:, m, :], ALU.mult).then_inc(s_qk, 1)
                dve.wait_ge(s_e, 4)
                for m in range(NP):
                    nc.vector.tensor_tensor(k4[:, m, :], K[:, m, :], k4[:, m, :], ALU.mult).then_inc(s_k4, 1)
                for m in range(NP):
                    ch.step(nc.vector.scalar_tensor_tensor(out=q2[:, m, :], in0=Q[:, m, :], scalar=scale,
                                                           in1=q2[:, m, :], op0=ALU.mult, op1=ALU.mult))
                for h in range(GLA_HEADS):
                    dve.wait_ge(s_at, h + 1)
                    if h == 0:
                        ch.wait()
                    nc.vector.copy_predicated(AT[:, h, :, :], mask[:].unsqueeze(1).broadcast_to([P, NT, P]),
                                              bank[h][:].rearrange("p (t i) -> p t i", t=NT)).then_inc(s_ats, 1)
                for m in range(NP):
                    dve.wait_ge(s_ks, m + 1)
                    nc.vector.tensor_copy(KS[:, m, :, :], bank[6 + m][:].rearrange("p (t i) -> p t i", t=NT)).then_inc(s_kss, 1)
                dve.wait_ge(s_a, NP + 1 + NP)
                for n in range(NCH - 1):
                    for m in range(NP):
                        i = n * NP + m
                        dve.wait_ge(s_kv, i + 1)
                        if n:
                            dve.wait_ge(s_s, i - 1)
                        nc.vector.scalar_tensor_tensor(
                            out=SS[:, m, n + 1, :], in0=SS[:, m, n, :], scalar=decay[:, m, n:n + 1],
                            in1=bank[4 + i % 4][:, 0:2 * GLA_DV], op0=ALU.mult, op1=ALU.add).then_inc(s_s, 1)
                for t in range(NT):
                    dve.wait_ge(s_sq, 2 * (t + 1))
                    nc.vector.tensor_reduce(ssq[:, t * GLA_HEADS:(t + 1) * GLA_HEADS], AT[:, t, :, :], AX.X,
                                            ALU.add).then_inc(s_ss, 1)
                dve.wait_ge(s_sr, 1)
                ch.step(nc.vector.reciprocal(rstd[:], rms[:]))
                ch.wait()
                dve.wait_ge(s_silu, 1)
                W = GLA_HEADS * GLA_DV
                for t in range(NT):
                    o = c.MIX[:, t, 0:W].rearrange("p (h e) -> p h e", e=GLA_DV)
                    for s in range(2):
                        ch.step(nc.vector.tensor_tensor(
                            o[:, s::2, :], bank[t + NT * s][:, 0:NP * GLA_DV].rearrange("p (h e) -> p h e", e=GLA_DV),
                            rstd[:, t * GLA_HEADS + s:(t + 1) * GLA_HEADS:2].unsqueeze(2)
                            .broadcast_to([P, NP, GLA_DV]), ALU.mult))
                ch.wait()
                for t in range(NT):
                    o = c.MIX[:, t, 0:W].rearrange("p (h e) -> p h e", e=GLA_DV)
                    ch.step(nc.vector.tensor_tensor(o, o, hn[:].unsqueeze(1).broadcast_to([P, GLA_HEADS, GLA_DV]),
                                                    ALU.mult))
                ch.wait()
                for t in range(NT):
                    nc.vector.tensor_tensor(c.MIX[:, t, 0:W], c.MIX[:, t, 0:W], c.TOK[:, t, W:2 * W],
                                            ALU.mult).then_inc(s_m, 1)


def band_attention(c):
    nc = c.nc
    steps = [(t, h) for t in range(NT) for h in range(ATT_HEADS)]
    N = len(steps)
    scale = ATT_DH ** -0.5
    V0 = 2 * GLA_HEADS * GLA_DV
    with c.stage() as mem:
        def sb(name, shape, dt=F32):
            return mem.enter_context(nc.sbuf_tensor(name, shape, dt))

        sc = [sb(f"att_sc{i}", [P, SEQ]) for i in range(2)]
        pr = [sb(f"att_p{i}", [P, SEQ]) for i in range(2)]
        pt = [sb(f"att_pt{i}", [P, SEQ]) for i in range(2)]
        nmax = sb("att_nmax", [P, N])
        rsum = sb("att_rsum", [P, N])
        rinv = sb("att_rinv", [P, N])
        ps_s = [mem.enter_context(nc.psum_tensor(f"as{i}", [P, SEQ], F32)) for i in range(2)]
        ps_t = [mem.enter_context(nc.psum_tensor(f"at{i}", [P, SEQ], F32)) for i in range(2)]
        ps_o = [mem.enter_context(nc.psum_tensor(f"ao{i}", [P, SEQ], F32)) for i in range(2)]
        s_qk, s_sc, s_mx, s_p, s_pt, s_pts = (c.sem("att_" + n) for n in ("qk", "biased", "max", "exp", "ptr", "pts"))
        s_pv, s_o, s_ri = (c.sem("att_" + n) for n in ("pv", "out", "rinv"))

        with nc.Block() as block:

            @block.tensor
            def _(pe):
                def scores(i):
                    t, h = steps[i]
                    r = ATT_DH * (h % 2)
                    q0 = (UAQ + h // 2) * SEQ + t * P
                    k0 = (UAK + h // 2) * SEQ
                    if i >= 2:
                        pe.wait_ge(s_sc, 2 * (i - 1))
                    nc.tensor.matmul(ps_s[i % 2][:, 0:(t + 1) * P], c.PROJ[r:r + ATT_DH, q0:q0 + P],
                                     c.PROJ[r:r + ATT_DH, k0:k0 + (t + 1) * P], start=True, stop=True).then_inc(s_qk, 1)

                def flip(i):
                    t, h = steps[i]
                    pe.wait_ge(s_p, i + 1)
                    if i >= 2:
                        pe.wait_ge(s_pts, i - 1)
                    for k in range(t + 1):
                        last = nc.tensor.transpose(ps_t[i % 2][:, k * P:(k + 1) * P], pr[i % 2][:, k * P:(k + 1) * P],
                                                   c.ident[:])
                    last.then_inc(s_pt, 1)

                def values(i):
                    t, h = steps[i]
                    pe.wait_ge(s_pts, i + 1)
                    if h == 0 and t >= 2:
                        pe.wait_ge(s_o, t - 1)
                    for k in range(t + 1):
                        last = nc.tensor.matmul(ps_o[t % 2][:, h * ATT_DH:(h + 1) * ATT_DH], pt[i % 2][:, k * P:(k + 1) * P],
                                                c.TOK[:, k, V0 + h * ATT_DH:V0 + (h + 1) * ATT_DH],
                                                start=(k == 0), stop=(k == t))
                    last.then_inc(s_pv, 1)

                for i in range(N + 2):
                    if i < N:
                        scores(i)
                    if 0 <= i - 1 < N:
                        flip(i - 1)
                    if i - 2 >= 0:
                        values(i - 2)

            @block.vector
            def _(dve):
                def biased(i):
                    t, h = steps[i]
                    dve.wait_ge(s_qk, i + 1)
                    if i >= 2:
                        dve.wait_ge(s_p, i - 1)
                    far = max(0, (t - 1) * P)
                    n = (t + 1) * P - far
                    if far:
                        nc.vector.tensor_scalar(sc[i % 2][:, 0:far], ps_s[i % 2][:, 0:far], scale, c.BIAS[:, h, 0:1],
                                                ALU.mult, ALU.add).then_inc(s_sc, 1)
                    nc.vector.scalar_tensor_tensor(
                        out=sc[i % 2][:, far:far + n], in0=ps_s[i % 2][:, far:far + n], scalar=scale,
                        in1=c.BIAS[:, h, 2 * P - n:2 * P], op0=ALU.mult, op1=ALU.add).then_inc(s_sc, 1 if far else 2)
                    dve.wait_ge(s_sc, 2 * (i + 1))
                    nc.vector.tensor_reduce(nmax[:, i:i + 1], sc[i % 2][:, 0:far + n], AX.X, ALU.max,
                                            negate=True).then_inc(s_mx, 1)

                def keep(i):
                    t, h = steps[i]
                    dve.wait_ge(s_pt, i + 1)
                    if i >= 2:
                        dve.wait_ge(s_pv, i - 1)
                    nc.vector.tensor_copy(pt[i % 2][:, 0:(t + 1) * P], ps_t[i % 2][:, 0:(t + 1) * P]).then_inc(s_pts, 1)

                def output(t):
                    a = t * ATT_HEADS
                    dve.wait_ge(s_p, a + ATT_HEADS)
                    nc.vector.reciprocal(rinv[:, a:a + ATT_HEADS], rsum[:, a:a + ATT_HEADS]).then_inc(s_ri, 1)
                    dve.wait_ge(s_ri, t + 1)
                    dve.wait_ge(s_pv, a + ATT_HEADS)
                    nc.vector.tensor_tensor(
                        c.MIX[:, t, SEQ:2 * SEQ].rearrange("p (h e) -> p h e", e=ATT_DH),
                        ps_o[t % 2][:].rearrange("p (h e) -> p h e", e=ATT_DH),
                        rinv[:, a:a + ATT_HEADS].unsqueeze(2).broadcast_to([P, ATT_HEADS, ATT_DH]),
                        ALU.mult).then_inc(s_o, 1)

                for i in range(N + 3):
                    if i < N:
                        biased(i)
                    if 0 <= i - 1 < N:
                        keep(i - 1)
                    if i - 2 >= 0 and (i - 2) % ATT_HEADS == ATT_HEADS - 1 and i - 2 < N:
                        output((i - 2) // ATT_HEADS)

            @block.scalar
            def _(act):
                for i, (t, h) in enumerate(steps):
                    act.wait_ge(s_mx, i + 1)
                    if i >= 2:
                        act.wait_ge(s_pt, i - 1)
                    nc.scalar.activation(pr[i % 2][:, 0:(t + 1) * P], sc[i % 2][:, 0:(t + 1) * P], ACT.Exp,
                                         bias=nmax[:, i:i + 1], accum_out=rsum[:, i:i + 1]).then_inc(s_p, 1)


def key_scores(c, subkeys):
    nc = c.nc
    U = 2 * PH
    with c.stage() as mem:
        keys = mem.enter_context(nc.sbuf_tensor("keys", [P, U, P], F32))
        kh = mem.enter_context(nc.sbuf_tensor("keys_hi", [P, U * P], F32R))
        kl = mem.enter_context(nc.sbuf_tensor("keys_lo", [P, U * P], F32R))
        ps = [mem.enter_context(nc.psum_tensor(f"kt{i}", [P, SEQ], F32)) for i in range(4)]
        s_k, s_tr, s_hi, s_lo = c.sem("keys_loaded"), c.sem("keys_tr"), c.sem("keys_high"), c.sem("keys_low")
        s_sc, s_st = c.sem("scores"), [c.sem("scores_even"), c.sem("scores_odd")]
        with nc.Block() as block:

            @block.sync
            def _(sp):
                sp.dma_start(keys[:], subkeys.rearrange("h s n d -> n (h s) d")).then_inc(s_k, 16)

            @block.tensor
            def _(pe):
                pe.wait_ge(s_k, 16)
                for g in range(U // 4):
                    for j in range(4):
                        last = nc.tensor.transpose(ps[g][:, j * P:(j + 1) * P], keys[:, 4 * g + j, :], c.ident[:])
                    last.then_inc(s_tr, 1)
                pe.wait_ge(s_lo, U // 4)
                for u in range(U):
                    if u >= 4:
                        pe.wait_ge(s_st[u % 2], (u - 4) // 2 + 1)
                    for t in range(NT):
                        a = slice(u * SEQ + t * P, u * SEQ + (t + 1) * P)
                        k = slice(u * P, (u + 1) * P)
                        last = three_pass(nc, ps[u % 4][:, t * P:(t + 1) * P], c.QH[:, a], c.QL[:, a], kh[:, k],
                                          kl[:, k], True, True)
                    last.then_inc(s_sc, 1)

            @block.scalar
            def _(act):
                for g in range(U // 4):
                    act.wait_ge(s_tr, g + 1)
                    nc.scalar.activation(kh[:, g * SEQ:(g + 1) * SEQ], ps[g][:], ACT.Copy).then_inc(s_hi, 1)
                for u in range(0, U, 2):
                    act.wait_ge(s_sc, u + 1)
                    nc.scalar.activation(c.SC[:, :, u, :], ps[u % 4][:].rearrange("p (t n) -> p t n", t=NT),
                                         ACT.Copy).then_inc(s_st[0], 1)

            @block.vector
            def _(dve):
                for g in range(U // 4):
                    dve.wait_ge(s_hi, g + 1)
                    nc.vector.tensor_tensor(kl[:, g * SEQ:(g + 1) * SEQ], ps[g][:],
                                            kh[:, g * SEQ:(g + 1) * SEQ].bitcast(F32), ALU.subtract).then_inc(s_lo, 1)
                for u in range(1, U, 2):
                    dve.wait_ge(s_sc, u + 1)
                    nc.vector.tensor_copy(c.SC[:, :, u, :],
                                          ps[u % 4][:].rearrange("p (t n) -> p t n", t=NT)).then_inc(s_st[1], 1)


class Ahead:

    def __init__(self, c, mem, u_tab, count):
        nc = c.nc

        def sb(name, shape, dt=F32):
            return [mem.enter_context(nc.sbuf_tensor(f"{name}{j}", shape, dt)) for j in range(2)]

        def sem(name):
            return c.ctx.enter_context(nc.semaphore(name))

        self.nc, self.c, self.u_tab, self.count = nc, c, u_tab, count
        self.ust, self.ut, self.gel = sb("au", [P, D]), sb("au_t", [P, ND, P]), sb("a_gelu", [P, SEQ])
        self.uh, self.ul = sb("au_hi", [P, ND, P], F32R), sb("au_lo", [P, ND, P], F32R)
        self.tr = [mem.enter_context(nc.psum_tensor(f"a_tr{k}", [P, 4, P], F32)) for k in range(2)]
        self.pa = [mem.enter_context(nc.psum_tensor(f"a_acts{j}", [P, SEQ], F32)) for j in range(2)]
        self.s_u, self.s_st = [sem("a_u_loaded0"), sem("a_u_loaded1")], [sem("a_put_aside0"), sem("a_put_aside1")]
        self.s_tr, self.s_hi, self.s_lo = sem("a_transposed"), sem("a_high"), sem("a_low")
        self.s_act, self.s_gelu = sem("a_acts"), sem("a_gelu")

    def load(self, sp, h, j, first=False):
        if not first:
            sp.wait_ge(self.s_tr, h * 2 + (j - 1))
        sp.dma_start(self.ust[j][:], self.u_tab[bass.ds(h * (2 * P) + j * P, P), :]).then_inc(self.s_u[j], 16)

    def flip(self, pe, h, j, first=False):
        pe.wait_ge(self.s_u[j], h * 16 + 16)
        if not (first and j == 0):
            pe.wait_ge(self.s_hi, h * 2 + j)
        for k in range(2):
            for d in range(4):
                a = (4 * k + d) * P
                last = self.nc.tensor.transpose(self.tr[k][:, d, :], self.ust[j][:, a:a + P], self.c.ident[:])
        last.then_inc(self.s_tr, 1)

    def acts(self, pe, h, j, first=False):
        pe.wait_ge(self.s_lo, h * 2 + (j + 1))
        if not first:
            pe.wait_ge(self.s_gelu, h * 2 + (j - 1))
        for d in range(ND):
            last = three_pass(self.nc, self.pa[j][:], self.uh[j][:, d, :], self.ul[j][:, d, :], self.c.XH[:, d, :],
                              self.c.XL[:, d, :], d == 0, d == ND - 1)
        last.then_inc(self.s_act, 1)

    def high(self, act, h, j, first=False):
        act.wait_ge(self.s_tr, h * 2 + (j + 1))
        if not first:
            act.wait_ge(self.s_act, h * 2 + (j - 1))
        for k in range(2):
            self.nc.scalar.activation(self.ut[j][:, 4 * k:4 * k + 4, :], self.tr[k][:], ACT.Copy)
            last = self.nc.scalar.activation(self.uh[j][:, 4 * k:4 * k + 4, :], self.tr[k][:], ACT.Copy)
        last.then_inc(self.s_hi, 1)

    def gelu(self, act, h, j, first=False):
        act.wait_ge(self.s_act, h * 2 + (j + 1))
        if not first:
            act.wait_ge(self.s_st[j], h * 16)
        self.nc.scalar.activation(self.gel[j][:], self.pa[j][:], ACT.Gelu).then_inc(self.s_gelu, 1)

    def low(self, pool, h, j):
        pool.wait_ge(self.s_hi, h * 2 + (j + 1))
        self.nc.gpsimd.tensor_tensor(self.ul[j][:], self.ut[j][:], self.uh[j][:].bitcast(F32),
                                     ALU.subtract).then_inc(self.s_lo, 1)

    def put_aside(self, sp, h, j):
        sp.wait_ge(self.s_gelu, h * 2 + (j + 1))
        sp.dma_start(self.c.aside[bass.ds(h * 2 + j, 1)].rearrange("a p t -> p (a t)"),
                     self.gel[j][:]).then_inc(self.s_st[j], 16)

    def sync_step(self, sp, h, final=False):
        for j in range(2):
            if not final:
                self.load(sp, h + 1, j)
            self.put_aside(sp, h, j)

    def tensor_step(self, pe, h, first=False, final=False):
        self.flip(pe, h, 1, first)
        self.acts(pe, h, 0, first)
        if not final:
            self.flip(pe, h + 1, 0)
        self.acts(pe, h, 1, first)

    def scalar_step(self, act, h, first=False, final=False):
        self.high(act, h, 1, first)
        self.gelu(act, h, 0, first)
        if not final:
            self.high(act, h + 1, 0)
        self.gelu(act, h, 1, first)

    def pool_step(self, pool, h):
        self.low(pool, h, 0)
        self.low(pool, h, 1)


def select_experts(c, ahead, steps):
    nc = c.nc
    U, NPAIR = 2 * PH, PH * TOPK
    runs, off = [], 0
    for a, n in CAND:
        if runs and runs[-1][2] == n:
            runs[-1][1] += 1
        else:
            runs.append([a, 1, n, off])
        off += n
    with c.stage() as mem:
        def sb(name, shape, dt=F32):
            return mem.enter_context(nc.sbuf_tensor(name, shape, dt))

        rest = sb("rest", [P, U, NKEYS])
        top = sb("top", [P, U, TOPK])
        idx = sb("idx", [P, U, TOPK], U32)
        idxf = sb("idxf", [P, U, TOPK])
        cv = sb("cand_values", [P, PH, NCAND])
        cr = sb("cand_rest", [P, PH, NCAND])
        ce = sb("cand_experts", [P, PH, NCAND])
        best = sb("best", [P, PH, TOPK])
        pos = sb("pos", [P, PH, TOPK], U32)
        posf = sb("posf", [P, PH, TOPK])
        iota = sb("iota_cand", [P, NCAND])
        hit = sb("hit", [P, PH, TOPK, NCAND])
        ex = sb("exp_gate", [P, NT, PH, TOPK])
        esum = sb("exp_sum", [P, NT * PH])
        gate = sb("gate", [P, NT, NPAIR])
        expert = sb("expert", [P, NT, NPAIR])
        e_int = sb("expert_int", [P, NT, NPAIR], I32)
        part = [sb(f"expert_part{i}", [P, NT, NPAIR], I32) for i in range(2)]
        partf = [sb(f"expert_partf{i}", [P, NT, NPAIR]) for i in range(2)]
        ps = [mem.enter_context(nc.psum_tensor(f"se{i}", [P, SEQ], F32)) for i in range(3)]
        s_iota, s_v, s_d, s_ex = c.sem("iota_cand_set"), c.sem("select_dve"), c.sem("gate_diffs"), c.sem("gate_exps")
        s_tr = c.sem("pairs_tr")
        with nc.Block() as block:

            @block.gpsimd
            def _(pool):
                nc.gpsimd.iota(iota[:], [[1, NCAND]], base=0, channel_multiplier=0,
                               allow_small_or_imprecise_dtypes=True).then_inc(s_iota, 1)
                with pool.Fori(0, steps) as i:
                    ahead.pool_step(pool, i)

            @block.sync
            def _(sp):
                ahead.load(sp, 0, 0, True)
                ahead.load(sp, 0, 1, True)
                with sp.Fori(0, steps) as i:
                    ahead.sync_step(sp, i)

            @block.scalar
            def _(act):
                ahead.high(act, 0, 0, True)
                ahead.scalar_step(act, 0, first=True)
                with act.Fori(1, steps) as i:
                    ahead.scalar_step(act, i)
                act.wait_ge(s_d, NT)
                nc.scalar.activation(ex[:], ex[:], ACT.Exp).then_inc(s_ex, 1)

            @block.vector
            def _(dve):
                ch = Chain(dve, s_v)

                for t in range(NT):
                    for u in range(U):
                        ch.step(nc.vector.max(top[:, u, 0:8], c.SC[:, t, u, :]))
                    ch.wait()
                    for u in range(U):
                        ch.step(nc.vector.match_replace(rest[:, u, :], top[:, u, 0:8], c.SC[:, t, u, :], LOWEST))
                    for u in range(U):
                        ch.step(nc.vector.max_index(idx[:, u, 0:8], top[:, u, 0:8], c.SC[:, t, u, :]))
                    ch.wait(ch.n - U)
                    for u in range(U):
                        ch.step(nc.vector.max(top[:, u, 8:16], rest[:, u, :]))
                    ch.wait()
                    for u in range(U):
                        ch.step(nc.vector.max_index(idx[:, u, 8:16], top[:, u, 8:16], rest[:, u, :]))
                    v = top[:].rearrange("p (h s) k -> p h s k", s=2)
                    for a0, na, n, o in runs:
                        ch.step(nc.vector.tensor_tensor(
                            cv[:, :, o:o + na * n].rearrange("p h (a b) -> p h a b", b=n),
                            v[:, :, 0, a0:a0 + na].unsqueeze(3).broadcast_to([P, PH, na, n]),
                            v[:, :, 1, 0:n].unsqueeze(2).broadcast_to([P, PH, na, n]), ALU.add))
                    ch.wait()
                    ch.step(nc.vector.tensor_copy(idxf[:], idx[:]))
                    for h in range(PH):
                        ch.step(nc.vector.max(best[:, h, 0:8], cv[:, h, :]))
                    ch.wait(ch.n - PH)
                    i1 = idxf[:].rearrange("p (h s) k -> p h s k", s=2)[:, :, 0, :]
                    i2 = idxf[:].rearrange("p (h s) k -> p h s k", s=2)[:, :, 1, :]
                    ch.step(nc.vector.tensor_scalar(i1, i1, float(NKEYS), None, ALU.mult))
                    ch.wait()
                    for h in range(PH):
                        ch.step(nc.vector.match_replace(cr[:, h, :], best[:, h, 0:8], cv[:, h, :], LOWEST))
                    for a0, na, n, o in runs:
                        ch.step(nc.vector.tensor_tensor(
                            ce[:, :, o:o + na * n].rearrange("p h (a b) -> p h a b", b=n),
                            i1[:, :, a0:a0 + na].unsqueeze(3).broadcast_to([P, PH, na, n]),
                            i2[:, :, 0:n].unsqueeze(2).broadcast_to([P, PH, na, n]), ALU.add))
                    ch.wait()
                    for h in range(PH):
                        ch.step(nc.vector.max(best[:, h, 8:16], cr[:, h, :]))
                    for h in range(PH):
                        ch.step(nc.vector.max_index(pos[:, h, 0:8], best[:, h, 0:8], cv[:, h, :]))
                    ch.wait(ch.n - PH)
                    for h in range(PH):
                        ch.step(nc.vector.max_index(pos[:, h, 8:16], best[:, h, 8:16], cr[:, h, :]))
                    nc.vector.tensor_tensor(ex[:, t, :, :], best[:], best[:, :, 0:1].broadcast_to([P, PH, TOPK]),
                                            ALU.subtract).then_inc(s_d, 1)
                    ch.wait()
                    ch.step(nc.vector.tensor_copy(posf[:], pos[:]))
                    ch.wait()
                    if t == 0:
                        dve.wait_ge(s_iota, 1)
                    for h in range(PH):
                        ch.step(nc.vector.tensor_tensor(
                            hit[:, h, :, :], iota[:].unsqueeze(1).broadcast_to([P, TOPK, NCAND]),
                            posf[:, h, :].unsqueeze(2).broadcast_to([P, TOPK, NCAND]), ALU.is_equal))
                    ch.wait()
                    for h in range(PH):
                        ch.step(nc.vector.tensor_tensor(hit[:, h, :, :], hit[:, h, :, :],
                                                        ce[:, h, :].unsqueeze(1).broadcast_to([P, TOPK, NCAND]),
                                                        ALU.mult))
                    ch.wait()
                    ch.step(nc.vector.tensor_reduce(expert[:, t, :].rearrange("p (h k) -> p h k", h=PH), hit[:], AX.X,
                                                    ALU.add))
                    ch.wait()
                dve.wait_ge(s_ex, 1)
                ex3 = ex[:].rearrange("p t h k -> p (t h) k")
                ch.step(nc.vector.tensor_reduce(esum[:], ex3, AX.X, ALU.add))
                ch.wait()
                ch.step(nc.vector.reciprocal(esum[:], esum[:]))
                ch.wait()
                ch.step(nc.vector.tensor_tensor(gate[:].rearrange("p t (h k) -> p (t h) k", h=PH), ex3,
                                                esum[:].unsqueeze(2).broadcast_to([P, NT * PH, TOPK]), ALU.mult))
                ch.step(nc.vector.tensor_copy(e_int[:], expert[:]))
                ch.wait()
                ch.step(nc.vector.tensor_scalar(part[0][:], e_int[:], 7, None, ALU.arith_shift_right))
                ch.step(nc.vector.tensor_scalar(part[1][:], e_int[:], NKEYS - 1, None, ALU.bitwise_and))
                ch.wait()
                for i in range(2):
                    ch.step(nc.vector.tensor_copy(partf[i][:], part[i][:]))
                for i, dst in enumerate((c.I1T, c.I2T, c.GT)):
                    dve.wait_ge(s_tr, i + 1)
                    nc.vector.tensor_copy(dst[:], ps[i][:])
                c.select_steps = ch.n

            @block.tensor
            def _(pe):
                ahead.flip(pe, 0, 0, True)
                ahead.tensor_step(pe, 0, first=True)
                with pe.Fori(1, steps) as i:
                    ahead.tensor_step(pe, i)
                pe.wait_ge(s_v, c.select_steps)
                for i, src in enumerate((partf[0], partf[1], gate)):
                    for t in range(NT):
                        last = nc.tensor.transpose(ps[i][:, t * P:(t + 1) * P], src[:, t, :], c.ident[:])
                    last.then_inc(s_tr, 1)


SELECT_STEPS = 16
EXTRA_STEPS = 2
N_AHEAD = 2 * (SELECT_STEPS + SEQ // 32 + EXTRA_STEPS)
GT_BLK = 64
NB = SEQ // GT_BLK


def dense_gates(c, ahead, h0, v_tab):
    nc = c.nc
    RING, SLOTS, Q = 32, 16, 4
    TURN = 2 * GT_BLK
    T = SEQ // TURN
    NQ = RING // Q
    PIECES = 4
    with c.stage() as mem:
        iota = mem.enter_context(nc.sbuf_tensor("iota_keys", [P, NKEYS], F32))
        oh2 = mem.enter_context(nc.sbuf_tensor("one_hot2", [P, SLOTS, NKEYS], F32))
        oh1 = mem.enter_context(nc.sbuf_tensor("gated_hot1", [P, SLOTS, NKEYS], F32))
        block1 = mem.enter_context(nc.sbuf_tensor("gate_block", [P, NKEYS, GT_BLK], F32))
        blk = [c.SC[:].rearrange("p t u n -> p (t u n)").rearrange("p (n t) -> p n t", t=GT_BLK), block1[:]]
        ps = [mem.enter_context(nc.psum_tensor(f"dg{i}", [P, SEQ], F32)) for i in range(4)]
        s_iota, s_hot, s_pe, s_st = c.sem("iota_keys_set"), c.sem("one_hots"), c.sem("gates_made"), c.sem("gates_stored")
        s_dma, s_v = [c.sem("gate_block_out0"), c.sem("gate_block_out1")], c.sem("first_v_loaded")

        def turns(eng, body):
            body(0, True, False)
            with eng.Fori(1, T - 1) as i:
                body(i, False, False)
            body(T - 1, False, True)

        def steps(i, final):
            n = TURN // RING
            return [i * n + (h0 + k) for k in range(n + (EXTRA_STEPS if final else 0))]

        FINAL = h0 + SEQ // RING + EXTRA_STEPS - 1

        with nc.Block() as block:

            @block.gpsimd
            def _(pool):
                nc.gpsimd.iota(iota[:], [[1, NKEYS]], base=0, channel_multiplier=0,
                               allow_small_or_imprecise_dtypes=True).then_inc(s_iota, 1)
                with pool.Fori(0, SEQ // RING + EXTRA_STEPS) as i:
                    ahead.pool_step(pool, i + h0)

            @block.vector
            def _(dve):
                dve.wait_ge(s_iota, 1)

                def hots(i, first):
                    for r in range(RING):
                        if r % Q == 0 and not (first and r < SLOTS):
                            dve.wait_ge(s_pe, i * NQ + (r // Q - (SLOTS // Q - 1)))
                        tok = bass.ds(i * RING + r, 1)
                        nc.vector.tensor_scalar(oh2[:, r % SLOTS, :], iota[:], c.I2T[:, tok], None, ALU.is_equal)
                        last = nc.vector.tensor_scalar(oh1[:, r % SLOTS, :], iota[:], c.I1T[:, tok], c.GT[:, tok],
                                                       ALU.is_equal, ALU.mult)
                        if r % Q == Q - 1:
                            last.then_inc(s_hot, 1)
                hots(0, True)
                with dve.Fori(1, SEQ // RING) as i:
                    hots(i, False)

            @block.tensor
            def _(pe):
                def turn(i, first, last):
                    for k, h in enumerate(steps(i, last)):
                        final = last and h == FINAL
                        if k >= TURN // RING:
                            ahead.tensor_step(pe, h, final=final)
                            continue
                        for q in range(NQ):
                            g = k * NQ + q
                            pe.wait_ge(s_hot, i * (TURN // Q) + (g + 1))
                            if not (first and g < 4):
                                pe.wait_ge(s_st, i * (TURN // Q) + (g - 3))
                            for r in range(q * Q, q * Q + Q):
                                made = nc.tensor.matmul(ps[q % 4][:, (r % Q) * P:(r % Q + 1) * P], oh2[:, r % SLOTS, :],
                                                        oh1[:, r % SLOTS, :], start=True, stop=True)
                            made.then_inc(s_pe, 1)
                            if q == 1:
                                ahead.flip(pe, h, 1)
                            elif q == 3:
                                ahead.acts(pe, h, 0)
                            elif q == 5:
                                ahead.flip(pe, h + 1, 0)
                            elif q == 7:
                                ahead.acts(pe, h, 1)
                turns(pe, turn)

            @block.scalar
            def _(act):
                def turn(i, first, last):
                    for k, h in enumerate(steps(i, last)):
                        if k >= TURN // RING:
                            ahead.scalar_step(act, h, final=last and h == FINAL)
                            continue
                        for q in range(NQ):
                            g = k * NQ + q
                            b, o = divmod(g, GT_BLK // Q)
                            if o == 0 and not first:
                                act.wait_ge(s_dma[b], i * (16 * PIECES))
                            act.wait_ge(s_pe, i * (TURN // Q) + (g + 1))
                            nc.scalar.activation(blk[b][:, :, o * Q:(o + 1) * Q],
                                                 ps[q % 4][:].rearrange("p (t n) -> p n t", t=Q),
                                                 ACT.Copy).then_inc(s_st, 1)
                            if q == 2:
                                ahead.high(act, h, 1)
                            elif q == 4:
                                ahead.gelu(act, h, 0)
                            elif q == 6:
                                ahead.high(act, h + 1, 0)
                            elif q == 7:
                                ahead.gelu(act, h, 1)
                turns(act, turn)

            @block.sync
            def _(sp):
                def piece(i, b, n):
                    sp.wait_ge(s_st, i * (TURN // Q) + (b + 1) * (GT_BLK // Q))
                    rows = slice(n * NKEYS // PIECES, (n + 1) * NKEYS // PIECES)
                    sp.dma_start(c.gates[bass.ds(i * 2 + b, 1), :, rows, :].rearrange("a p n t -> p (a n t)"),
                                 blk[b][:, rows, :].rearrange("p n t -> p (n t)")).then_inc(s_dma[b], 16)

                def turn(i, first, last):
                    for k, h in enumerate(steps(i, last)):
                        for j in range(2):
                            if not (last and h == FINAL):
                                ahead.load(sp, h + 1, j)
                            ahead.put_aside(sp, h, j)
                            n = 2 * (k % 2) + j
                            if k in (2, 3):
                                piece(i, 0, n)
                            elif k >= 4:
                                piece(i, 1, n)
                            elif not first:
                                piece(i - 1, 1, n)
                turns(sp, turn)
                for j in range(len(c.vst)):
                    sp.dma_start(c.vst[j][:], v_tab[j * P:(j + 1) * P, :]).then_inc(s_v, 16)
                sp.wait_ge(s_v, 16 * len(c.vst))
                for b in range(2):
                    sp.wait_ge(s_dma[b], 16 * PIECES * T)
                    sp.wait_ge(ahead.s_st[b], 16 * (ahead.count // 2))


def experts(c, u_tab, v_tab, n0, n1, ready):
    nc = c.nc
    G, B = 2, 4
    HALF = D // 2
    tag = "_r" if ready else "_f"
    with c.stage() as mem:
        def sb(name, shape, dt=F32):
            return mem.enter_context(nc.sbuf_tensor(name + tag, shape, dt))

        ust = [] if ready else [sb(f"u{j}", [P, D]) for j in range(B)]
        vst = c.vst
        uh = [sb(f"u_hi{j}", [P, ND, P], F32R) for j in range(0 if ready else 2)]
        ul = [sb(f"u_lo{j}", [P, ND, P], F32R) for j in range(0 if ready else 2)]
        vh = [sb(f"v_hi{j}", [P, D], F32R) for j in range(B)]
        vl = [sb(f"v_lo{j}", [P, D], F32R) for j in range(B)]
        gst = [sb(f"g{j}", [P, NB, G * GT_BLK]) for j in range(2)]
        NG = B if ready else 2
        gel = [sb(f"gelu{j}", [P, SEQ]) for j in range(NG)]
        s_back = [c.sem(f"acts_back{j}") for j in range(B)]
        hid = [sb(f"hid{j}", [P, SEQ]) for j in range(2)]
        hh = [sb(f"hid_hi{j}", [P, SEQ], F32R) for j in range(B)]
        hl = [sb(f"hid_lo{j}", [P, SEQ], F32R) for j in range(B)]
        tr = [] if ready else \
            [[mem.enter_context(nc.psum_tensor(f"ut{j}{k}", [P, 4, P], F32)) for k in range(2)] for j in range(2)]
        pa = [] if ready else [mem.enter_context(nc.psum_tensor(f"acts{j}", [P, SEQ], F32)) for j in range(2)]
        NPO = 8 if ready else 2
        po = [mem.enter_context(nc.psum_tensor(f"outs{j}{tag}", [P, HALF], F32)) for j in range(NPO)]
        s_u = [c.sem(f"u_loaded{j}") for j in range(B)]
        s_vl = [c.sem(f"v_loaded{j}") for j in range(B)]
        s_g = [c.sem(f"g_loaded{j}") for j in range(2)]
        s_tr, s_uhi, s_ulo, s_act = c.sem("u_transposed"), c.sem("u_high"), c.sem("u_low"), c.sem("acts_made")
        s_gelu, s_hid, s_hh, s_hl = c.sem("gelu_done"), c.sem("hid_made"), c.sem("hid_high"), c.sem("hid_low")
        s_vh, s_vlo, s_out, s_acc = c.sem("v_high"), c.sem("v_low"), c.sem("outs_made"), c.sem("outs_added")
        outs = [(t, h) for t in range(NT) for h in range(2)]
        NO = len(outs)
        T = (n1 - n0) // B

        def turns(eng, body):
            body(0, True, False)
            with eng.Fori(1, T - 1) as i:
                body(i, False, False)
            body(T - 1, False, True)

        with nc.Block() as block:

            @block.sync
            def _(sp):
                def loads(i, first, last):
                    for j in range(B):
                        n = i * B + (n0 + j)
                        if ready:
                            if not first:
                                sp.wait_ge(s_hid, i * B + (j - 3))
                            sp.dma_start(gel[j][:], c.aside[bass.ds(n, 1)].rearrange("a p t -> p (a t)"))\
                                .then_inc(s_back[j], 16)
                        else:
                            if not first:
                                sp.wait_ge(s_tr, i * B + (j - 3))
                            sp.dma_start(ust[j][:], u_tab[bass.ds(n * P, P), :]).then_inc(s_u[j], 16)
                        if j % G == 0:
                            if not first:
                                sp.wait_ge(s_hid, i * B + (j - 2))
                            sp.dma_start(gst[j // G][:], c.gates[:, :, bass.ds(n, G), :].rearrange(
                                "b p i t -> p b (i t)")).then_inc(s_g[j // G], 16)
                        if not first:
                            sp.wait_ge(s_vlo, i * B + (j - 3))
                        if not (first and ready):
                            sp.dma_start(vst[j][:], v_tab[bass.ds(n * P, P), :]).then_inc(s_vl[j], 16)
                turns(sp, loads)

            @block.tensor
            def _(pe):
                def flip(i, j, first):
                    pe.wait_ge(s_u[j % B], 16 * i + (16 if j < B else 32))
                    if not (first and j < 2):
                        pe.wait_ge(s_ulo, i * B + (j - 1))
                    for k in range(2):
                        for d in range(4):
                            last = nc.tensor.transpose(tr[j % 2][k][:, d, :], ust[j % B][:, (4 * k + d) * P:(4 * k + d + 1) * P],
                                                       c.ident[:])
                    last.then_inc(s_tr, 1)

                def acts(i, j, first):
                    pe.wait_ge(s_ulo, i * B + (j + 1))
                    if not (first and j < 2):
                        pe.wait_ge(s_gelu, i * B + (j - 1))
                    for d in range(ND):
                        last = three_pass(nc, pa[j % 2][:], uh[j % 2][:, d, :], ul[j % 2][:, d, :], c.XH[:, d, :],
                                          c.XL[:, d, :], d == 0, d == ND - 1)
                    last.then_inc(s_act, 1)

                def values(i, g, first):
                    pe.wait_ge(s_vlo, i * B + (G * g + G))
                    pe.wait_ge(s_hl, i * B + (G * g + G))
                    for o, (t, h) in enumerate(outs):
                        if not (first and g == 0 and o < NPO):
                            pe.wait_ge(s_acc, i * (2 * NO) + (g * NO + o - (NPO - 1)))
                        for k in range(G):
                            j = (G * g + k) % B
                            a, v = slice(t * P, (t + 1) * P), slice(h * HALF, (h + 1) * HALF)
                            last = three_pass(nc, po[o % NPO][:], hh[j][:, a], hl[j][:, a], vh[j][:, v], vl[j][:, v],
                                              k == 0, k == G - 1)
                        last.then_inc(s_out, 1)

                def turn(i, first, last):
                    if first and not ready:
                        flip(0, 0, True)
                    for j in range(B):
                        if not ready:
                            if not (last and j == B - 1):
                                flip(i, j + 1, first)
                            acts(i, j, first)
                        if j % G == G - 1 and not (first and j < G):
                            values(i, j // G - 1, first)
                    if last:
                        values(i, 1, first)
                turns(pe, turn)

            @block.scalar
            def _(act):
                def u_high(i, j, first):
                    act.wait_ge(s_tr, i * B + (j + 1))
                    if not (first and j < 2):
                        act.wait_ge(s_act, i * B + (j - 1))
                    for k in range(2):
                        nc.scalar.activation(uh[j % 2][:, 4 * k:4 * k + 4, :], tr[j % 2][k][:], ACT.Copy).then_inc(s_uhi, 1)

                def turn(i, first, last):
                    if first and not ready:
                        u_high(0, 0, True)
                    for j in range(B):
                        if not (last and j == B - 1) and not ready:
                            u_high(i, j + 1, first)
                        if not (first and ready):
                            act.wait_ge(s_vl[j], 16 * i + (0 if ready else 16))
                        if not first:
                            act.wait_ge(s_out, i * (2 * NO) + (j // G - 1) * NO)
                        nc.scalar.activation(vh[j][:], vst[j][:], ACT.Copy).then_inc(s_vh, 1)
                        if not ready:
                            act.wait_ge(s_act, i * B + (j + 1))
                            if not (first and j < 2):
                                act.wait_ge(s_hid, i * B + (j - 1))
                            nc.scalar.activation(gel[j % NG][:], pa[j % 2][:], ACT.Gelu).then_inc(s_gelu, 1)
                        act.wait_ge(s_hid, i * B + (j + 1))
                        nc.scalar.activation(hh[j][:], hid[j % 2][:], ACT.Copy).then_inc(s_hh, 1)
                turns(act, turn)

            @block.gpsimd
            def _(pool):
                def turn(i, first, last):
                    for j in range(B):
                        pool.wait_ge(s_vh, i * B + (j + 1))
                        nc.gpsimd.tensor_tensor(vl[j][:], vst[j][:], vh[j][:].bitcast(F32), ALU.subtract).then_inc(s_vlo, 1)
                turns(pool, turn)

            @block.vector
            def _(dve):
                def u_low(i, j, first):
                    for k in range(2):
                        dve.wait_ge(s_uhi, i * (2 * B) + (2 * j + k + 1))
                        d = slice(4 * k, 4 * k + 4)
                        last = nc.vector.tensor_tensor(ul[j % 2][:, d, :], tr[j % 2][k][:], uh[j % 2][:, d, :].bitcast(F32),
                                                       ALU.subtract)
                    last.then_inc(s_ulo, 1)

                def add(i, g):
                    for o, (t, h) in enumerate(outs):
                        dve.wait_ge(s_out, i * (2 * NO) + (g * NO + o + 1))
                        H = c.H[:, t, h * HALF:(h + 1) * HALF]
                        nc.vector.tensor_tensor(H, H, po[o % NPO][:], ALU.add).then_inc(s_acc, 1)

                def turn(i, first, last):
                    if first and not ready:
                        u_low(0, 0, True)
                    for j in range(B):
                        if not (last and j == B - 1) and not ready:
                            u_low(i, j + 1, first)
                        if j % G == 0:
                            dve.wait_ge(s_g[j // G], 16 * i + 16)
                        if ready:
                            dve.wait_ge(s_back[j], 16 * i + 16)
                        else:
                            dve.wait_ge(s_gelu, i * B + (j + 1))
                        if not (first and j < 2):
                            dve.wait_ge(s_hl, i * B + (j - 1))
                        nc.vector.tensor_tensor(
                            hid[j % 2][:].rearrange("p (b t) -> p b t", b=NB), gel[j % NG][:].rearrange("p (b t) -> p b t", b=NB),
                            gst[j // G][:, :, (j % G) * GT_BLK:(j % G + 1) * GT_BLK], ALU.mult).then_inc(s_hid, 1)
                        dve.wait_ge(s_hh, i * B + (j + 1))
                        nc.vector.tensor_tensor(hl[j][:], hid[j % 2][:], hh[j][:].bitcast(F32), ALU.subtract).then_inc(s_hl, 1)
                        if j % G == G - 1 and not (first and j < G):
                            add(i, j // G - 1)
                    if last:
                        add(i, 1)
                turns(dve, turn)


def load_tokens(c, tag, dst, src):
    nc = c.nc
    s = c.sem(f"loaded_{tag}")
    with nc.Block() as block:

        @block.sync
        def _(sp):
            sp.dma_start(dst, src).then_inc(s, 16)
            sp.wait_ge(s, 16)


def gated(c, z, r):
    nc = c.nc
    s_s = c.sem("sigmoids")
    with nc.Block() as block:

        @block.scalar
        def _(act):
            for d in range(ND):
                nc.scalar.activation(z[:, d * SEQ:(d + 1) * SEQ], z[:, d * SEQ:(d + 1) * SEQ], ACT.Sigmoid).then_inc(s_s, 1)

        @block.vector
        def _(dve):
            for d in range(ND):
                dve.wait_ge(s_s, d + 1)
                a = slice(d * SEQ, (d + 1) * SEQ)
                nc.vector.tensor_tensor(z[:, a], z[:, a], r[:, a], ALU.mult)


def finish(c, gain, out):
    nc = c.nc
    s_m, s_o = c.sem("final_scaled"), c.sem("final_out")
    with nc.Block() as block:

        @block.vector
        def _(dve):
            for t in range(NT):
                nc.vector.tensor_tensor(c.XN[:, t, :], c.XN[:, t, :], gain[:], ALU.mult).then_inc(s_m, 1)

        @block.sync
        def _(sp):
            for t in range(NT):
                sp.wait_ge(s_m, t + 1)
                sp.dma_start(out[0, t * P:(t + 1) * P, :], c.XN[:, t, :]).then_inc(s_o, 16)
            sp.wait_ge(s_o, 16 * NT)


def build(nc, ins, out):
    with ExitStack() as ctx:
        c = Chip(nc, ctx)
        c.H = c.keep("H", [P, NT, D], F32)
        c.XH = c.keep("XH", [P, ND, SEQ], F32R)
        c.XL = c.keep("XL", [P, ND, SEQ], F32R)
        c.ident = c.keep("ident", [P, P], F32)
        c.eps = c.keep("eps", [P, 1], F32)
        g_mix = c.keep("g_mix", [P, ND], F32)
        g_ffn = c.keep("g_ffn", [P, ND], F32)
        g_ple = c.keep("g_ple", [P, ND], F32)

        small = [(g_mix[:], ins["norm_mix"][0].rearrange("(k p) -> p k", p=P)),
                 (g_ffn[:], ins["norm_ffn"][0].rearrange("(k p) -> p k", p=P)),
                 (g_ple[:], ins["norm_ple"][0].rearrange("(k p) -> p k", p=P))]
        with nc.allow_non_contiguous_dma(reason="three gains of 4 KiB, once"):
            constants_and_load(c, ins["x"], small)
        s_eps = c.sem("eps_set")
        with nc.Block() as block:
            @block.vector
            def _(dve):
                nc.vector.memset(c.eps[:], EPS).then_inc(s_eps, 1)

        w_in = ins["w_in"][0].rearrange("(k p) n -> p k n", p=P)
        with ExitStack() as mem:
            c.PROJ = mem.enter_context(nc.sbuf_tensor("PROJ", [P, NU_IN * SEQ], F32))
            c.GLR = mem.enter_context(nc.sbuf_tensor("GLR", [RANK, SEQ], F32))
            with ExitStack() as m2:
                c.XN = m2.enter_context(nc.sbuf_tensor("XN", [P, NT, D], F32))
                normalize(c, "mix")
                feature_major(c, "mix", c.XN, gain=g_mix)

            def keep_tile(base):
                def store(dve, ps, u, n, sem):
                    nc.vector.tensor_scalar(c.PROJ[:, bass.ds(u * SEQ + base * SEQ, SEQ)], ps[:], 1.0, None,
                                            ALU.mult).then_inc(sem, 1)
                return store

            def keep_rank(dve, ps, u, n, sem):
                nc.vector.tensor_copy(c.GLR[:], ps[0:RANK, :]).then_inc(sem, 1)
            project(c, "in", [
                (1, lambda u: w_in[:, :, GLR_COL:GLR_COL + RANK], ND, RANK, keep_rank),
                (8, lambda u: w_in[:, :, bass.ds(u * P, P)], ND, P, keep_tile(0)),
                (16, lambda u: w_in[:, :, bass.ds(u * P + (GLR_COL + RANK), P)], ND, P, keep_tile(8)),
            ])
            c.TOK = mem.enter_context(nc.sbuf_tensor("TOK", [P, NT, 1536], F32))
            c.MIX = mem.enter_context(nc.sbuf_tensor("MIX", [P, NT, D], F32))
            c.BIAS = mem.enter_context(nc.sbuf_tensor("BIAS", [P, ATT_HEADS, 2 * P], F32))
            relative_bias(c, ins["rel_bias"])
            tokens_as_rows(c)
            gla(c, ins)
            band_attention(c)
            feature_major(c, "att", c.MIX)

        def keep_in(dst):
            def store(dve, ps, u, n, sem):
                nc.vector.tensor_scalar(dst[:, bass.ds(u * SEQ, SEQ)], ps[:], 1.0, None, ALU.mult).then_inc(sem, 1)
            return store

        def columns(w, k):
            w = w.rearrange("(k p) n -> p k n", p=P)
            return lambda u: w[:, :, bass.ds(u * P, P)]

        with ExitStack() as mem:
            rows = mem.enter_context(nc.sbuf_tensor("out_proj", [P, ND * SEQ], F32))
            project(c, "out", [(ND, columns(ins["w_out"][0], ND), ND, P, keep_in(rows))])
            add_rows(c, "out", rows)
        with ExitStack() as mem:
            c.XN = mem.enter_context(nc.sbuf_tensor("XN2", [P, NT, D], F32))
            normalize(c, "ffn")
            feature_major(c, "ffn", c.XN, gain=g_ffn)
        c.vst = [c.keep(f"v{j}", [P, D], F32) for j in range(4)]
        with ExitStack() as mem:
            c.SC = mem.enter_context(nc.sbuf_tensor("scores", [P, NT, 2 * PH, NKEYS], F32))
            with ExitStack() as m2:
                c.QH = m2.enter_context(nc.sbuf_tensor("queries_hi", [P, 2 * PH * SEQ], F32R))
                c.QL = m2.enter_context(nc.sbuf_tensor("queries_lo", [P, 2 * PH * SEQ], F32R))
                s_qh = c.sem("query_high")

                def split_query(dve, ps, u, n, sem):
                    a = bass.ds(u * SEQ, SEQ)
                    nc.vector.tensor_scalar(c.QH[:, a], ps[:], 1.0, None, ALU.mult).then_inc(s_qh, 1)
                    dve.wait_ge(s_qh, n + 1)
                    nc.vector.tensor_tensor(c.QL[:, a], ps[:], c.QH[:, a].bitcast(F32), ALU.subtract).then_inc(sem, 1)
                project(c, "query", [(2 * PH, columns(ins["peer_wq"][0], ND), ND, P, split_query)])
                key_scores(c, ins["peer_subkeys"][0])
            c.I1T = mem.enter_context(nc.sbuf_tensor("I1T", [P, SEQ], F32))
            c.I2T = mem.enter_context(nc.sbuf_tensor("I2T", [P, SEQ], F32))
            c.GT = mem.enter_context(nc.sbuf_tensor("GT", [P, SEQ], F32))
            c.gates = nc.dram_tensor("gates", (NB, NKEYS, NKEYS, GT_BLK), F32, kind="Internal").ap()
            c.aside = nc.dram_tensor("acts_aside", (N_AHEAD, P, SEQ), F32, kind="Internal").ap()
            ahead = Ahead(c, mem, ins["peer_u"][0], N_AHEAD)
            select_experts(c, ahead, SELECT_STEPS)
            dense_gates(c, ahead, SELECT_STEPS, ins["peer_v"][0])
        experts(c, ins["peer_u"][0], ins["peer_v"][0], 0, N_AHEAD, True)
        experts(c, ins["peer_u"][0], ins["peer_v"][0], N_AHEAD, NKEYS, False)
        with ExitStack() as mem:
            c.XN = mem.enter_context(nc.sbuf_tensor("XN3", [P, NT, D], F32))
            z = mem.enter_context(nc.sbuf_tensor("ple_gate", [P, ND * SEQ], F32))
            r = mem.enter_context(nc.sbuf_tensor("ple_value", [P, ND * SEQ], F32))
            gain = mem.enter_context(nc.sbuf_tensor("final_gain", [P, D], F32))
            normalize(c, "ple")
            feature_major(c, "ple", c.XN, gain=g_ple)
            project(c, "gate", [(ND, columns(ins["w_ple_gate"][0], ND), ND, P, keep_in(z))])
            load_tokens(c, "p", c.XN[:, :, 0:PLE], ins["p"][0, 0].rearrange("(t p) d -> p t d", p=P))
            feature_major(c, "emb", c.XN, nd=PLE // P)
            project(c, "emb", [(ND, columns(ins["w_ple"][0], 2), PLE // P, P, keep_in(r))])
            gated(c, z, r)
            add_rows(c, "ple", z)
            load_tokens(c, "gain", gain[:], ins["final_norm"].unsqueeze(0).broadcast_to([P, D]))
            normalize(c, "final")
            finish(c, gain, out)


_INS = ["x", "p", "norm_mix", "w_in", "gla_gate_w2", "gla_gate_b", "gla_head_norm", "rel_bias", "w_out", "norm_ffn",
        "peer_wq", "peer_subkeys", "peer_u", "peer_v", "norm_ple", "w_ple_gate", "w_ple", "final_norm"]

def kernel(**inputs):
    import numpy as _np
    import concourse.bacc as _bacc
    from concourse import mybir as _mybir
    from concourse.bass_utils import run_bass_kernel_spmd as _run

    nc = _bacc.Bacc("TRN2", target_bir_lowering=False, num_devices=1)
    arrays, args = {}, {}
    for name in _INS:
        a = _np.ascontiguousarray(inputs[name])
        arrays[f"in_{name}_dram"] = a
        args[name] = nc.dram_tensor(f"in_{name}_dram", a.shape, _mybir.dt.from_np(a.dtype), kind="ExternalInput").ap()
    out = nc.dram_tensor("out_0_dram", (1, SEQ, D), _mybir.dt.float32, kind="ExternalOutput").ap()
    build(nc, args, out)
    r = _run(nc, [arrays], core_ids=[0])
    return r.results[0]["out_0_dram"]
```

```python
import concourse.bass as bass
from concourse import mybir
from contextlib import ExitStack, contextmanager

F32 = mybir.dt.float32
F32R = mybir.dt.float32r
I32 = mybir.dt.int32
U32 = mybir.dt.uint32
ALU = mybir.AluOpType
ACT = mybir.ActivationFunctionType
AX = mybir.AxisListType

P = 128
SEQ, D = 512, 1024
NT, ND = SEQ // P, D // P
CHUNK = 64
NCH = SEQ // CHUNK
GLA_HEADS, GLA_DK, GLA_DV, RANK = 4, 64, 128, 16
ATT_HEADS, ATT_DH = 8, 64
REL_CLIP = 128
NEG = -1e30
EPS = 1e-6
GATE_NORM = 16.0
PH, NKEYS, TOPK = 8, 128, 16
PLE = 256
LOWEST = -3.0e38

UQ, UK, UV, UG, UAQ, UAK, UAV = 0, 2, 4, 8, 12, 16, 20
NU_IN = 24
GLR_COL = 1024
CAND = [(a, TOPK // (a + 1)) for a in range(TOPK)]
NCAND = sum(n for _, n in CAND)


class Chip:

    def __init__(self, nc, ctx):
        self.nc, self.ctx, self.used, self.names = nc, ctx, [], []

    def sem(self, name):
        self.names.append(name)
        again = self.names.count(name)
        self.used.append(self.nc.alloc_semaphore(name if again == 1 else f"{name}_{again}"))
        return self.used[-1]

    @contextmanager
    def stage(self):
        before, self.used = self.used, []
        with ExitStack() as mem:
            yield mem
        self.nc.clear_and_free_semaphores(self.used)
        self.nc.all_engine_barrier()
        self.used = before

    def keep(self, name, shape, dt):
        return self.ctx.enter_context(self.nc.sbuf_tensor(name, shape, dt))


class Chain:

    def __init__(self, eng, sem):
        self.eng, self.sem, self.n = eng, sem, 0

    def step(self, ins):
        self.n += 1
        ins.then_inc(self.sem, 1)
        return self.n

    def wait(self, n=None):
        self.eng.wait_ge(self.sem, self.n if n is None else n)


def three_pass(nc, out, ah, al, bh, bl, first, final):
    nc.tensor.matmul(out, ah, bh, start=first, stop=False)
    nc.tensor.matmul(out, ah, bl, start=False, stop=False)
    return nc.tensor.matmul(out, al, bh, start=False, stop=final)


class Norm:

    def __init__(self, c, mem, tag, gain):
        nc = c.nc
        self.nc, self.c, self.gain = nc, c, gain
        self.ssq, self.rms, self.rstd = [mem.enter_context(nc.sbuf_tensor(f"{n}_{tag}", [P, NT], F32))
                                         for n in ("ssq", "rms", "rstd")]
        self.s_ssq, self.s_rms, self.s_rstd, self.s_xn = [c.sem(f"{n}_{tag}") for n in ("ssq", "rms", "rstd", "xn")]

    def square(self, act, t, out):
        self.nc.scalar.activation(out, self.c.H[:, t, :], ACT.Square,
                                  accum_out=self.ssq[:, t:t + 1]).then_inc(self.s_ssq, 1)

    def root(self, act, t0, t1):
        act.wait_ge(self.s_ssq, t1)
        self.nc.scalar.activation(self.rms[:, t0:t1], self.ssq[:, t0:t1], ACT.Sqrt, scale=1.0 / D,
                                  bias=self.c.eps[:]).then_inc(self.s_rms, t1 - t0)

    def invert(self, dve, t0, t1):
        dve.wait_ge(self.s_rms, t1)
        self.nc.vector.reciprocal(self.rstd[:, t0:t1], self.rms[:, t0:t1]).then_inc(self.s_rstd, t1 - t0)

    def scale(self, dve, t, out):
        dve.wait_ge(self.s_rstd, t + 1)
        self.nc.vector.scalar_tensor_tensor(out=out, in0=self.c.H[:, t, :], scalar=self.rstd[:, t:t + 1],
                                            in1=self.gain, op0=ALU.mult, op1=ALU.mult).then_inc(self.s_xn, 1)


class Flip:

    def __init__(self, c, tag, src, banks):
        self.nc, self.c, self.src, self.banks = c.nc, c, src, banks
        self.s_tr, self.s_hi, self.s_lo = c.sem(f"flipped_{tag}"), c.sem(f"flip_high_{tag}"), c.sem(f"flip_low_{tag}")

    def bank(self, t, g):
        return self.banks[(2 * t + g) % 4][:].rearrange("p (d t) -> p d t", d=4)

    def transpose(self, pe, t):
        for g in range(2):
            if t >= 2:
                pe.wait_ge(self.s_lo, 2 * t + g - 3)
            for d in range(4):
                last = self.nc.tensor.transpose(self.bank(t, g)[:, d, :], self.src[:, t, (4 * g + d) * P:(4 * g + d + 1) * P],
                                                self.c.ident[:])
            last.then_inc(self.s_tr, 1)

    def high(self, act, t):
        for g in range(2):
            act.wait_ge(self.s_tr, 2 * t + g + 1)
            self.nc.scalar.activation(self.c.XH[:, 4 * g:4 * g + 4, t * P:(t + 1) * P], self.bank(t, g),
                                      ACT.Copy).then_inc(self.s_hi, 1)

    def low(self, dve, t):
        for g in range(2):
            dve.wait_ge(self.s_hi, 2 * t + g + 1)
            a = (slice(None), slice(4 * g, 4 * g + 4), slice(t * P, (t + 1) * P))
            self.nc.vector.tensor_tensor(self.c.XL[a], self.bank(t, g), self.c.XH[a].bitcast(F32),
                                         ALU.subtract).then_inc(self.s_lo, 1)


class RowWeights:

    N = ND
    HALF = D // 2

    def __init__(self, c, mem, tag, w, stage, loaded=0, by_vector=()):
        nc = c.nc
        self.nc, self.stage, self.w, self.loaded, self.by_vector = nc, stage, w, loaded, by_vector
        self.wh = mem.enter_context(nc.sbuf_tensor(f"rw_hi_{tag}", [P, self.N, D], F32R))
        self.wl = mem.enter_context(nc.sbuf_tensor(f"rw_lo_{tag}", [P, self.N, D], F32R))
        self.s_w = [c.sem(f"rw_loaded_{tag}{i}") for i in range(4)]
        self.s_hi, self.s_lo, self.s_lov = [c.sem(f"rw_{n}_{tag}") for n in ("high", "low", "low_dve")]

    def load(self, sp, n):
        if n >= 4:
            self.wait_low(sp, n - 4)
        sp.dma_start(self.stage[n % 4][:].rearrange("p (k n) -> p k n", k=2),
                     self.unit(self.w, n)).then_inc(self.s_w[n % 4], 16)

    @classmethod
    def unit(cls, w, n):
        h, k = n // 4, 2 * (n % 4)
        return w.rearrange("(k p) n -> p k n", p=P)[:, k:k + 2, h * cls.HALF:(h + 1) * cls.HALF]

    def high(self, act, n):
        if n >= self.loaded:
            act.wait_ge(self.s_w[n % 4], 16 * (n // 4 + (n % 4 >= self.loaded)))
        self.nc.scalar.activation(self.wh[:, n, :], self.stage[n % 4][:], ACT.Copy).then_inc(self.s_hi, 1)

    def low(self, pool, n):
        pool.wait_ge(self.s_hi, n + 1)
        self.nc.gpsimd.tensor_tensor(self.wl[:, n, :], self.stage[n % 4][:], self.wh[:, n, :].bitcast(F32),
                                     ALU.subtract).then_inc(self.s_lo, 1)

    def low_by_vector(self, dve, n):
        dve.wait_ge(self.s_hi, n + 1)
        self.nc.vector.tensor_tensor(self.wl[:, n, :], self.stage[n % 4][:], self.wh[:, n, :].bitcast(F32),
                                     ALU.subtract).then_inc(self.s_lov, 1)

    def wait_low(self, eng, n):
        mine = [k for k in range(n + 1) if (k in self.by_vector) == (n in self.by_vector)]
        eng.wait_ge(self.s_lov if n in self.by_vector else self.s_lo, len(mine))

    def product(self, pe, c, out, half, t, made):
        for d in range(ND):
            n = 4 * half + d // 2
            if d % 2 == 0 and t == 0:
                self.wait_low(pe, n)
            cols = slice((d % 2) * self.HALF, (d % 2 + 1) * self.HALF)
            tok = slice(t * P, (t + 1) * P)
            last = three_pass(self.nc, out, c.XH[:, d, tok], c.XL[:, d, tok], self.wh[:, n, cols], self.wl[:, n, cols],
                              d == 0, d == ND - 1)
        last.then_inc(made, 1)


class Columns:

    def __init__(self, c, mem, tag, source):
        nc = c.nc
        self.nc, self.c, self.source = nc, c, source
        self.stage = [mem.enter_context(nc.sbuf_tensor(f"wst_{tag}{i}", [P, ND, P], F32)) for i in range(4)]
        self.wh = [mem.enter_context(nc.sbuf_tensor(f"wh_{tag}{i}", [P, ND, P], F32R)) for i in range(2)]
        self.wl = [mem.enter_context(nc.sbuf_tensor(f"wl_{tag}{i}", [P, ND, P], F32R)) for i in range(2)]
        self.s_w = [c.sem(f"w_{tag}{i}") for i in range(4)]
        self.s_hi, self.s_lo, self.s_pe, self.s_out = [c.sem(f"{n}_{tag}") for n in ("whi", "wlo", "prod", "stored")]

    @staticmethod
    def tiles(eng, body, n0, n1):
        n = n0
        while n < n1 and (n < 4 or n % 4):
            body(n, n % 4, n // 4 + 1)
            n += 1
        turns = (n1 - n) // 4
        if turns >= 2:
            with eng.Fori(0, turns) as i:
                for j in range(4):
                    body(i * 4 + (n + j), j, i + (n // 4 + 1))
            n += 4 * turns
        while n < n1:
            body(n, n % 4, n // 4 + 1)
            n += 1

    @staticmethod
    def early(n, k):
        return isinstance(n, int) and n < k

    def load(self, sp, n, r, fills, cols=P):
        if not self.early(n, 4):
            sp.wait_ge(self.s_lo, n - 3)
        sp.dma_start(self.stage[r][:, :, 0:cols], self.source(n)).then_inc(self.s_w[r], 16)

    def high(self, act, n, r, fills, cols=P):
        act.wait_ge(self.s_w[r], fills * 16)
        if not self.early(n, 2):
            act.wait_ge(self.s_pe, n - 1)
        self.nc.scalar.activation(self.wh[r % 2][:, :, 0:cols], self.stage[r][:, :, 0:cols], ACT.Copy)\
            .then_inc(self.s_hi, 1)

    def low(self, pool, n, r, fills, cols=P):
        pool.wait_ge(self.s_hi, n + 1)
        self.nc.gpsimd.tensor_tensor(self.wl[r % 2][:, :, 0:cols], self.stage[r][:, :, 0:cols],
                                     self.wh[r % 2][:, :, 0:cols].bitcast(F32), ALU.subtract).then_inc(self.s_lo, 1)

    def product(self, pe, ps, n, r, cols=P, part=(0, ND)):
        if part[0] == 0:
            pe.wait_ge(self.s_lo, n + 1)
            if not self.early(n, 2):
                pe.wait_ge(self.s_out, n - 1)
        for d in range(*part):
            last = three_pass(self.nc, ps[r % 2][0:cols, :], self.wh[r % 2][:, d, 0:cols], self.wl[r % 2][:, d, 0:cols],
                              self.c.XH[:, d, :], self.c.XL[:, d, :], d == 0, d == ND - 1)
        if part[1] == ND:
            last.then_inc(self.s_pe, 1)

    def keep(self, dve, ps, n, r, dst):
        dve.wait_ge(self.s_pe, n + 1)
        self.nc.vector.tensor_scalar(dst, ps, 1.0, None, ALU.mult).then_inc(self.s_out, 1)


def start(c, cols, x, gain_src, rel_bias, table):
    nc = c.nc
    with c.stage() as mem:
        gain = mem.enter_context(nc.sbuf_tensor("gain_mix", [P, D], F32))
        XN = c.MIX
        bank = [mem.enter_context(nc.psum_tensor(f"sb{i}", [P, SEQ], F32)) for i in range(4)]
        norm, flip = Norm(c, mem, "mix", gain[:]), Flip(c, "mix", XN, bank)
        s_x, s_g, s_t = [c.sem(f"x_loaded{t}") for t in range(NT)], c.sem("gain_loaded"), c.sem("table_loaded")
        s_eps, s_id = c.sem("eps_set"), c.sem("ident_steps")
        with nc.Block() as block:

            @block.sync
            def _(sp):
                for t in range(NT):
                    sp.dma_start(c.H[:, t, :], x[0, t * P:(t + 1) * P, :]).then_inc(s_x[t], 16)
                    if t == 0:
                        sp.dma_start(gain[:], gain_src).then_inc(s_g, 16)
                Columns.tiles(sp, lambda n, r, fills: cols.load(sp, n, r, fills), 0, 4)
                sp.dma_start(table, rel_bias.broadcast_to([P, ATT_HEADS, 2 * REL_CLIP + 1])).then_inc(s_t, 16)
                sp.wait_ge(s_t, 16)

            @block.gpsimd
            def _(pool):
                nc.gpsimd.memset(c.ident[:], 0.0).then_inc(s_id, 1)
                pool.wait_ge(s_id, 1)
                nc.gpsimd.affine_select(out=c.ident[:], in_=c.ident[:], compare_op=ALU.not_equal, fill=1.0, base=0,
                                        pattern=[[-1, P]], channel_multiplier=1).then_inc(s_id, 1)
                Columns.tiles(pool, lambda n, r, fills: cols.low(pool, n, r, fills), 0, 2)

            @block.tensor
            def _(pe):
                pe.wait_ge(s_id, 2)
                for t in range(NT):
                    pe.wait_ge(norm.s_xn, t + 1)
                    flip.transpose(pe, t)

            @block.scalar
            def _(act):
                for t in range(NT):
                    act.wait_ge(s_x[t], 16)
                    norm.square(act, t, XN[:, t, :])
                    if t == 0:
                        act.wait_ge(s_eps, 1)
                    norm.root(act, t, t + 1)
                for t in range(NT):
                    flip.high(act, t)
                    if t in (1, 2):
                        cols.high(act, t - 1, t - 1, 1)

            @block.vector
            def _(dve):
                nc.vector.memset(c.eps[:], EPS).then_inc(s_eps, 1)
                dve.wait_ge(s_g, 16)
                for t in range(NT + 1):
                    if t < NT:
                        norm.invert(dve, t, t + 1)
                        norm.scale(dve, t, XN[:, t, :])
                    if t >= 1:
                        flip.low(dve, t - 1)


N_TABLE = ATT_HEADS * (2 * REL_CLIP + 1)
ATT_TILES = 12
IN_TILES = NU_IN + 1
Z_TILE = 18


def in_unit(n):
    if isinstance(n, int) and not 4 <= n < ATT_TILES:
        return n + UAV if n < 4 else n - ATT_TILES - 1
    return n + (UAQ - 4)


def in_width(n):
    return RANK if isinstance(n, int) and n == ATT_TILES else P


def attention_inputs(c, cols, table):
    nc = c.nc
    W = 3 * P
    rows = nc.dram_tensor("rev_tables", (P, ATT_HEADS, W), F32, kind="Internal").ap()
    with c.stage() as mem:
        rev = c.TOK[:].rearrange("p t e -> p (t e)")[:, N_TABLE:N_TABLE + ATT_HEADS * W].rearrange(
            "p (h k) -> p h k", h=ATT_HEADS)
        ps = [mem.enter_context(nc.psum_tensor(f"pa{i}", [P, SEQ], F32)) for i in range(2)]
        s_rev, s_out, s_in = c.sem("table_reversed"), c.sem("table_stored"), c.sem("bias_loaded")
        with nc.Block() as block:

            @block.sync
            def _(sp):
                sp.wait_ge(s_rev, 3)
                sp.dma_start(rows, rev).then_inc(s_out, 16)
                sp.wait_ge(s_out, 16)
                src = bass.AP(tensor=rows.tensor, offset=P - 1, ap=[[ATT_HEADS * W - 1, P], [W, ATT_HEADS], [1, 2 * P]])
                sp.dma_start(c.BIAS[:], src).then_inc(s_in, 16)
                cols.tiles(sp, lambda n, r, fills: cols.load(sp, n, r, fills), 4, ATT_TILES)
                cols.tiles(sp, lambda n, r, fills: cols.load(sp, n, r, fills, in_width(n)), ATT_TILES, ATT_TILES + 4)

            @block.vector
            def _(dve):
                nc.vector.tensor_copy(rev[:, :, P - 1:W - 1], table[:, :, 2 * REL_CLIP:0:-1]).then_inc(s_rev, 1)
                nc.vector.tensor_copy(rev[:, :, 0:P - 1], table[:, :, 2 * REL_CLIP:2 * REL_CLIP + 1]
                                      .broadcast_to([P, ATT_HEADS, P - 1])).then_inc(s_rev, 1)
                nc.vector.tensor_copy(rev[:, :, W - 1:W], table[:, :, 0:1]).then_inc(s_rev, 1)
                cols.tiles(dve, lambda n, r, fills: cols.keep(dve, ps[r % 2][:], n, r, c.PROJ[:, bass.ds(
                    in_unit(n) * SEQ, SEQ)]), 0, ATT_TILES)

            @block.scalar
            def _(act):
                cols.tiles(act, lambda n, r, fills: cols.high(act, n, r, fills, in_width(n)), 2, ATT_TILES + 1)

            @block.gpsimd
            def _(pool):
                cols.tiles(pool, lambda n, r, fills: cols.low(pool, n, r, fills, in_width(n)), 2, ATT_TILES + 1)
                pool.wait_ge(s_in, 16)
                nc.gpsimd.memset(c.BIAS[0:CHUNK, :, P + CHUNK:2 * P], NEG)

            @block.tensor
            def _(pe):
                cols.tiles(pe, lambda n, r, fills: cols.product(pe, ps, n, r), 0, ATT_TILES)


class GateChain:

    def __init__(self, c, mem, ins):
        nc = c.nc
        NP = GLA_HEADS // 2

        def sb(name, shape):
            return mem.enter_context(nc.sbuf_tensor(name, shape, F32))

        self.nc, self.c, self.ins, self.NP = nc, c, ins, NP
        self.w2, self.b = sb("gate_w2", [RANK, GLA_HEADS * GLA_DK]), sb("gate_b", [P, NP])
        self.one = sb("one", [P, 1])
        self.starts = c.TOK[:, 1, 0:SEQ]
        self.dm = c.TOK[:, 0, 0:NP * SEQ].rearrange("p (m t) -> p m t", m=NP)
        self.q1, self.k1 = c.MIX[:, 0:NP, 0:SEQ], c.MIX[:, NP:2 * NP, 0:SEQ]
        self.k4, self.cum = [c.early[:, j, :].rearrange("p (m t) -> p m t", m=NP) for j in range(2)]
        self.s_in, self.s_set, self.s_z, self.s_abs, self.s_exp, self.s_min = [
            c.sem("chain_" + n) for n in ("loaded", "consts", "z", "abs", "exp", "min")]
        self.s_ln, self.s_g, self.s_cum, self.s_d, self.s_e, self.s_qk = [
            c.sem("chain_" + n) for n in ("ln", "log_gates", "sums", "diffs", "exps", "products")]

    @staticmethod
    def chunks(x):
        return x.rearrange("p (n c) -> p n c", c=CHUNK)

    def load(self, sp):
        sp.dma_start(self.w2[:], self.ins["gla_gate_w2"][0]).then_inc(self.s_in, 16)
        with self.nc.allow_non_contiguous_dma(reason="1 KiB of gate bias, once"):
            sp.dma_start(self.b[:], self.ins["gla_gate_b"][0].rearrange("(m p) -> p m", p=P)).then_inc(self.s_in, 16)

    def constants(self, pool):
        self.nc.gpsimd.memset(self.starts, 1.0).then_inc(self.s_set, 1)
        self.nc.gpsimd.memset(self.one[:], 1.0).then_inc(self.s_set, 1)
        pool.wait_ge(self.s_set, 2)
        self.nc.gpsimd.memset(self.chunks(self.starts)[:, :, 0:1], 0.0).then_inc(self.s_set, 1)

    def z(self, pe, m, out):
        if m == 0:
            pe.wait_ge(self.s_in, 32)
        self.nc.tensor.matmul(out, self.w2[:, m * P:(m + 1) * P], self.c.GLR[:], start=True,
                              stop=True).then_inc(self.s_z, 1)

    def magnitude(self, act, m, z):
        if m == 0:
            act.wait_ge(self.s_in, 32)
        act.wait_ge(self.s_z, m + 1)
        self.nc.scalar.activation(self.k1[:, m, :], z, ACT.Abs, bias=self.b[:, m:m + 1]).then_inc(self.s_abs, 1)

    def logarithm(self, act):
        act.wait_ge(self.s_abs, self.NP)
        self.nc.scalar.activation(self.k1, self.k1, ACT.Exp, scale=-1.0).then_inc(self.s_exp, 1)
        act.wait_ge(self.s_exp, 1)
        act.wait_ge(self.s_set, 3)
        self.nc.scalar.activation(self.k1, self.k1, ACT.Ln, bias=self.one[:]).then_inc(self.s_ln, 1)

    def minimum(self, dve, m, z):
        dve.wait_ge(self.s_abs, m + 1)
        self.nc.vector.tensor_scalar(self.q1[:, m, :], z, self.b[:, m:m + 1], 0.0, ALU.add, ALU.min).then_inc(self.s_min, 1)

    def sums(self, dve):
        dve.wait_ge(self.s_ln, 1)
        dve.wait_ge(self.s_min, self.NP)
        for m in range(self.NP):
            self.nc.vector.tensor_tensor(self.q1[:, m, :], self.q1[:, m, :], self.k1[:, m, :],
                                         ALU.subtract).then_inc(self.s_g, 1)
        dve.wait_ge(self.s_set, 3)
        for m in range(self.NP):
            dve.wait_ge(self.s_g, m + 1)
            self.nc.vector.tensor_tensor_scan(self.cum[:, m, :], self.starts, self.q1[:, m, :], 0.0, ALU.mult,
                                              ALU.add).then_inc(self.s_cum, 1)

    def differences(self, dve):
        dve.wait_ge(self.s_cum, self.NP)
        for m in range(self.NP):
            x = self.chunks(self.cum[:, m, :])
            self.nc.vector.tensor_tensor(self.chunks(self.dm[:, m, :]), x, x[:, :, CHUNK // 2:CHUNK // 2 + 1]
                                         .broadcast_to([P, NCH, CHUNK]), ALU.subtract).then_inc(self.s_d, 1)
            self.nc.vector.tensor_tensor(self.chunks(self.k4[:, m, :]), x[:, :, CHUNK - 1:CHUNK]
                                         .broadcast_to([P, NCH, CHUNK]), x, ALU.subtract).then_inc(self.s_d, 1)

    def exponentials(self, act):
        act.wait_ge(self.s_d, 2 * self.NP)
        for dst, src, sign in ((self.q1, self.dm, 1), (self.k1, self.dm, -1), (self.k4, self.k4, 1)):
            self.nc.scalar.activation(dst, src, ACT.Exp, scale=sign / GATE_NORM).then_inc(self.s_e, 1)

    def products(self, dve):
        Q, K = [self.c.PROJ[:, u * SEQ:(u + self.NP) * SEQ].rearrange("p (m t) -> p m t", m=self.NP) for u in (UQ, UK)]
        dve.wait_ge(self.s_e, 3)
        for m in range(self.NP):
            self.nc.vector.scalar_tensor_tensor(out=self.q1[:, m, :], in0=Q[:, m, :], scalar=GLA_DK ** -0.5,
                                                in1=self.q1[:, m, :], op0=ALU.mult, op1=ALU.mult).then_inc(self.s_qk, 1)
            self.nc.vector.tensor_tensor(self.k1[:, m, :], K[:, m, :], self.k1[:, m, :], ALU.mult).then_inc(self.s_qk, 1)
            self.nc.vector.tensor_tensor(self.k4[:, m, :], K[:, m, :], self.k4[:, m, :], ALU.mult).then_inc(self.s_qk, 1)


def gla(c, ins, chain):
    nc = c.nc
    NP = GLA_HEADS // 2
    with c.stage() as mem:
        def sb(name, shape, dt=F32):
            return mem.enter_context(nc.sbuf_tensor(name, shape, dt))

        q1, k1, k4, cum = chain.q1, chain.k1, chain.k4, chain.cum
        hn = sb("head_norm", [P, GLA_DV])
        q2 = sb("q2", [P, NP, SEQ])
        decay = sb("decay", [P, NP, NCH])
        KS = sb("KS", [P, NP, NT, P])
        AT = sb("AT", [P, GLA_HEADS, NT, P])
        SS = sb("states", [P, NP, NCH, 2 * GLA_DV])
        maskf = sb("maskf", [P, P])
        mask = sb("mask", [P, P], I32)
        ssq = sb("gla_ssq", [P, NT * GLA_HEADS])
        rms = sb("gla_rms", [P, NT * GLA_HEADS])
        rstd = sb("gla_rstd", [P, NT * GLA_HEADS])
        bank = [mem.enter_context(nc.psum_tensor(f"gb{i}", [P, SEQ], F32)) for i in range(8)]
        s_in, s_set, s_early = c.sem("gla_loaded"), c.sem("gla_consts"), c.sem("w_out_loaded")
        s_e, s_a, s_v = c.sem("gla_exps"), c.sem("gla_act"), c.sem("gla_dve")
        s_ks, s_kss, s_at, s_ats = c.sem("gla_kst"), c.sem("gla_ks"), c.sem("gla_scores"), c.sem("gla_masked")
        s_kv, s_s, s_o, s_sq, s_sr, s_silu = c.sem("gla_kv"), c.sem("gla_state"), c.sem("gla_o"), c.sem("gla_sq"), \
            c.sem("gla_rms"), c.sem("gla_silu")
        s_gg, s_m = c.sem("gla_gates_scaled"), c.sem("gla_out")
        s_tk, s_tka, s_tkd = c.sem("tok_flipped"), c.sem("tok_kept_act"), c.sem("tok_kept_dve")
        tok_units = [UV + i for i in range(4)] + [UG + i for i in range(4)]

        def tok_bank(j):
            return bank[(0, 1, 2, 3, 6, 7, 0, 1)[j]]

        def tok_dst(j):
            return c.TOK[:, :, j * P:(j + 1) * P], tok_bank(j)[:].rearrange("p (t e) -> p t e", t=NT)

        def o_head(t, h):
            return bank[t + NT * (h % 2)][:, (h // 2) * GLA_DV:(h // 2 + 1) * GLA_DV]

        def chunks(x):
            return x.rearrange("p (n c) -> p n c", c=CHUNK)

        with nc.Block() as block:

            @block.sync
            def _(sp):
                sp.dma_start(hn[:], ins["gla_head_norm"].broadcast_to([P, GLA_DV])).then_inc(s_in, 16)
                sp.wait_ge(s_e, 1)
                sp.wait_ge(s_a, NP)
                sp.wait_ge(s_ks, NP)
                for n in range(2):
                    sp.dma_start(c.early[:, n, :].rearrange("p (k n) -> p k n", k=2),
                                 RowWeights.unit(ins["w_out"][0], n)).then_inc(s_early, 16)
                sp.wait_ge(s_early, 32)

            @block.gpsimd
            def _(pool):
                nc.gpsimd.memset(maskf[:], 1.0).then_inc(s_set, 1)
                nc.gpsimd.memset(AT[:], 0.0).then_inc(s_set, 1)
                for m in range(NP):
                    nc.gpsimd.memset(SS[:, m, 0, :], 0.0).then_inc(s_set, 1)
                pool.wait_ge(s_set, 2 + NP)
                nc.gpsimd.affine_select(out=maskf[:], in_=maskf[:], compare_op=ALU.is_ge, fill=0.0, base=0,
                                        pattern=[[1, P]], channel_multiplier=-1).then_inc(s_set, 1)
                pool.wait_ge(s_set, 3 + NP)
                nc.gpsimd.memset(maskf[0:CHUNK, CHUNK:P], 0.0).then_inc(s_set, 1)
                pool.wait_ge(s_in, 16)
                pool.wait_ge(s_silu, 1)
                W = GLA_HEADS * GLA_DV
                for t in range(NT):
                    g = c.TOK[:, t, W:2 * W].rearrange("p (h e) -> p h e", e=GLA_DV)
                    nc.gpsimd.tensor_tensor(g, g, hn[:].unsqueeze(1).broadcast_to([P, GLA_HEADS, GLA_DV]),
                                            ALU.mult).then_inc(s_gg, 1)

            ALL_SET = 4 + NP

            @block.tensor
            def _(pe):
                def as_rows(j):
                    if j == 6:
                        pe.wait_ge(s_tka, 1)
                    if j == 7:
                        pe.wait_ge(s_tkd, 1)
                    for t in range(NT):
                        a = tok_units[j] * SEQ + t * P
                        last = nc.tensor.transpose(tok_bank(j)[:, t * P:(t + 1) * P], c.PROJ[:, a:a + P], c.ident[:])
                    last.then_inc(s_tk, 1)

                for j in range(8):
                    as_rows(j)
                pe.wait_ge(s_tka, 4)
                pe.wait_ge(s_tkd, 4)
                for h in range(GLA_HEADS):
                    m, r = h // 2, GLA_DK * (h % 2)
                    for t in range(NT):
                        last = nc.tensor.matmul(bank[h][:, t * P:(t + 1) * P], k1[r:r + GLA_DK, m, t * P:(t + 1) * P],
                                                q1[r:r + GLA_DK, m, t * P:(t + 1) * P], start=True, stop=True)
                    last.then_inc(s_at, 1)
                for m in range(NP):
                    for t in range(NT):
                        last = nc.tensor.transpose(bank[6 + m][:, t * P:(t + 1) * P], k4[:, m, t * P:(t + 1) * P],
                                                   c.ident[:])
                    last.then_inc(s_ks, 1)
                pe.wait_ge(s_kss, NP)
                for n in range(NCH - 1):
                    for m in range(NP):
                        i = n * NP + m
                        if i >= 4:
                            pe.wait_ge(s_s, i - 3)
                        rows = slice(CHUNK * (n % 2), CHUNK * (n % 2) + CHUNK)
                        nc.tensor.matmul(bank[4 + i % 4][:, 0:2 * GLA_DV], KS[rows, m, n // 2, :],
                                         c.TOK[rows, n // 2, m * 2 * GLA_DV:(m + 1) * 2 * GLA_DV],
                                         start=True, stop=True).then_inc(s_kv, 1)
                pe.wait_ge(s_ats, GLA_HEADS)
                pe.wait_ge(s_s, NP * (NCH - 1))
                for t in range(NT):
                    for h in range(GLA_HEADS):
                        m, r = h // 2, GLA_DK * (h % 2)
                        o = bank[t + NT * (h % 2)]
                        cols = slice(m * GLA_DV, (m + 1) * GLA_DV)
                        nc.tensor.matmul(o[:, cols], AT[:, h, t, :], c.TOK[:, t, h * GLA_DV:(h + 1) * GLA_DV],
                                         start=True, stop=False, skip_group_check=True)
                        for half in range(2):
                            n = 2 * t + half
                            rows = slice(CHUNK * half, CHUNK * half + CHUNK)
                            last = nc.tensor.matmul(
                                o[rows, cols], q2[r:r + GLA_DK, m, n * CHUNK:(n + 1) * CHUNK],
                                SS[r:r + GLA_DK, m, n, (h % 2) * GLA_DV:(h % 2 + 1) * GLA_DV],
                                start=False, stop=True, skip_group_check=True)
                    last.then_inc(s_o, 1)

            @block.scalar
            def _(act):
                ch = Chain(act, s_a)
                for j in range(0, 8, 2):
                    act.wait_ge(s_tk, j + 1)
                    dst, src = tok_dst(j)
                    nc.scalar.activation(dst, src, ACT.Copy).then_inc(s_tka, 1)
                g = 1.0 / GATE_NORM
                nc.scalar.activation(q2[:], cum, ACT.Exp, scale=g).then_inc(s_e, 1)
                for m in range(NP):
                    ch.step(nc.scalar.activation(decay[:, m, :], chunks(cum[:, m, :])[:, :, CHUNK - 1], ACT.Exp, scale=g))
                gates = c.TOK[:, :, GLA_HEADS * GLA_DV:2 * GLA_HEADS * GLA_DV]
                act.wait_ge(s_tka, 4)
                act.wait_ge(s_tkd, 4)
                nc.scalar.activation(gates, gates, ACT.Silu).then_inc(s_silu, 1)
                for t in range(NT):
                    act.wait_ge(s_o, t + 1)
                    for h in range(GLA_HEADS):
                        nc.scalar.activation(c.MIX[:, t, h * GLA_DV:(h + 1) * GLA_DV], o_head(t, h), ACT.Square,
                                             accum_out=ssq[:, t * GLA_HEADS + h:t * GLA_HEADS + h + 1]).then_inc(s_sq, 1)
                    act.wait_ge(s_sq, (t + 1) * GLA_HEADS)
                    heads = slice(t * GLA_HEADS, (t + 1) * GLA_HEADS)
                    nc.scalar.activation(rms[:, heads], ssq[:, heads], ACT.Sqrt, scale=1.0 / GLA_DV,
                                         bias=c.eps[:]).then_inc(s_sr, 1)

            @block.vector
            def _(dve):
                ch = Chain(dve, s_v)
                dve.wait_ge(s_set, ALL_SET)
                ch.step(nc.vector.tensor_copy(mask[:], maskf[:]))
                for j in range(1, 8, 2):
                    dve.wait_ge(s_tk, j + 1)
                    dst, src = tok_dst(j)
                    nc.vector.tensor_copy(dst, src).then_inc(s_tkd, 1)
                Q = c.PROJ[:, UQ * SEQ:(UQ + NP) * SEQ].rearrange("p (m t) -> p m t", m=NP)
                scale = GLA_DK ** -0.5
                dve.wait_ge(s_e, 1)
                for m in range(NP):
                    ch.step(nc.vector.scalar_tensor_tensor(out=q2[:, m, :], in0=Q[:, m, :], scalar=scale,
                                                           in1=q2[:, m, :], op0=ALU.mult, op1=ALU.mult))
                for h in range(GLA_HEADS):
                    dve.wait_ge(s_at, h + 1)
                    if h == 0:
                        ch.wait()
                    nc.vector.copy_predicated(AT[:, h, :, :], mask[:].unsqueeze(1).broadcast_to([P, NT, P]),
                                              bank[h][:].rearrange("p (t i) -> p t i", t=NT)).then_inc(s_ats, 1)
                for m in range(NP):
                    dve.wait_ge(s_ks, m + 1)
                    nc.vector.tensor_copy(KS[:, m, :, :], bank[6 + m][:].rearrange("p (t i) -> p t i", t=NT)).then_inc(s_kss, 1)
                dve.wait_ge(s_a, NP)
                for n in range(NCH - 1):
                    for m in range(NP):
                        i = n * NP + m
                        dve.wait_ge(s_kv, i + 1)
                        if n:
                            dve.wait_ge(s_s, i - 1)
                        nc.vector.scalar_tensor_tensor(
                            out=SS[:, m, n + 1, :], in0=SS[:, m, n, :], scalar=decay[:, m, n:n + 1],
                            in1=bank[4 + i % 4][:, 0:2 * GLA_DV], op0=ALU.mult, op1=ALU.add).then_inc(s_s, 1)
                W = GLA_HEADS * GLA_DV
                for t in range(NT):
                    heads = slice(t * GLA_HEADS, (t + 1) * GLA_HEADS)
                    dve.wait_ge(s_sr, t + 1)
                    ch.step(nc.vector.reciprocal(rstd[:, heads], rms[:, heads]))
                    ch.wait()
                    dve.wait_ge(s_gg, t + 1)
                    for h in range(GLA_HEADS):
                        cols = slice(h * GLA_DV, (h + 1) * GLA_DV)
                        nc.vector.scalar_tensor_tensor(
                            out=c.MIX[:, t, cols], in0=o_head(t, h), scalar=rstd[:, t * GLA_HEADS + h:t * GLA_HEADS + h + 1],
                            in1=c.TOK[:, t, W + h * GLA_DV:W + (h + 1) * GLA_DV], op0=ALU.mult,
                            op1=ALU.mult).then_inc(s_m, 1)


def band_attention(c, cols, chain):
    nc = c.nc
    steps = [(t, h) for t in range(NT) for h in range(ATT_HEADS)]
    N = len(steps)
    scale = ATT_DH ** -0.5
    V0 = 2 * GLA_HEADS * GLA_DV
    with c.stage() as mem:
        def sb(name, shape, dt=F32):
            return mem.enter_context(nc.sbuf_tensor(name, shape, dt))

        sc = [sb(f"att_sc{i}", [P, SEQ]) for i in range(2)]
        pr = [sb(f"att_p{i}", [P, SEQ]) for i in range(2)]
        pt = [sb(f"att_pt{i}", [P, SEQ]) for i in range(2)]
        nmax = sb("att_nmax", [P, N])
        rsum = sb("att_rsum", [P, N])
        rinv = sb("att_rinv", [P, N])
        ps_s = [mem.enter_context(nc.psum_tensor(f"as{i}", [P, SEQ], F32)) for i in range(2)]
        ps_t = [mem.enter_context(nc.psum_tensor(f"at{i}", [P, SEQ], F32)) for i in range(2)]
        ps_o = [mem.enter_context(nc.psum_tensor(f"ao{i}", [P, SEQ], F32)) for i in range(2)]
        s_qk, s_sc, s_mx, s_p, s_pt, s_pts = (c.sem("att_" + n) for n in ("qk", "biased", "max", "exp", "ptr", "pts"))
        s_pv, s_o, s_ri = (c.sem("att_" + n) for n in ("pv", "out", "rinv"))
        s_vt, s_vk = c.sem("att_v_flipped"), c.sem("att_v_kept")
        ps_p = [mem.enter_context(nc.psum_tensor(f"ap{i}", [P, SEQ], F32)) for i in range(2)]
        halves = 2 * (IN_TILES - ATT_TILES)

        def work(i):
            a, b = [min(k, N) * halves // N for k in (i, i + 1)]
            return [(ATT_TILES + k // 2, k % 2) for k in range(a, b)]

        def ordinal(i):
            return i - next(k for k in range(N) if (Z_TILE, 0) in work(k))

        with nc.Block() as block:

            @block.tensor
            def _(pe):
                def scores(i):
                    t, h = steps[i]
                    r = ATT_DH * (h % 2)
                    q0 = (UAQ + h // 2) * SEQ + t * P
                    k0 = (UAK + h // 2) * SEQ
                    if i >= 2:
                        pe.wait_ge(s_sc, 2 * (i - 1))
                    nc.tensor.matmul(ps_s[i % 2][:, 0:(t + 1) * P], c.PROJ[r:r + ATT_DH, q0:q0 + P],
                                     c.PROJ[r:r + ATT_DH, k0:k0 + (t + 1) * P], start=True, stop=True).then_inc(s_qk, 1)

                def flip(i):
                    t, h = steps[i]
                    pe.wait_ge(s_p, i + 1)
                    if i >= 2:
                        pe.wait_ge(s_pts, i - 1)
                    for k in range(t + 1):
                        last = nc.tensor.transpose(ps_t[i % 2][:, k * P:(k + 1) * P], pr[i % 2][:, k * P:(k + 1) * P],
                                                   c.ident[:])
                    last.then_inc(s_pt, 1)

                def values(i):
                    t, h = steps[i]
                    pe.wait_ge(s_pts, i + 1)
                    if h == 0 and t >= 2:
                        pe.wait_ge(s_o, t - 1)
                    for k in range(t + 1):
                        last = nc.tensor.matmul(ps_o[t % 2][:, h * ATT_DH:(h + 1) * ATT_DH], pt[i % 2][:, k * P:(k + 1) * P],
                                                c.TOK[:, k, V0 + h * ATT_DH:V0 + (h + 1) * ATT_DH],
                                                start=(k == 0), stop=(k == t))
                    last.then_inc(s_pv, 1)

                for j in range(4):
                    for t in range(NT):
                        a = (UAV + j) * SEQ + t * P
                        last = nc.tensor.transpose((ps_t + ps_o)[j][:, t * P:(t + 1) * P], c.PROJ[:, a:a + P], c.ident[:])
                    last.then_inc(s_vt, 1)
                for i in range(N + 2):
                    if i < N:
                        scores(i)
                    if ordinal(i) == 0:
                        pe.wait_ge(cols.s_out, Z_TILE)
                        for m in range(2):
                            chain.z(pe, m, ps_p[(Z_TILE + m) % 2][:])
                    for n, half in work(i):
                        if half == 0 and n in (Z_TILE, Z_TILE + 1):
                            pe.wait_ge(chain.s_min, n - Z_TILE + 1)
                        cols.product(pe, ps_p, n, n % 4, in_width(n), (half * ND // 2, (half + 1) * ND // 2))
                    if i == 1:
                        pe.wait_ge(s_vk, 4)
                    if 0 <= i - 1 < N:
                        flip(i - 1)
                    if i - 2 >= 0:
                        values(i - 2)

            @block.vector
            def _(dve):
                def biased(i):
                    t, h = steps[i]
                    dve.wait_ge(s_qk, i + 1)
                    if i >= 2:
                        dve.wait_ge(s_p, i - 1)
                    far = max(0, (t - 1) * P)
                    n = (t + 1) * P - far
                    if far:
                        nc.vector.tensor_scalar(sc[i % 2][:, 0:far], ps_s[i % 2][:, 0:far], scale, c.BIAS[:, h, 0:1],
                                                ALU.mult, ALU.add).then_inc(s_sc, 1)
                    nc.vector.scalar_tensor_tensor(
                        out=sc[i % 2][:, far:far + n], in0=ps_s[i % 2][:, far:far + n], scalar=scale,
                        in1=c.BIAS[:, h, 2 * P - n:2 * P], op0=ALU.mult, op1=ALU.add).then_inc(s_sc, 1 if far else 2)
                    dve.wait_ge(s_sc, 2 * (i + 1))
                    nc.vector.tensor_reduce(nmax[:, i:i + 1], sc[i % 2][:, 0:far + n], AX.X, ALU.max,
                                            negate=True).then_inc(s_mx, 1)

                def keep(i):
                    t, h = steps[i]
                    dve.wait_ge(s_pt, i + 1)
                    if i >= 2:
                        dve.wait_ge(s_pv, i - 1)
                    nc.vector.tensor_copy(pt[i % 2][:, 0:(t + 1) * P], ps_t[i % 2][:, 0:(t + 1) * P]).then_inc(s_pts, 1)

                def output(t):
                    a = t * ATT_HEADS
                    dve.wait_ge(s_p, a + ATT_HEADS)
                    nc.vector.reciprocal(rinv[:, a:a + ATT_HEADS], rsum[:, a:a + ATT_HEADS]).then_inc(s_ri, 1)
                    dve.wait_ge(s_ri, t + 1)
                    dve.wait_ge(s_pv, a + ATT_HEADS)
                    nc.vector.tensor_tensor(
                        c.MIX[:, t, SEQ:2 * SEQ].rearrange("p (h e) -> p h e", e=ATT_DH),
                        ps_o[t % 2][:].rearrange("p (h e) -> p h e", e=ATT_DH),
                        rinv[:, a:a + ATT_HEADS].unsqueeze(2).broadcast_to([P, ATT_HEADS, ATT_DH]),
                        ALU.mult).then_inc(s_o, 1)

                for j in range(4):
                    dve.wait_ge(s_vt, j + 1)
                    nc.vector.tensor_copy(c.TOK[:, :, V0 + j * P:V0 + (j + 1) * P],
                                          (ps_t + ps_o)[j][:].rearrange("p (t e) -> p t e", t=NT)).then_inc(s_vk, 1)
                for i in range(N + 3):
                    if i < N:
                        biased(i)
                    if ordinal(i) == 0:
                        for m in range(2):
                            chain.minimum(dve, m, ps_p[(Z_TILE + m) % 2][:])
                    if 0 <= i - 1 < N:
                        keep(i - 1)
                    if ordinal(i) == 2:
                        chain.sums(dve)
                    if ordinal(i) == 3:
                        chain.differences(dve)
                    if ordinal(i) == 6:
                        chain.products(dve)
                    for n, half in work(i):
                        if half == 1:
                            rank = n == ATT_TILES
                            dst = c.GLR[:] if rank else c.PROJ[:, in_unit(n) * SEQ:(in_unit(n) + 1) * SEQ]
                            cols.keep(dve, ps_p[n % 2][0:in_width(n), :], n, n % 4, dst)
                    if i - 2 >= 0 and (i - 2) % ATT_HEADS == ATT_HEADS - 1 and i - 2 < N:
                        output((i - 2) // ATT_HEADS)

            @block.scalar
            def _(act):
                n = ATT_TILES + 1
                cols.high(act, n, n % 4, n // 4 + 1)
                for i, (t, h) in enumerate(steps):
                    act.wait_ge(s_mx, i + 1)
                    if i >= 2:
                        act.wait_ge(s_pt, i - 1)
                    nc.scalar.activation(pr[i % 2][:, 0:(t + 1) * P], sc[i % 2][:, 0:(t + 1) * P], ACT.Exp,
                                         bias=nmax[:, i:i + 1], accum_out=rsum[:, i:i + 1]).then_inc(s_p, 1)
                    if ordinal(i) == 0:
                        for m in range(2):
                            chain.magnitude(act, m, ps_p[(Z_TILE + m) % 2][:])
                        chain.logarithm(act)
                    if ordinal(i) == 5:
                        chain.exponentials(act)
                    for n, half in work(i):
                        if half == 1 and n + 2 < IN_TILES:
                            cols.high(act, n + 2, (n + 2) % 4, (n + 2) // 4 + 1, in_width(n + 2))

            @block.gpsimd
            def _(pool):
                chain.constants(pool)
                for n in range(ATT_TILES + 1, IN_TILES):
                    cols.low(pool, n, n % 4, n // 4 + 1, in_width(n))

            @block.sync
            def _(sp):
                chain.load(sp)
                for n in range(ATT_TILES + 4, IN_TILES):
                    cols.load(sp, n, n % 4, n // 4 + 1, in_width(n))


def mixer_output(c, w_out, gain_src, cols):
    nc = c.nc
    HALF = D // 2
    with c.stage() as mem:
        gain = mem.enter_context(nc.sbuf_tensor("gain_ffn", [P, D], F32))
        bank = [mem.enter_context(nc.psum_tensor(f"mb{i}", [P, SEQ], F32)) for i in range(8)]
        staging = [c.early[:, j, :] for j in range(2)] + [c.SC[:, j].rearrange("p u n -> p (u n)")[:, 0:D] for j in range(2)]
        mixed, flip, norm = Flip(c, "att", c.MIX, bank[0:4]), Flip(c, "ffn", c.MIX, bank[4:8]), \
            Norm(c, mem, "ffn", gain[:])
        w = RowWeights(c, mem, "out", w_out, staging, loaded=2, by_vector=(1, 3))
        s_g, s_o, s_add = c.sem("gain_ffn_loaded"), c.sem("out_made"), c.sem("out_added")
        units = [(half, t) for half in range(2) for t in range(NT)]

        def o_bank(n):
            return bank[(n + 4) % 8][:]

        with nc.Block() as block:

            @block.sync
            def _(sp):
                for n in range(2, 4):
                    w.load(sp, n)
                sp.dma_start(gain[:], gain_src).then_inc(s_g, 16)
                for n in range(4, w.N):
                    w.load(sp, n)
                cols.tiles(sp, lambda n, r, fills: cols.load(sp, n, r, fills), 0, 4)

            @block.tensor
            def _(pe):
                mixed.transpose(pe, 0)
                mixed.transpose(pe, 1)
                for n, (half, t) in enumerate(units):
                    if half == 0:
                        pe.wait_ge(mixed.s_lo, 2 * t + 2)
                    w.product(pe, c, o_bank(n), half, t, s_o)
                    if n < 2:
                        mixed.transpose(pe, n + 2)
                for t in range(NT):
                    pe.wait_ge(norm.s_xn, t + 1)
                    flip.transpose(pe, t)

            @block.scalar
            def _(act):
                w.high(act, 0)
                mixed.high(act, 0)
                w.high(act, 1)
                mixed.high(act, 1)
                w.high(act, 2)
                w.high(act, 3)
                mixed.high(act, 2)
                mixed.high(act, 3)
                for n in range(4, w.N):
                    w.high(act, n)
                cols.tiles(act, lambda n, r, fills: cols.high(act, n, r, fills), 0, 2)
                for t in range(NT):
                    act.wait_ge(s_add, NT + t + 1)
                    norm.square(act, t, c.MIX[:, t, :])
                    norm.root(act, t, t + 1)
                for t in range(NT):
                    flip.high(act, t)

            @block.gpsimd
            def _(pool):
                for n in range(w.N):
                    if n not in w.by_vector:
                        w.low(pool, n)
                cols.tiles(pool, lambda n, r, fills: cols.low(pool, n, r, fills), 0, 2)

            @block.vector
            def _(dve):
                mixed.low(dve, 0)
                w.low_by_vector(dve, 1)
                mixed.low(dve, 1)
                w.low_by_vector(dve, 3)
                mixed.low(dve, 2)
                mixed.low(dve, 3)
                def scaled(t):
                    norm.invert(dve, t, t + 1)
                    norm.scale(dve, t, c.MIX[:, t, :])

                for n, (half, t) in enumerate(units):
                    if n == NT + 1:
                        dve.wait_ge(s_g, 16)
                    dve.wait_ge(s_o, n + 1)
                    h = c.H[:, t, half * HALF:(half + 1) * HALF]
                    nc.vector.tensor_tensor(h, h, o_bank(n), ALU.add).then_inc(s_add, 1)
                    if n > NT:
                        scaled(t - 1)
                scaled(NT - 1)
                for t in range(NT):
                    flip.low(dve, t)


def queries(c, cols, subkeys, kt):
    nc = c.nc
    U, G = 2 * PH, PH // 2
    with c.stage() as mem:
        keys = mem.enter_context(nc.sbuf_tensor("keys", [P, U, P], F32))
        ps = [mem.enter_context(nc.psum_tensor(f"pq{i}", [P, SEQ], F32)) for i in range(2)]
        pk = [mem.enter_context(nc.psum_tensor(f"pk{i}", [P, SEQ], F32)) for i in range(G)]
        s_k, s_tr, s_kt = c.sem("keys_loaded"), c.sem("keys_flipped"), c.sem("keys_copied")
        with nc.Block() as block:

            @block.sync
            def _(sp):
                sp.dma_start(keys[:], subkeys.rearrange("h s n d -> n (h s) d")).then_inc(s_k, 16)
                cols.tiles(sp, lambda n, r, fills: cols.load(sp, n, r, fills), 4, U)

            @block.tensor
            def _(pe):
                cols.tiles(pe, lambda n, r, fills: cols.product(pe, ps, n, r), 0, U)
                pe.wait_ge(s_k, 16)
                for g in range(G):
                    for j in range(4):
                        last = nc.tensor.transpose(pk[g][:, j * P:(j + 1) * P], keys[:, 4 * g + j, :], c.ident[:])
                    last.then_inc(s_tr, 1)

            @block.scalar
            def _(act):
                cols.tiles(act, lambda n, r, fills: cols.high(act, n, r, fills), 2, U)
                for g in range(G):
                    act.wait_ge(s_tr, g + 1)
                    nc.scalar.activation(kt[:, g * SEQ:(g + 1) * SEQ], pk[g][:], ACT.Copy).then_inc(s_kt, 1)

            @block.gpsimd
            def _(pool):
                cols.tiles(pool, lambda n, r, fills: cols.low(pool, n, r, fills), 2, U)

            @block.vector
            def _(dve):
                cols.tiles(dve, lambda n, r, fills: cols.keep(dve, ps[r % 2][:], n, r,
                                                              c.Q[:, bass.ds(n * SEQ, SEQ)]), 0, U)


def key_scores(c, kt, u_tab):
    nc = c.nc
    U = 2 * PH
    with c.stage() as mem:
        ps = [mem.enter_context(nc.psum_tensor(f"ks{i}", [P, SEQ], F32)) for i in range(8)]
        s_sc, s_st, s_u = c.sem("scores"), [c.sem("scores_even"), c.sem("scores_odd")], c.sem("first_u_loaded")
        with nc.Block() as block:

            @block.sync
            def _(sp):
                sp.dma_start(c.early[:], u_tab[0:2 * P, :].rearrange("(j p) d -> p j d", p=P)).then_inc(s_u, 16)
                sp.wait_ge(s_u, 16)

            @block.tensor
            def _(pe):
                for u in range(U):
                    if u >= 8:
                        pe.wait_ge(s_st[u % 2], (u - 8) // 2 + 1)
                    for t in range(NT):
                        last = nc.tensor.matmul(ps[u % 8][:, t * P:(t + 1) * P],
                                                c.Q[:, u * SEQ + t * P:u * SEQ + (t + 1) * P],
                                                kt[:, u * P:(u + 1) * P], start=True, stop=True)
                    last.then_inc(s_sc, 1)

            @block.scalar
            def _(act):
                for u in range(0, U, 2):
                    act.wait_ge(s_sc, u + 1)
                    nc.scalar.activation(c.SC[:, :, u, :], ps[u % 8][:].rearrange("p (t n) -> p t n", t=NT),
                                         ACT.Copy).then_inc(s_st[0], 1)

            @block.vector
            def _(dve):
                for u in range(1, U, 2):
                    dve.wait_ge(s_sc, u + 1)
                    nc.vector.tensor_copy(c.SC[:, :, u, :],
                                          ps[u % 8][:].rearrange("p (t n) -> p t n", t=NT)).then_inc(s_st[1], 1)


class Ahead:

    def __init__(self, c, mem, u_tab, count):
        nc = c.nc

        def sb(name, shape, dt=F32):
            return [mem.enter_context(nc.sbuf_tensor(f"{name}{j}", shape, dt)) for j in range(2)]

        def sem(name):
            return c.ctx.enter_context(nc.semaphore(name))

        self.nc, self.c, self.u_tab, self.count = nc, c, u_tab, count
        self.ust = [c.early[:, j, :] for j in range(2)]
        self.ut, self.gel = sb("au_t", [P, ND, P]), sb("a_gelu", [P, SEQ])
        self.uh, self.ul = sb("au_hi", [P, ND, P], F32R), sb("au_lo", [P, ND, P], F32R)
        self.tr = [mem.enter_context(nc.psum_tensor(f"a_tr{k}", [P, 4, P], F32)) for k in range(2)]
        self.pa = [mem.enter_context(nc.psum_tensor(f"a_acts{j}", [P, SEQ], F32)) for j in range(2)]
        self.s_u, self.s_st = [sem("a_u_loaded0"), sem("a_u_loaded1")], [sem("a_put_aside0"), sem("a_put_aside1")]
        self.s_tr, self.s_hi, self.s_lo = sem("a_transposed"), sem("a_high"), sem("a_low")
        self.s_act, self.s_gelu = sem("a_acts"), sem("a_gelu")

    def load(self, sp, h, j):
        sp.wait_ge(self.s_tr, h * 2 + (j - 1))
        sp.dma_start(self.ust[j][:], self.u_tab[bass.ds(h * (2 * P) + j * P, P), :]).then_inc(self.s_u[j], 16)

    def flip(self, pe, h, j, first=False):
        if not first:
            pe.wait_ge(self.s_u[j], h * 16)
        if not (first and j == 0):
            pe.wait_ge(self.s_hi, h * 2 + j)
        for k in range(2):
            for d in range(4):
                a = (4 * k + d) * P
                last = self.nc.tensor.transpose(self.tr[k][:, d, :], self.ust[j][:, a:a + P], self.c.ident[:])
        last.then_inc(self.s_tr, 1)

    def acts(self, pe, h, j, first=False):
        pe.wait_ge(self.s_lo, h * 2 + (j + 1))
        if not first:
            pe.wait_ge(self.s_gelu, h * 2 + (j - 1))
        for d in range(ND):
            last = three_pass(self.nc, self.pa[j][:], self.uh[j][:, d, :], self.ul[j][:, d, :], self.c.XH[:, d, :],
                              self.c.XL[:, d, :], d == 0, d == ND - 1)
        last.then_inc(self.s_act, 1)

    def high(self, act, h, j, first=False):
        act.wait_ge(self.s_tr, h * 2 + (j + 1))
        if not first:
            act.wait_ge(self.s_act, h * 2 + (j - 1))
        for k in range(2):
            self.nc.scalar.activation(self.ut[j][:, 4 * k:4 * k + 4, :], self.tr[k][:], ACT.Copy)
            last = self.nc.scalar.activation(self.uh[j][:, 4 * k:4 * k + 4, :], self.tr[k][:], ACT.Copy)
        last.then_inc(self.s_hi, 1)

    def gelu(self, act, h, j, first=False):
        act.wait_ge(self.s_act, h * 2 + (j + 1))
        if not first:
            act.wait_ge(self.s_st[j], h * 16)
        self.nc.scalar.activation(self.gel[j][:], self.pa[j][:], ACT.Gelu).then_inc(self.s_gelu, 1)

    def low(self, pool, h, j):
        pool.wait_ge(self.s_hi, h * 2 + (j + 1))
        self.nc.gpsimd.tensor_tensor(self.ul[j][:], self.ut[j][:], self.uh[j][:].bitcast(F32),
                                     ALU.subtract).then_inc(self.s_lo, 1)

    def put_aside(self, sp, h, j):
        sp.wait_ge(self.s_gelu, h * 2 + (j + 1))
        sp.dma_start(self.c.aside[bass.ds(h * 2 + j, 1)].rearrange("a p t -> p (a t)"),
                     self.gel[j][:]).then_inc(self.s_st[j], 16)

    def sync_step(self, sp, h, final=False):
        for j in range(2):
            if not final:
                self.load(sp, h + 1, j)
            self.put_aside(sp, h, j)

    def tensor_step(self, pe, h, first=False, final=False):
        self.flip(pe, h, 1, first)
        self.acts(pe, h, 0, first)
        if not final:
            self.flip(pe, h + 1, 0)
        self.acts(pe, h, 1, first)

    def scalar_step(self, act, h, first=False, final=False):
        self.high(act, h, 1, first)
        self.gelu(act, h, 0, first)
        if not final:
            self.high(act, h + 1, 0)
        self.gelu(act, h, 1, first)

    def pool_step(self, pool, h):
        self.low(pool, h, 0)
        self.low(pool, h, 1)


def select_experts(c, ahead, steps):
    nc = c.nc
    U, NPAIR = 2 * PH, PH * TOPK
    runs, off = [], 0
    for a, n in CAND:
        if runs and runs[-1][2] == n:
            runs[-1][1] += 1
        else:
            runs.append([a, 1, n, off])
        off += n
    with c.stage() as mem:
        def sb(name, shape, dt=F32):
            return mem.enter_context(nc.sbuf_tensor(name, shape, dt))

        rest = sb("rest", [P, U, NKEYS])
        top = sb("top", [P, U, TOPK])
        idx = sb("idx", [P, U, TOPK], U32)
        idxf = sb("idxf", [P, U, TOPK])
        cv = sb("cand_values", [P, PH, NCAND])
        cr = sb("cand_rest", [P, PH, NCAND])
        ce = sb("cand_experts", [P, PH, NCAND])
        best = sb("best", [P, PH, TOPK])
        pos = sb("pos", [P, PH, TOPK], U32)
        posf = sb("posf", [P, PH, TOPK])
        iota = sb("iota_cand", [P, NCAND])
        hit = sb("hit", [P, PH, TOPK, NCAND])
        ex = sb("exp_gate", [P, NT, PH, TOPK])
        esum = sb("exp_sum", [P, NT * PH])
        gate = sb("gate", [P, NT, NPAIR])
        expert = sb("expert", [P, NT, NPAIR])
        e_int = sb("expert_int", [P, NT, NPAIR], I32)
        part = [sb(f"expert_part{i}", [P, NT, NPAIR], I32) for i in range(2)]
        partf = [sb(f"expert_partf{i}", [P, NT, NPAIR]) for i in range(2)]
        ps = [mem.enter_context(nc.psum_tensor(f"se{i}", [P, SEQ], F32)) for i in range(3)]
        s_iota, s_v, s_d, s_ex = c.sem("iota_cand_set"), c.sem("select_dve"), c.sem("gate_diffs"), c.sem("gate_exps")
        s_tr = c.sem("pairs_tr")
        with nc.Block() as block:

            @block.gpsimd
            def _(pool):
                nc.gpsimd.iota(iota[:], [[1, NCAND]], base=0, channel_multiplier=0,
                               allow_small_or_imprecise_dtypes=True).then_inc(s_iota, 1)
                with pool.Fori(0, steps) as i:
                    ahead.pool_step(pool, i)

            @block.sync
            def _(sp):
                with sp.Fori(0, steps) as i:
                    ahead.sync_step(sp, i)

            @block.scalar
            def _(act):
                ahead.high(act, 0, 0, True)
                ahead.scalar_step(act, 0, first=True)
                with act.Fori(1, steps - 1) as i:
                    ahead.scalar_step(act, i)
                act.wait_ge(s_d, NT)
                nc.scalar.activation(ex[:], ex[:], ACT.Exp).then_inc(s_ex, 1)
                ahead.scalar_step(act, steps - 1)

            @block.vector
            def _(dve):
                ch = Chain(dve, s_v)

                for t in range(NT):
                    for u in range(U):
                        ch.step(nc.vector.max(top[:, u, 0:8], c.SC[:, t, u, :]))
                    ch.wait()
                    for u in range(U):
                        ch.step(nc.vector.match_replace(rest[:, u, :], top[:, u, 0:8], c.SC[:, t, u, :], LOWEST))
                    for u in range(U):
                        ch.step(nc.vector.max_index(idx[:, u, 0:8], top[:, u, 0:8], c.SC[:, t, u, :]))
                    ch.wait(ch.n - U)
                    for u in range(U):
                        ch.step(nc.vector.max(top[:, u, 8:16], rest[:, u, :]))
                    ch.wait()
                    for u in range(U):
                        ch.step(nc.vector.max_index(idx[:, u, 8:16], top[:, u, 8:16], rest[:, u, :]))
                    v = top[:].rearrange("p (h s) k -> p h s k", s=2)
                    for a0, na, n, o in runs:
                        ch.step(nc.vector.tensor_tensor(
                            cv[:, :, o:o + na * n].rearrange("p h (a b) -> p h a b", b=n),
                            v[:, :, 0, a0:a0 + na].unsqueeze(3).broadcast_to([P, PH, na, n]),
                            v[:, :, 1, 0:n].unsqueeze(2).broadcast_to([P, PH, na, n]), ALU.add))
                    ch.wait()
                    ch.step(nc.vector.tensor_copy(idxf[:], idx[:]))
                    for h in range(PH):
                        ch.step(nc.vector.max(best[:, h, 0:8], cv[:, h, :]))
                    ch.wait(ch.n - PH)
                    i1 = idxf[:].rearrange("p (h s) k -> p h s k", s=2)[:, :, 0, :]
                    i2 = idxf[:].rearrange("p (h s) k -> p h s k", s=2)[:, :, 1, :]
                    ch.step(nc.vector.tensor_scalar(i1, i1, float(NKEYS), None, ALU.mult))
                    ch.wait()
                    for h in range(PH):
                        ch.step(nc.vector.match_replace(cr[:, h, :], best[:, h, 0:8], cv[:, h, :], LOWEST))
                    for a0, na, n, o in runs:
                        ch.step(nc.vector.tensor_tensor(
                            ce[:, :, o:o + na * n].rearrange("p h (a b) -> p h a b", b=n),
                            i1[:, :, a0:a0 + na].unsqueeze(3).broadcast_to([P, PH, na, n]),
                            i2[:, :, 0:n].unsqueeze(2).broadcast_to([P, PH, na, n]), ALU.add))
                    ch.wait()
                    for h in range(PH):
                        ch.step(nc.vector.max(best[:, h, 8:16], cr[:, h, :]))
                    for h in range(PH):
                        ch.step(nc.vector.max_index(pos[:, h, 0:8], best[:, h, 0:8], cv[:, h, :]))
                    ch.wait(ch.n - PH)
                    for h in range(PH):
                        ch.step(nc.vector.max_index(pos[:, h, 8:16], best[:, h, 8:16], cr[:, h, :]))
                    nc.vector.tensor_tensor(ex[:, t, :, :], best[:], best[:, :, 0:1].broadcast_to([P, PH, TOPK]),
                                            ALU.subtract).then_inc(s_d, 1)
                    ch.wait()
                    ch.step(nc.vector.tensor_copy(posf[:], pos[:]))
                    ch.wait()
                    if t == 0:
                        dve.wait_ge(s_iota, 1)
                    for h in range(PH):
                        ch.step(nc.vector.tensor_tensor(
                            hit[:, h, :, :], iota[:].unsqueeze(1).broadcast_to([P, TOPK, NCAND]),
                            posf[:, h, :].unsqueeze(2).broadcast_to([P, TOPK, NCAND]), ALU.is_equal))
                    ch.wait()
                    for h in range(PH):
                        ch.step(nc.vector.tensor_tensor(hit[:, h, :, :], hit[:, h, :, :],
                                                        ce[:, h, :].unsqueeze(1).broadcast_to([P, TOPK, NCAND]),
                                                        ALU.mult))
                    ch.wait()
                    ch.step(nc.vector.tensor_reduce(expert[:, t, :].rearrange("p (h k) -> p h k", h=PH), hit[:], AX.X,
                                                    ALU.add))
                    ch.wait()
                dve.wait_ge(s_ex, 1)
                ex3 = ex[:].rearrange("p t h k -> p (t h) k")
                ch.step(nc.vector.tensor_reduce(esum[:], ex3, AX.X, ALU.add))
                ch.wait()
                ch.step(nc.vector.reciprocal(esum[:], esum[:]))
                ch.wait()
                ch.step(nc.vector.tensor_tensor(gate[:].rearrange("p t (h k) -> p (t h) k", h=PH), ex3,
                                                esum[:].unsqueeze(2).broadcast_to([P, NT * PH, TOPK]), ALU.mult))
                ch.step(nc.vector.tensor_copy(e_int[:], expert[:]))
                ch.wait()
                ch.step(nc.vector.tensor_scalar(part[0][:], e_int[:], 7, None, ALU.arith_shift_right))
                ch.step(nc.vector.tensor_scalar(part[1][:], e_int[:], NKEYS - 1, None, ALU.bitwise_and))
                ch.wait()
                for i in range(2):
                    ch.step(nc.vector.tensor_copy(partf[i][:], part[i][:]))
                for i, dst in enumerate((c.I1T, c.I2T, c.GT)):
                    dve.wait_ge(s_tr, i + 1)
                    nc.vector.tensor_copy(dst[:], ps[i][:])
                c.select_steps = ch.n

            @block.tensor
            def _(pe):
                ahead.flip(pe, 0, 0, True)
                ahead.tensor_step(pe, 0, first=True)
                with pe.Fori(1, steps - 1) as i:
                    ahead.tensor_step(pe, i)
                ahead.flip(pe, steps - 1, 1)
                ahead.acts(pe, steps - 1, 0)
                ahead.flip(pe, steps, 0)
                pe.wait_ge(s_v, c.select_steps)
                for i, src in enumerate((partf[0], partf[1], gate)):
                    for t in range(NT):
                        last = nc.tensor.transpose(ps[i][:, t * P:(t + 1) * P], src[:, t, :], c.ident[:])
                    last.then_inc(s_tr, 1)
                ahead.acts(pe, steps - 1, 1)


SELECT_STEPS = 16
EXTRA_STEPS = 2
N_AHEAD = 2 * (SELECT_STEPS + SEQ // 32 + EXTRA_STEPS)
GT_BLK = 64
NB = SEQ // GT_BLK


def dense_gates(c, ahead, h0, v_tab):
    nc = c.nc
    RING, SLOTS, Q = 32, 16, 4
    TURN = 2 * GT_BLK
    T = SEQ // TURN
    NQ = RING // Q
    PIECES = 4
    with c.stage() as mem:
        iota = mem.enter_context(nc.sbuf_tensor("iota_keys", [P, NKEYS], F32))
        oh2 = mem.enter_context(nc.sbuf_tensor("one_hot2", [P, SLOTS, NKEYS], F32))
        oh1 = mem.enter_context(nc.sbuf_tensor("gated_hot1", [P, SLOTS, NKEYS], F32))
        block1 = mem.enter_context(nc.sbuf_tensor("gate_block", [P, NKEYS, GT_BLK], F32))
        blk = [c.SC[:].rearrange("p t u n -> p (t u n)").rearrange("p (n t) -> p n t", t=GT_BLK), block1[:]]
        ps = [mem.enter_context(nc.psum_tensor(f"dg{i}", [P, SEQ], F32)) for i in range(4)]
        s_iota, s_hot, s_pe, s_st = c.sem("iota_keys_set"), c.sem("one_hots"), c.sem("gates_made"), c.sem("gates_stored")
        s_last = c.sem("last_block_first_piece_out")
        s_dma, s_v = [c.sem("gate_block_out0"), c.sem("gate_block_out1")], c.sem("first_v_loaded")

        def turns(eng, body):
            body(0, True, False)
            with eng.Fori(1, T - 1) as i:
                body(i, False, False)
            body(T - 1, False, True)

        def steps(i, final):
            n = TURN // RING
            return [i * n + (h0 + k) for k in range(n + (EXTRA_STEPS if final else 0))]

        FINAL = h0 + SEQ // RING + EXTRA_STEPS - 1

        with nc.Block() as block:

            @block.gpsimd
            def _(pool):
                nc.gpsimd.iota(iota[:], [[1, NKEYS]], base=0, channel_multiplier=0,
                               allow_small_or_imprecise_dtypes=True).then_inc(s_iota, 1)
                with pool.Fori(0, SEQ // RING + EXTRA_STEPS) as i:
                    ahead.pool_step(pool, i + h0)

            @block.vector
            def _(dve):
                dve.wait_ge(s_iota, 1)

                def hots(i, first):
                    for r in range(RING):
                        if r % Q == 0 and not (first and r < SLOTS):
                            dve.wait_ge(s_pe, i * NQ + (r // Q - (SLOTS // Q - 1)))
                        tok = bass.ds(i * RING + r, 1)
                        nc.vector.tensor_scalar(oh2[:, r % SLOTS, :], iota[:], c.I2T[:, tok], None, ALU.is_equal)
                        last = nc.vector.tensor_scalar(oh1[:, r % SLOTS, :], iota[:], c.I1T[:, tok], c.GT[:, tok],
                                                       ALU.is_equal, ALU.mult)
                        if r % Q == Q - 1:
                            last.then_inc(s_hot, 1)
                hots(0, True)
                with dve.Fori(1, SEQ // RING) as i:
                    hots(i, False)

            @block.tensor
            def _(pe):
                def turn(i, first, last):
                    for k, h in enumerate(steps(i, last)):
                        final = last and h == FINAL
                        if k >= TURN // RING:
                            ahead.tensor_step(pe, h, final=final)
                            continue
                        for q in range(NQ):
                            g = k * NQ + q
                            pe.wait_ge(s_hot, i * (TURN // Q) + (g + 1))
                            if not (first and g < 4):
                                pe.wait_ge(s_st, i * (TURN // Q) + (g - 3))
                            for r in range(q * Q, q * Q + Q):
                                made = nc.tensor.matmul(ps[q % 4][:, (r % Q) * P:(r % Q + 1) * P], oh2[:, r % SLOTS, :],
                                                        oh1[:, r % SLOTS, :], start=True, stop=True)
                            made.then_inc(s_pe, 1)
                            if q == 1:
                                ahead.flip(pe, h, 1)
                            elif q == 3:
                                ahead.acts(pe, h, 0)
                            elif q == 5:
                                ahead.flip(pe, h + 1, 0)
                            elif q == 7:
                                ahead.acts(pe, h, 1)
                turns(pe, turn)

            @block.scalar
            def _(act):
                def turn(i, first, last):
                    for k, h in enumerate(steps(i, last)):
                        if k >= TURN // RING:
                            ahead.scalar_step(act, h, final=last and h == FINAL)
                            continue
                        for q in range(NQ):
                            g = k * NQ + q
                            b, o = divmod(g, GT_BLK // Q)
                            if o == 0 and not first:
                                act.wait_ge(s_dma[b], i * (16 * PIECES))
                            act.wait_ge(s_pe, i * (TURN // Q) + (g + 1))
                            nc.scalar.activation(blk[b][:, :, o * Q:(o + 1) * Q],
                                                 ps[q % 4][:].rearrange("p (t n) -> p n t", t=Q),
                                                 ACT.Copy).then_inc(s_st, 1)
                            if q == 2:
                                ahead.high(act, h, 1)
                            elif q == 4:
                                ahead.gelu(act, h, 0)
                            elif q == 6:
                                ahead.high(act, h + 1, 0)
                            elif q == 7:
                                ahead.gelu(act, h, 1)
                turns(act, turn)

            @block.sync
            def _(sp):
                def piece(i, b, n, sem):
                    sp.wait_ge(s_st, i * (TURN // Q) + (b + 1) * (GT_BLK // Q))
                    rows = slice(n * NKEYS // PIECES, (n + 1) * NKEYS // PIECES)
                    sp.dma_start(c.gates[bass.ds(i * 2 + b, 1), :, rows, :].rearrange("a p n t -> p (a n t)"),
                                 blk[b][:, rows, :].rearrange("p n t -> p (n t)")).then_inc(sem, 16)

                def turn(i, first, last):
                    for k, h in enumerate(steps(i, last)):
                        for j in range(2):
                            if not (last and h == FINAL):
                                ahead.load(sp, h + 1, j)
                            if k < TURN // RING:
                                ahead.put_aside(sp, h, j)
                            n = 2 * (k % 2) + j
                            if k in (2, 3):
                                piece(i, 0, n, s_dma[0])
                            elif k >= 4:
                                piece(i, 1, n, s_dma[1] if n else s_last)
                                if n == 2:
                                    for m in range(2):
                                        sp.wait_ge(ahead.s_st[m], 16)
                                    sp.wait_ge(s_dma[0], 16 * PIECES * T)
                                    sp.wait_ge(s_last, 16)
                                    sp.dma_start(c.first_acts, c.aside[0:2].rearrange("a p t -> p a t")).then_inc(s_v, 16)
                                    sp.dma_start(c.first_gates, c.gates[:, :, 0:2, :].rearrange(
                                        "b p i t -> p b (i t)")).then_inc(s_v, 16)
                            elif not first:
                                piece(i - 1, 1, n, s_dma[1])
                            if k >= TURN // RING:
                                ahead.put_aside(sp, h, j)
                for j in range(2):
                    sp.dma_start(c.vst[j], v_tab[j * P:(j + 1) * P, :]).then_inc(s_v, 16)
                turns(sp, turn)
                sp.wait_ge(s_v, 64)
                for b in range(2):
                    sp.wait_ge(s_dma[b], 16 * (PIECES * T - b))
                    sp.wait_ge(ahead.s_st[b], 16 * (ahead.count // 2))


def experts(c, u_tab, v_tab, n0, n1, ready, later=()):
    nc = c.nc
    G, B = 2, 4
    HALF = D // 2
    tag = "_r" if ready else "_f"
    with c.stage() as mem:
        def sb(name, shape, dt=F32):
            return mem.enter_context(nc.sbuf_tensor(name + tag, shape, dt))

        ust = c.ust
        vst = c.vst
        uh = [sb(f"u_hi{j}", [P, ND, P], F32R) for j in range(0 if ready else 2)]
        ul = [sb(f"u_lo{j}", [P, ND, P], F32R) for j in range(0 if ready else 2)]
        vh = [sb(f"v_hi{j}", [P, D], F32R) for j in range(B)]
        vl = [sb(f"v_lo{j}", [P, D], F32R) for j in range(B)]
        gst = [sb(f"g{j}", [P, NB, G * GT_BLK]) for j in range(2)]
        NG = B if ready else 2
        gel = [sb(f"gelu{j}", [P, SEQ]) for j in range(NG)]
        s_back, s_later = [c.sem(f"acts_back{j}") for j in range(B)], c.sem("later_loaded")
        hid = [sb(f"hid{j}", [P, SEQ]) for j in range(2)]
        hh = [sb(f"hid_hi{j}", [P, SEQ], F32R) for j in range(B)]
        hl = [sb(f"hid_lo{j}", [P, SEQ], F32R) for j in range(B)]
        tr = [] if ready else [mem.enter_context(nc.psum_tensor(f"ut{k}", [P, 4, P], F32)) for k in range(2)]
        pa = [] if ready else [mem.enter_context(nc.psum_tensor(f"acts{j}", [P, SEQ], F32)) for j in range(2)]
        NPO = 8 if ready else 4
        po = [mem.enter_context(nc.psum_tensor(f"outs{j}{tag}", [P, HALF], F32)) for j in range(NPO)]
        s_u = [c.sem(f"u_loaded{j}") for j in range(B)]
        s_vl = [c.sem(f"v_loaded{j}") for j in range(B)]
        s_g = [c.sem(f"g_loaded{j}") for j in range(2)]
        s_tr, s_uhi, s_ulo, s_act = c.sem("u_transposed"), c.sem("u_high"), c.sem("u_low"), c.sem("acts_made")
        s_gelu, s_hid, s_hh, s_hl = c.sem("gelu_done"), c.sem("hid_made"), c.sem("hid_high"), c.sem("hid_low")
        s_vh, s_vlo, s_out, s_acc = c.sem("v_high"), c.sem("v_low"), c.sem("outs_made"), c.sem("outs_added")
        outs = [(t, h) for t in range(NT) for h in range(2)]
        NO = len(outs)
        T = (n1 - n0) // B

        def turns(eng, body):
            body(0, True, False)
            with eng.Fori(1, T - 1) as i:
                body(i, False, False)
            body(T - 1, False, True)

        with nc.Block() as block:

            @block.sync
            def _(sp):
                def loads(i, first, last):
                    for j in range(B):
                        n = i * B + (n0 + j)
                        if ready and not (first and j < G):
                            if not first:
                                sp.wait_ge(s_hid, i * B + (j - 3))
                            sp.dma_start(gel[j][:], c.aside[bass.ds(n, 1)].rearrange("a p t -> p (a t)"))\
                                .then_inc(s_back[j], 16)
                        elif not ready:
                            if not first:
                                sp.wait_ge(s_tr, i * B + (j - 3))
                                sp.dma_start(ust[j][:], u_tab[bass.ds(n * P, P), :]).then_inc(s_u[j], 16)
                        if j % G == 0 and not (ready and first and j == 0):
                            if not first:
                                sp.wait_ge(s_hid, i * B + (j - 2))
                            sp.dma_start(gst[j // G][:], c.gates[:, :, bass.ds(n, G), :].rearrange(
                                "b p i t -> p b (i t)")).then_inc(s_g[j // G], 16)
                        if not first:
                            sp.wait_ge(s_vlo, i * B + (j - 3))
                        if ready and first and j == G:
                            sp.wait_ge(s_hid, G)
                        if not (first and ready and j < G):
                            sp.dma_start(vst[j][:], v_tab[bass.ds(n * P, P), :]).then_inc(s_vl[j], 16)
                turns(sp, loads)
                for dst, src in later:
                    sp.dma_start(dst, src).then_inc(s_later, 16)
                if later:
                    sp.wait_ge(s_later, 16 * len(later))

            @block.tensor
            def _(pe):
                def flip(i, j, first):
                    if not (first and j < B):
                        pe.wait_ge(s_u[j % B], 16 * i + (0 if j < B else 16))
                    if not (first and j == 0):
                        pe.wait_ge(s_ulo, i * B + j)
                    for k in range(2):
                        for d in range(4):
                            last = nc.tensor.transpose(tr[k][:, d, :], ust[j % B][:, (4 * k + d) * P:(4 * k + d + 1) * P],
                                                       c.ident[:])
                    last.then_inc(s_tr, 1)

                def acts(i, j, first):
                    pe.wait_ge(s_ulo, i * B + (j + 1))
                    if not (first and j < 2):
                        pe.wait_ge(s_gelu, i * B + (j - 1))
                    for d in range(ND):
                        last = three_pass(nc, pa[j % 2][:], uh[j % 2][:, d, :], ul[j % 2][:, d, :], c.XH[:, d, :],
                                          c.XL[:, d, :], d == 0, d == ND - 1)
                    last.then_inc(s_act, 1)

                def values(i, g, first):
                    pe.wait_ge(s_vlo, i * B + (G * g + G))
                    pe.wait_ge(s_hl, i * B + (G * g + G))
                    for o, (t, h) in enumerate(outs):
                        if not (first and g == 0 and o < NPO):
                            pe.wait_ge(s_acc, i * (2 * NO) + (g * NO + o - (NPO - 1)))
                        for k in range(G):
                            j = (G * g + k) % B
                            a, v = slice(t * P, (t + 1) * P), slice(h * HALF, (h + 1) * HALF)
                            last = three_pass(nc, po[o % NPO][:], hh[j][:, a], hl[j][:, a], vh[j][:, v], vl[j][:, v],
                                              k == 0, k == G - 1)
                        last.then_inc(s_out, 1)

                def turn(i, first, last):
                    if first and not ready:
                        flip(0, 0, True)
                    for j in range(B):
                        if not ready:
                            if not (last and j == B - 1):
                                flip(i, j + 1, first)
                            acts(i, j, first)
                        if j % G == G - 1 and not (first and j < G):
                            values(i, j // G - 1, first)
                    if last:
                        values(i, 1, first)
                turns(pe, turn)

            @block.scalar
            def _(act):
                def u_high(i, j, first):
                    act.wait_ge(s_tr, i * B + (j + 1))
                    if not (first and j < 2):
                        act.wait_ge(s_act, i * B + (j - 1))
                    for k in range(2):
                        nc.scalar.activation(uh[j % 2][:, 4 * k:4 * k + 4, :], tr[k][:], ACT.Copy).then_inc(s_uhi, 1)

                def v_high(i, j, first):
                    if not (first and ready and j < G):
                        act.wait_ge(s_vl[j], 16 * i + (0 if ready and j < G else 16))
                    if not first:
                        act.wait_ge(s_out, i * (2 * NO) + (j // G - 1) * NO)
                    nc.scalar.activation(vh[j][:], vst[j][:], ACT.Copy).then_inc(s_vh, 1)

                def turn(i, first, last):
                    if first and not ready:
                        u_high(0, 0, True)
                    if first and ready:
                        v_high(0, 0, True)
                        v_high(0, 1, True)
                    for j in range(B):
                        if not (last and j == B - 1) and not ready:
                            u_high(i, j + 1, first)
                        if not (first and ready and j < G):
                            v_high(i, j, first)
                        if not ready:
                            act.wait_ge(s_act, i * B + (j + 1))
                            if not (first and j < 2):
                                act.wait_ge(s_hid, i * B + (j - 1))
                            nc.scalar.activation(gel[j % NG][:], pa[j % 2][:], ACT.Gelu).then_inc(s_gelu, 1)
                        act.wait_ge(s_hid, i * B + (j + 1))
                        nc.scalar.activation(hh[j][:], hid[j % 2][:], ACT.Copy).then_inc(s_hh, 1)
                turns(act, turn)

            @block.gpsimd
            def _(pool):
                def turn(i, first, last):
                    for j in range(B):
                        pool.wait_ge(s_vh, i * B + (j + 1))
                        nc.gpsimd.tensor_tensor(vl[j][:], vst[j][:], vh[j][:].bitcast(F32), ALU.subtract).then_inc(s_vlo, 1)
                turns(pool, turn)

            @block.vector
            def _(dve):
                def u_low(i, j, first):
                    for k in range(2):
                        dve.wait_ge(s_uhi, i * (2 * B) + (2 * j + k + 1))
                        d = slice(4 * k, 4 * k + 4)
                        last = nc.vector.tensor_tensor(ul[j % 2][:, d, :], tr[k][:], uh[j % 2][:, d, :].bitcast(F32),
                                                       ALU.subtract)
                    last.then_inc(s_ulo, 1)

                def add(i, g):
                    for o, (t, h) in enumerate(outs):
                        dve.wait_ge(s_out, i * (2 * NO) + (g * NO + o + 1))
                        H = c.H[:, t, h * HALF:(h + 1) * HALF]
                        nc.vector.tensor_tensor(H, H, po[o % NPO][:], ALU.add).then_inc(s_acc, 1)

                def turn(i, first, last):
                    if first and not ready:
                        u_low(0, 0, True)
                    for j in range(B):
                        if not (last and j == B - 1) and not ready:
                            u_low(i, j + 1, first)
                        here = ready and j < G
                        if j % G == 0 and not (here and first):
                            dve.wait_ge(s_g[j // G], 16 * i + (0 if here else 16))
                        if ready and not (here and first):
                            dve.wait_ge(s_back[j], 16 * i + (0 if here else 16))
                        if not ready:
                            dve.wait_ge(s_gelu, i * B + (j + 1))
                        if not (first and j < 2):
                            dve.wait_ge(s_hl, i * B + (j - 1))
                        acts, gates = (c.first_acts[:, j], c.first_gates) if here and first else (gel[j % NG][:], gst[j // G])
                        nc.vector.tensor_tensor(
                            hid[j % 2][:].rearrange("p (b t) -> p b t", b=NB), acts.rearrange("p (b t) -> p b t", b=NB),
                            gates[:, :, (j % G) * GT_BLK:(j % G + 1) * GT_BLK], ALU.mult).then_inc(s_hid, 1)
                        dve.wait_ge(s_hh, i * B + (j + 1))
                        nc.vector.tensor_tensor(hl[j][:], hid[j % 2][:], hh[j][:].bitcast(F32), ALU.subtract).then_inc(s_hl, 1)
                        if j % G == G - 1 and not (first and j < G):
                            add(i, j // G - 1)
                    if last:
                        add(i, 1)
                turns(dve, turn)


def gated_embedding(c, w_gate, emb, w_emb, gain_ple, gain_final, out):
    nc = c.nc
    HALF = D // 2
    KE = PLE // P
    with c.stage() as mem:
        def sb(name, shape):
            return mem.enter_context(nc.sbuf_tensor(name, shape, F32))

        XN, value, et = sb("XN_tail", [P, NT, D]), sb("ple_value", [P, NT, D]), sb("emb_t", [P, KE, SEQ])
        gate = [sb(f"ple_gate{i}", [P, HALF]) for i in range(2)]
        bank = [mem.enter_context(nc.psum_tensor(f"tb{i}", [P, SEQ], F32)) for i in range(8)]
        norm, final = Norm(c, mem, "ple", gain_ple), Norm(c, mem, "final", gain_final)
        flip = Flip(c, "ple", XN, bank[0:4])
        w = RowWeights(c, mem, "gate", w_gate, c.vst)
        s_et, s_ett, s_val, s_vals = c.sem("emb_flipped"), c.sem("emb_copied"), c.sem("values_made"), c.sem("values_kept")
        s_z, s_sig, s_mul, s_add, s_o = c.sem("gates_z"), c.sem("gates_sig"), c.sem("gated"), c.sem("embedding_added"), \
            c.sem("out_stored")
        units = [(half, t) for half in range(2) for t in range(NT)]

        def z_bank(n):
            return bank[(n + 4) % 8]

        with nc.Block() as block:

            @block.sync
            def _(sp):
                for n in range(w.N):
                    w.load(sp, n)
                for t in range(NT):
                    sp.wait_ge(final.s_xn, t + 1)
                    sp.dma_start(out[0, t * P:(t + 1) * P, :], XN[:, t, :]).then_inc(s_o, 16)
                sp.wait_ge(s_o, 16 * NT)

            @block.tensor
            def _(pe):
                for k in range(KE):
                    for t in range(NT):
                        last = nc.tensor.transpose(bank[k][:, t * P:(t + 1) * P], emb[:, t, k * P:(k + 1) * P], c.ident[:])
                    last.then_inc(s_et, 1)

                def values(half):
                    for t in range(NT):
                        if half:
                            pe.wait_ge(s_vals, t + 1)
                        for k in range(KE):
                            last = nc.tensor.matmul(bank[4 + t][:], et[:, k, t * P:(t + 1) * P],
                                                    w_emb[:, k, half * HALF:(half + 1) * HALF],
                                                    start=(k == 0), stop=(k == KE - 1))
                        last.then_inc(s_val, 1)

                def gates(n):
                    half, t = units[n]
                    if half == 0:
                        pe.wait_ge(flip.s_lo, 2 * t + 2)
                        pe.wait_ge(s_vals, NT + t + 1)
                    w.product(pe, c, z_bank(n)[:], half, t, s_z)

                pe.wait_ge(s_ett, KE)
                values(0)
                for t in range(2):
                    pe.wait_ge(norm.s_xn, t + 1)
                    flip.transpose(pe, t)
                values(1)
                for n in range(len(units)):
                    gates(n)
                    if n < 2:
                        pe.wait_ge(norm.s_xn, n + 3)
                        flip.transpose(pe, n + 2)

            @block.scalar
            def _(act):
                for k in range(KE):
                    act.wait_ge(s_et, k + 1)
                    nc.scalar.activation(et[:, k, :], bank[k][:], ACT.Copy).then_inc(s_ett, 1)
                for t in range(NT):
                    norm.square(act, t, XN[:, t, :])
                norm.root(act, 0, NT)
                for n in range(4):
                    w.high(act, n)
                for t in range(2):
                    flip.high(act, t)
                w.high(act, 4)
                w.high(act, 5)
                for n, (half, t) in enumerate(units):
                    if n < 2:
                        flip.high(act, n + 2)
                        w.high(act, n + 6)
                    act.wait_ge(s_z, n + 1)
                    if n >= 2:
                        act.wait_ge(s_add, n - 1)
                    nc.scalar.activation(gate[n % 2][:], z_bank(n)[:], ACT.Sigmoid).then_inc(s_sig, 1)
                    if half == 1:
                        act.wait_ge(s_add, n + 1)
                        final.square(act, t, XN[:, t, :])
                        final.root(act, t, t + 1)

            @block.gpsimd
            def _(pool):
                for n in range(w.N):
                    w.low(pool, n)

            @block.vector
            def _(dve):
                def keep(n):
                    half, t = units[n]
                    dve.wait_ge(s_val, n + 1)
                    nc.vector.tensor_copy(value[:, t, half * HALF:(half + 1) * HALF], bank[4 + t][:]).then_inc(s_vals, 1)

                norm.invert(dve, 0, NT)
                for t in range(2):
                    norm.scale(dve, t, XN[:, t, :])
                for n in range(NT):
                    keep(n)
                for t in range(2):
                    flip.low(dve, t)
                    norm.scale(dve, t + 2, XN[:, t + 2, :])
                for n in range(NT, 2 * NT):
                    keep(n)
                for n, (half, t) in enumerate(units):
                    if n < 2:
                        flip.low(dve, n + 2)
                    cols = slice(half * HALF, (half + 1) * HALF)
                    dve.wait_ge(s_sig, n + 1)
                    nc.vector.tensor_tensor(gate[n % 2][:], gate[n % 2][:], value[:, t, cols], ALU.mult).then_inc(s_mul, 1)
                    dve.wait_ge(s_mul, n + 1)
                    nc.vector.tensor_tensor(c.H[:, t, cols], c.H[:, t, cols], gate[n % 2][:], ALU.add).then_inc(s_add, 1)
                    if half == 1:
                        final.invert(dve, t, t + 1)
                        final.scale(dve, t, XN[:, t, :])


def build(nc, ins, out):
    with ExitStack() as ctx:
        c = Chip(nc, ctx)
        c.H = c.keep("H", [P, NT, D], F32)
        c.XH = c.keep("XH", [P, ND, SEQ], F32R)
        c.XL = c.keep("XL", [P, ND, SEQ], F32R)
        c.ident = c.keep("ident", [P, P], F32)
        c.eps = c.keep("eps", [P, 1], F32)
        c.MIX = c.keep("MIX", [P, NT, D], F32)
        c.vst = [c.MIX[:, j, :] for j in range(4)]
        c.first_gates = c.MIX[:, 2, :].rearrange("p (b n) -> p b n", b=NB)
        c.first_acts = c.MIX[:, 3, :].rearrange("p (a t) -> p a t", a=2)
        c.early = c.keep("early", [P, 2, D], F32)
        w_in = ins["w_in"][0].rearrange("(k p) n -> p k n", p=P)

        def in_columns(n):
            if in_width(n) == RANK:
                return w_in[:, :, GLR_COL:GLR_COL + RANK]
            u = in_unit(n)
            a = u * P + (0 if isinstance(u, int) and u < UG else RANK)
            return w_in[:, :, bass.ds(a, P)]

        with c.stage() as mem:
            def sb(name, shape):
                return mem.enter_context(nc.sbuf_tensor(name, shape, F32))

            c.PROJ, c.GLR, c.TOK = sb("PROJ", [P, NU_IN * SEQ]), sb("GLR", [RANK, SEQ]), sb("TOK", [P, NT, 1536])
            chain = GateChain(c, mem, ins)
            with c.stage() as m2:
                c.BIAS = m2.enter_context(nc.sbuf_tensor("BIAS", [P, ATT_HEADS, 2 * P], F32))
                cols = Columns(c, m2, "in", in_columns)
                table = c.TOK[:].rearrange("p t e -> p (t e)")[:, 0:N_TABLE].rearrange("p (h k) -> p h k", h=ATT_HEADS)
                start(c, cols, ins["x"], ins["norm_mix"].broadcast_to([P, D]), ins["rel_bias"], table)
                attention_inputs(c, cols, table)
                band_attention(c, cols, chain)
            gla(c, ins, chain)

        with ExitStack() as mem:
            c.SC = mem.enter_context(nc.sbuf_tensor("scores", [P, NT, 2 * PH, NKEYS], F32))
            w_q = ins["peer_wq"][0].rearrange("(k p) n -> p k n", p=P)
            with c.stage() as m2:
                cols = Columns(c, m2, "query", lambda n: w_q[:, :, bass.ds(n * P, P)])
                mixer_output(c, ins["w_out"][0], ins["norm_ffn"].broadcast_to([P, D]), cols)
                c.Q = m2.enter_context(nc.sbuf_tensor("queries", [P, 2 * PH * SEQ], F32))
                kt = m2.enter_context(nc.sbuf_tensor("keys_t", [P, 2 * PH * P], F32))
                queries(c, cols, ins["peer_subkeys"][0], kt)
                key_scores(c, kt, ins["peer_u"][0])
            c.I1T = mem.enter_context(nc.sbuf_tensor("I1T", [P, SEQ], F32))
            c.I2T = mem.enter_context(nc.sbuf_tensor("I2T", [P, SEQ], F32))
            c.GT = mem.enter_context(nc.sbuf_tensor("GT", [P, SEQ], F32))
            c.gates = nc.dram_tensor("gates", (NB, NKEYS, NKEYS, GT_BLK), F32, kind="Internal").ap()
            c.aside = nc.dram_tensor("acts_aside", (N_AHEAD, P, SEQ), F32, kind="Internal").ap()
            ahead = Ahead(c, mem, ins["peer_u"][0], N_AHEAD)
            select_experts(c, ahead, SELECT_STEPS)
            dense_gates(c, ahead, SELECT_STEPS, ins["peer_v"][0])
        u_tab = ins["peer_u"][0]
        emb, w_emb = c.keep("emb", [P, NT, PLE], F32), c.keep("w_emb", [P, PLE // P, D], F32)
        gain_ple, gain_final = c.keep("gain_ple", [P, D], F32), c.keep("gain_final", [P, D], F32)
        with ExitStack() as mem:
            c.ust = [mem.enter_context(nc.sbuf_tensor(f"u{j}", [P, D], F32)) for j in range(4)]
            experts(c, u_tab, ins["peer_v"][0], 0, N_AHEAD, True,
                    [(c.ust[j][:], u_tab[(N_AHEAD + j) * P:(N_AHEAD + j + 1) * P, :]) for j in range(4)])
            experts(c, u_tab, ins["peer_v"][0], N_AHEAD, NKEYS, False, [
                (emb[:], ins["p"][0, 0].rearrange("(t p) d -> p t d", p=P)),
                (w_emb[:], ins["w_ple"][0].rearrange("(k p) n -> p k n", p=P)),
                (gain_ple[:], ins["norm_ple"].broadcast_to([P, D])),
                (gain_final[:], ins["final_norm"].unsqueeze(0).broadcast_to([P, D]))])
        gated_embedding(c, ins["w_ple_gate"][0], emb, w_emb, gain_ple[:], gain_final[:], out)


_INS = ["x", "p", "norm_mix", "w_in", "gla_gate_w2", "gla_gate_b", "gla_head_norm", "rel_bias", "w_out", "norm_ffn",
        "peer_wq", "peer_subkeys", "peer_u", "peer_v", "norm_ple", "w_ple_gate", "w_ple", "final_norm"]

def kernel(**inputs):
    import numpy as _np
    import concourse.bacc as _bacc
    from concourse import mybir as _mybir
    from concourse.bass_utils import run_bass_kernel_spmd as _run

    nc = _bacc.Bacc("TRN2", target_bir_lowering=False, num_devices=1)
    arrays, args = {}, {}
    for name in _INS:
        a = _np.ascontiguousarray(inputs[name])
        arrays[f"in_{name}_dram"] = a
        args[name] = nc.dram_tensor(f"in_{name}_dram", a.shape, _mybir.dt.from_np(a.dtype), kind="ExternalInput").ap()
    out = nc.dram_tensor("out_0_dram", (1, SEQ, D), _mybir.dt.float32, kind="ExternalOutput").ap()
    build(nc, args, out)
    r = _run(nc, [arrays], core_ids=[0])
    return r.results[0]["out_0_dram"]
```
